# Optimizing a Trainium2 kernel written in Bass

```python
import functools
import jax
import jax.numpy as jnp
from jax import lax
import numpy as np

D_MODEL = 1024
BATCH = 1
SEQ = 2048
DEPTH = 1
DEC_BATCH = 1
DEC_SEQ = 32
PAST_LEN = 256

CHUNK = 64
HEAD_DIM = 64
N_HEADS_R = 8
D_R = N_HEADS_R * HEAD_DIM
LORA_W = 64
LORA_A = 64
LORA_G = 128
R_PROJ = 3 * D_R + LORA_W + LORA_A + LORA_G
N_HEADS_A = 8
D_A = N_HEADS_A * HEAD_DIM
BAND_CHUNKS = 8
WINDOW = BAND_CHUNKS * CHUNK
BAND = WINDOW + CHUNK
REL_CLIP = 128
N_REL = 2 * REL_CLIP + 1
D_FF = 4 * D_MODEL
IN_PROJ = R_PROJ + 3 * D_A + 2 * D_MODEL
NORM_EPS = 1e-6
GN_EPS = 64e-5
ATT_SCALE = HEAD_DIM ** -0.5

kernel_name = "hybrid_rwkv7_chunkband_stream_step"

def rms_norm(x, g):
    xf = x.astype(jnp.float32)
    y = xf * lax.rsqrt(jnp.mean(xf * xf, axis=-1, keepdims=True) + NORM_EPS)
    return (y * g.astype(jnp.float32)).astype(x.dtype)

def modulate(x, g, shift, scale):
    return rms_norm(x, g) * (1 + scale) + shift

def wkv7_scan(s0, r, w, k, v, kk, a):
    def step(S, inp):
        r_t, w_t, k_t, v_t, kk_t, a_t = inp
        sa = jnp.einsum("bhvk,bhk->bhv", S, kk_t)
        S = (S * w_t[:, :, None, :]
             - sa[..., None] * (kk_t * a_t)[:, :, None, :]
             + v_t[..., None] * k_t[:, :, None, :])
        return S, jnp.einsum("bhvk,bhk->bhv", S, r_t)
    xs = tuple(jnp.swapaxes(t.astype(jnp.float32), 0, 1) for t in (r, w, k, v, kk, a))
    S, o = lax.scan(step, s0.astype(jnp.float32), xs)
    return S, jnp.swapaxes(o, 0, 1)

def rwkv7_branch(p, prev_row, s0, mu, w_up, w0, a_up, a0, g_up, k_k, k_a, r_k, lnx_g, lnx_b):
    B, T, _ = p.shape
    p_prev = jnp.concatenate([prev_row[:, None, :].astype(p.dtype), p[:, :-1]], axis=1)
    xs = p + (p_prev - p) * mu
    r, k, v, xw, xa, xg = jnp.split(
        xs, [D_R, 2 * D_R, 3 * D_R, 3 * D_R + LORA_W, 3 * D_R + LORA_W + LORA_A], axis=-1)
    w_log = -jax.nn.softplus(-(w0 + jnp.tanh(xw) @ w_up)) - 0.5
    decay = jnp.exp(-jnp.exp(w_log.astype(jnp.float32)))
    a = jax.nn.sigmoid(a0 + xa @ a_up)
    g = jax.nn.sigmoid(xg) @ g_up
    heads = lambda t: t.reshape(B, T, N_HEADS_R, HEAD_DIM)
    kk = heads(k * k_k).astype(jnp.float32)
    kk = kk * lax.rsqrt(jnp.maximum(jnp.sum(kk * kk, axis=-1, keepdims=True), 1e-24))
    k = k * (1 + (a - 1) * k_a)
    rh, kh, vh = heads(r), heads(k), heads(v)
    S, o = wkv7_scan(s0, rh, heads(decay), kh, vh, kk, heads(a))
    mean = jnp.mean(o, axis=-1, keepdims=True)
    var = jnp.mean(jnp.square(o - mean), axis=-1, keepdims=True)
    o = ((o - mean) * lax.rsqrt(var + GN_EPS)).reshape(B, T, D_R)
    o = (o * lnx_g.astype(jnp.float32) + lnx_b.astype(jnp.float32)).astype(p.dtype)
    bonus = (jnp.sum(rh * kh * r_k, axis=-1, keepdims=True) * vh).reshape(B, T, D_R)
    return (o + bonus) * g, S.astype(s0.dtype), p[:, -1]

def rel_bias(table, q_pos, k_pos):
    idx = jnp.clip(q_pos[:, None] - k_pos[None, :], -REL_CLIP, REL_CLIP) + REL_CLIP
    return table[:, idx].astype(jnp.float32)

def band_attend(q, k, v, bias, valid):
    s = jnp.einsum("bqhd,bkhd->bhqk", q, k).astype(jnp.float32) * ATT_SCALE + bias
    s = jnp.where(valid, s, jnp.finfo(jnp.float32).min)
    p = jax.nn.softmax(s, axis=-1).astype(v.dtype)
    return jnp.einsum("bhqk,bkhd->bqhd", p, v)

def chunk_band_attention_prompt(q, k, v, table):
    B, T, H, Dh = q.shape
    n_chunks = T // CHUNK
    kp = jnp.pad(k, ((0, 0), (WINDOW, 0), (0, 0), (0, 0)))
    vp = jnp.pad(v, ((0, 0), (WINDOW, 0), (0, 0), (0, 0)))
    k_off = jnp.arange(BAND) - WINDOW
    bias = rel_bias(table, jnp.arange(CHUNK), k_off)

    def one_chunk(ci):
        start = ci * CHUNK
        qc = lax.dynamic_slice_in_dim(q, start, CHUNK, axis=1)
        kc = lax.dynamic_slice_in_dim(kp, start, BAND, axis=1)
        vc = lax.dynamic_slice_in_dim(vp, start, BAND, axis=1)
        return band_attend(qc, kc, vc, bias, (start + k_off) >= 0)

    out = lax.map(one_chunk, jnp.arange(n_chunks))
    return jnp.moveaxis(out, 0, 1).reshape(B, T, H, Dh)

def chunk_band_attention_step(q, k, v, table, cache_k, cache_v):
    T = q.shape[1]
    L = cache_k.shape[1]
    k_all = jnp.concatenate([cache_k.astype(k.dtype), k], axis=1)
    v_all = jnp.concatenate([cache_v.astype(v.dtype), v], axis=1)
    q_pos = PAST_LEN + jnp.arange(T)
    k_pos = jnp.concatenate([PAST_LEN - L + jnp.arange(L), q_pos])
    return band_attend(q, k_all, v_all, rel_bias(table, q_pos, k_pos), k_pos >= 0)

def trunk_layer(x, c, rwkv_prev, rwkv_s0, attend, P, l):
    B, T, _ = x.shape
    mod = (jax.nn.silu(c) @ P["w_ada"][l] + P["b_ada"][l])[:, None, :]
    sh1, sc1, g1, sh2, sc2, g2 = jnp.split(mod, 6, axis=-1)
    h = modulate(x, P["norm_mix_g"][l], sh1, sc1)
    proj = h @ P["w_in"][l]
    p_r, q, k, v, gates = jnp.split(
        proj, [R_PROJ, R_PROJ + D_A, R_PROJ + 2 * D_A, R_PROJ + 3 * D_A], axis=-1)
    y_r, s_new, last_row = rwkv7_branch(
        p_r, rwkv_prev, rwkv_s0, P["mu_shift"][l], P["w_lora_up"][l], P["w0"][l],
        P["a_lora_up"][l], P["a0"][l], P["g_lora_up"][l], P["k_k"][l], P["k_a"][l],
        P["r_k"][l], P["lnx_g"][l], P["lnx_b"][l])
    q, k, v = (t.reshape(B, T, N_HEADS_A, HEAD_DIM) for t in (q, k, v))
    y_a = attend(q, k, v, P["rel_table"][l]).reshape(B, T, D_A)
    gate_r, gate_a = jnp.split(jax.nn.sigmoid(gates), 2, axis=-1)
    merged = gate_r * (y_r @ P["w_br_r"][l]) + gate_a * (y_a @ P["w_br_a"][l])
    x = x + g1 * (merged @ P["w_out"][l])
    h2 = modulate(x, P["norm_mlp_g"][l], sh2, sc2)
    x = x + g2 * (jnp.square(jax.nn.relu(h2 @ P["w_ff1"][l])) @ P["w_ff2"][l])
    return x, s_new, last_row, k, v

def setup_inputs(seed: int = 0) -> dict:
    key = jax.random.key(seed)
    ks = iter(jax.random.split(key, 40))
    f32 = jnp.float32

    def nrm(shape, scale):
        return jax.random.normal(next(ks), shape, f32) * scale

    n_cache = min(WINDOW, PAST_LEN)
    D = D_MODEL
    return {
        "x_prompt": nrm((BATCH, SEQ, D), 1.0),
        "x_sample": nrm((DEC_BATCH, DEC_SEQ, D), 1.0),
        "c_prompt": nrm((BATCH, D), 1.0),
        "c_sample": nrm((DEC_BATCH, D), 1.0),
        "state_rwkv_wkv": nrm((DEPTH, DEC_BATCH, N_HEADS_R, HEAD_DIM, HEAD_DIM), 0.3),
        "state_rwkv_shift": nrm((DEPTH, DEC_BATCH, R_PROJ), 1.0),
        "cache_att_k": nrm((DEPTH, DEC_BATCH, n_cache, N_HEADS_A, HEAD_DIM), 1.0),
        "cache_att_v": nrm((DEPTH, DEC_BATCH, n_cache, N_HEADS_A, HEAD_DIM), 1.0),
        "w_ada": nrm((DEPTH, D, 6 * D), 0.5 * D ** -0.5),
        "b_ada": nrm((DEPTH, 6 * D), 0.02),
        "norm_mix_g": 1.0 + nrm((DEPTH, D), 0.05),
        "w_in": nrm((DEPTH, D, IN_PROJ), D ** -0.5),
        "mu_shift": jax.random.uniform(next(ks), (DEPTH, R_PROJ), f32),
        "w_lora_up": nrm((DEPTH, LORA_W, D_R), LORA_W ** -0.5),
        "w0": nrm((DEPTH, D_R), 0.5),
        "a_lora_up": nrm((DEPTH, LORA_A, D_R), 0.5 * LORA_A ** -0.5),
        "a0": nrm((DEPTH, D_R), 0.1),
        "g_lora_up": nrm((DEPTH, LORA_G, D_R), LORA_G ** -0.5),
        "k_k": 0.85 + nrm((DEPTH, D_R), 0.05),
        "k_a": 1.0 + nrm((DEPTH, D_R), 0.05),
        "r_k": nrm((DEPTH, N_HEADS_R, HEAD_DIM), 0.1),
        "lnx_g": 1.0 + nrm((DEPTH, D_R), 0.05),
        "lnx_b": nrm((DEPTH, D_R), 0.02),
        "rel_table": nrm((DEPTH, N_HEADS_A, N_REL), 0.1),
        "w_br_r": nrm((DEPTH, D_R, D), D_R ** -0.5),
        "w_br_a": nrm((DEPTH, D_A, D), D_A ** -0.5),
        "w_out": nrm((DEPTH, D, D), D ** -0.5),
        "norm_mlp_g": 1.0 + nrm((DEPTH, D), 0.05),
        "w_ff1": nrm((DEPTH, D, D_FF), D ** -0.5),
        "w_ff2": nrm((DEPTH, D_FF, D), D_FF ** -0.5),
        "final_norm_g": 1.0 + nrm((D,), 0.05),
    }

def reference(x_prompt, x_sample, c_prompt, c_sample, state_rwkv_wkv, state_rwkv_shift,
              cache_att_k, cache_att_v, w_ada, b_ada, norm_mix_g, w_in, mu_shift, w_lora_up, w0,
              a_lora_up, a0, g_lora_up, k_k, k_a, r_k, lnx_g, lnx_b, rel_table, w_br_r, w_br_a,
              w_out, norm_mlp_g, w_ff1, w_ff2, final_norm_g):
    P = dict(w_ada=w_ada, b_ada=b_ada, norm_mix_g=norm_mix_g, w_in=w_in, mu_shift=mu_shift,
             w_lora_up=w_lora_up, w0=w0, a_lora_up=a_lora_up, a0=a0, g_lora_up=g_lora_up,
             k_k=k_k, k_a=k_a, r_k=r_k, lnx_g=lnx_g, lnx_b=lnx_b, rel_table=rel_table,
             w_br_r=w_br_r, w_br_a=w_br_a, w_out=w_out, norm_mlp_g=norm_mlp_g,
             w_ff1=w_ff1, w_ff2=w_ff2)
    Bp, Tp, _ = x_prompt.shape
    n_keep = min(WINDOW, Tp)
    xp, xs = x_prompt, x_sample
    p_wkv, p_shift, p_k, p_v = [], [], [], []
    s_wkv, s_shift, s_k, s_v = [], [], [], []
    for l in range(DEPTH):
        zero_row = jnp.zeros((Bp, R_PROJ), x_prompt.dtype)
        zero_state = jnp.zeros((Bp, N_HEADS_R, HEAD_DIM, HEAD_DIM), x_prompt.dtype)
        xp, sp, rp, kp, vp = trunk_layer(xp, c_prompt, zero_row, zero_state,
                                         chunk_band_attention_prompt, P, l)
        p_wkv.append(sp)
        p_shift.append(rp)
        p_k.append(kp[:, Tp - n_keep:])
        p_v.append(vp[:, Tp - n_keep:])
        attend = functools.partial(chunk_band_attention_step,
                                   cache_k=cache_att_k[l], cache_v=cache_att_v[l])
        xs, ss, rs, ks_, vs_ = trunk_layer(xs, c_sample, state_rwkv_shift[l], state_rwkv_wkv[l],
                                           attend, P, l)
        s_wkv.append(ss)
        s_shift.append(rs)
        s_k.append(ks_)
        s_v.append(vs_)
    y_prompt = rms_norm(xp, final_norm_g)
    y_sample = rms_norm(xs, final_norm_g)
    return (y_prompt, y_sample,
            jnp.stack(p_wkv), jnp.stack(p_shift), jnp.stack(p_k), jnp.stack(p_v),
            jnp.stack(s_wkv), jnp.stack(s_shift), jnp.stack(s_k), jnp.stack(s_v))


_drawn_inputs = setup_inputs


def setup_inputs(seed=0):
    import zlib

    import numpy as np

    out = dict(_drawn_inputs(seed))
    spreads = {}
    factors = {'state_rwkv_wkv': 3.895,
     'state_rwkv_shift': 2.944,
     'cache_att_k': 4.512,
     'cache_att_v': 3.8,
     'k_k': 16.882,
     'lnx_g': 8.0,
     'lnx_b': 33.403,
     'rel_table': 8.0,
     'norm_mlp_g': 2.73}
    for name, (base, spread) in spreads.items():
        noise = np.random.default_rng([zlib.crc32(name.encode()), seed]).standard_normal(out[name].shape)
        drawn = base * np.exp(spread * noise) if base else spread * noise
        out[name] = jnp.asarray(drawn.astype(out[name].dtype))
    for name, factor in factors.items():
        out[name] = (out[name] * factor).astype(out[name].dtype)
    return out
```

```python
from contextlib import ExitStack

import concourse.bass as bass
from concourse import mybir

F32 = mybir.dt.float32
F32R = mybir.dt.float32r
ALU = mybir.AluOpType
ACT = mybir.ActivationFunctionType
AX = mybir.AxisListType
ds = bass.ds

P = 128
D = 1024
KD = D // P
SEQ, DEC = 2048, 32
NT = SEQ + DEC
NB, BW = 5, 416
SPLIT_AT = SEQ - (NB - 1) * BW
HD, NH, NP = 64, 8, 4
DR = NH * HD
R_PROJ = 1792
RT = R_PROJ // P
IN_T = 5376 // P
QT, KT_, VT, GT = RT, RT + 4, RT + 8, RT + 12
C = 64
NCH = SEQ // C
FF_T = 32
PAST = 256
WIN = 512
BAND = WIN + P
REL = 128
EXT = BAND + P - 1
NEG = -1.0e30
KAPPA = 0.6065306597126334
GN_EPS = 64e-5
EPS = 1e-6

VECS = [("b_ada", 48), ("norm_mix_g", 8), ("norm_mlp_g", 8), ("final_norm_g", 8), ("mu_shift", 14), ("w0", 4),
        ("a0", 4), ("k_k", 4), ("k_a", 4), ("r_k", 4), ("lnx_g", 4), ("lnx_b", 4)]
VROW = {}
NVEC = 0
for _name, _n in VECS:
    VROW[_name] = NVEC
    NVEC += _n
CROWS = {"c_prompt": 0, "c_sample": KD, "shift": 2 * KD}
NCROW = 2 * KD + RT


class Tensors:
    pass


class Steps:

    def __init__(self, ctx, nc, name, steps, base=0):
        self.sem = ctx.enter_context(nc.semaphore(name))
        self.place = {s: i + 1 for i, s in enumerate(steps)}
        assert len(self.place) == len(steps)
        self.per = len(steps)
        self.base = base
        self.last = 0

    def done(self, ins, step):
        at = self.place[step]
        assert at == self.last % self.per + 1, (step, at, self.last)
        self.last += 1
        ins.then_inc(self.sem, 1)

    def wait(self, eng, step, turn):
        eng.wait_ge(self.sem, (turn - self.base) * self.per + self.place[step])

    def open(self, eng):
        eng.sem_inc(self.sem, self.per)


def bc(ap, n):
    return ap.unsqueeze(2).broadcast_to([ap.shape[0], ap.shape[1], n])


def bcm(ap, m):
    return ap.unsqueeze(1).broadcast_to([ap.shape[0], m, ap.shape[1]])


def pieces(last):
    return [(0, SPLIT_AT, 0), (SPLIT_AT, BW, 1)] if last else [(0, BW, 0)]


def build_constants(nc, k):
    with ExitStack() as ctx:
        rows = ctx.enter_context(nc.sbuf_tensor("vec_rows", [NVEC, P], F32))
        crows = ctx.enter_context(nc.sbuf_tensor("c_rows", [NCROW, P], F32))
        ps = ctx.enter_context(nc.psum_tensor("vec_ps", [P, 512], F32))
        loaded = ctx.enter_context(nc.semaphore("vec_loaded"))
        made = ctx.enter_context(nc.semaphore("masks_made"))
        turned = ctx.enter_context(nc.semaphore("vecs_turned"))
        kept = ctx.enter_context(nc.semaphore("vecs_kept"))
        k.made_total = 0
        with nc.Block() as block:
            @block.sync
            def _(sp):
                for name, n in VECS:
                    r = VROW[name]
                    sp.dma_start(rows[r:r + n, :], k.vec_in[name].rearrange("(r p) -> r p", p=P)).then_inc(loaded, 16)
                for name, r in CROWS.items():
                    n = RT if name == "shift" else KD
                    sp.dma_start(crows[r:r + n, :], k.vec_in[name].rearrange("(r p) -> r p", p=P)).then_inc(loaded, 16)
                sp.dma_start(k.wa_up[0:64, :], k.w_lora_up).then_inc(loaded, 16)
                sp.dma_start(k.wa_up[64:128, :], k.a_lora_up).then_inc(loaded, 16)
                sp.dma_start(k.g_up[:, :], k.g_lora_up).then_inc(loaded, 16)

            @block.gpsimd
            def _(pool):
                n = [0]

                def step(ins):
                    n[0] += 1
                    ins.then_inc(made, 1)
                    pool.wait_ge(made, n[0])

                def select(out, pattern, base, cm, op, fill):
                    step(pool.affine_select(out=out, in_=out, compare_op=op, fill=fill, base=base,
                                            pattern=pattern, channel_multiplier=cm))

                step(pool.memset(k.ident[:, :], 0.0))
                select(k.ident[:, :], [[-1, P]], 0, 1, ALU.not_equal, 1.0)
                step(pool.memset(k.ii[:, :], 0.0))
                select(k.ii[:, :], [[-1, 64]], 0, 1, ALU.not_equal, 1.0)
                select(k.ii[:, :], [[-1, 64]], -64, 1, ALU.not_equal, 1.0)
                step(pool.memset(k.pair[:, :], 0.0))
                step(pool.memset(k.pair[0:64, 0:64], 1.0))
                step(pool.memset(k.pair[64:128, 64:128], 1.0))
                for m, base in ((k.m_lt, 0), (k.m_le, 1)):
                    step(pool.tensor_copy(m[:, :], k.pair[:, :]))
                    select(m[:, :], [[1, P]], base, -1, ALU.is_gt, 0.0)
                eight = k.m_lt8[:, :].rearrange("p (a b) -> p a b", b=8)
                step(pool.memset(k.m_lt8[:, :], 1.0))
                select(eight, [[-8, 16], [0, 8]], 0, 1, ALU.is_ge, 0.0)
                select(eight, [[8, 16], [0, 8]], 7, -1, ALU.is_ge, 0.0)
                step(pool.tensor_copy(k.m_gt8[:, :], k.m_lt8[:, :]))
                select(k.m_lt8[:, :], [[1, P]], 0, -1, ALU.is_gt, 0.0)
                select(k.m_gt8[:, :], [[-1, P]], 0, 1, ALU.is_gt, 0.0)
                step(pool.tensor_copy(k.m_gto[:, :], k.pair[:, :]))
                select(k.m_gto[:, :], [[-1, P]], 0, 1, ALU.is_gt, 0.0)
                step(pool.tensor_tensor(k.m_gto[:, :], k.m_gto[:, :], k.m_gt8[:, :], ALU.subtract))
                step(pool.memset(k.restart[:, :], 1.0))
                step(pool.memset(k.restart[:, :].rearrange("p (a t) -> p a t", t=C)[:, :, 0:1], 0.0))
                step(pool.memset(k.half_power[:, :], -0.5))
                step(pool.memset(k.one[:, :], 1.0))
                step(pool.memset(k.eps[:, :], EPS))
                k.made_total = n[0]

            @block.tensor
            def _(pe):
                pe.wait_ge(made, k.made_total)
                pe.wait_ge(loaded, 16 * (len(VECS) + len(CROWS) + 3))
                pe.transpose(ps[:, 0:NVEC], rows[:, :], k.ident[0:NVEC, 0:NVEC])
                pe.transpose(ps[:, 128:128 + NCROW], crows[:, :], k.ident[0:NCROW, 0:NCROW]).then_inc(turned, 1)

            @block.vector
            def _(dve):
                dve.wait_ge(turned, 1)
                dve.tensor_copy(k.vec[:, :], ps[:, 0:NVEC]).then_inc(kept, 1)
                dve.tensor_copy(k.cvec[:, :], ps[:, 128:128 + NCROW]).then_inc(kept, 1)
                dve.wait_ge(kept, 2)
                r = VROW["k_a"]
                dve.tensor_scalar(k.one_minus_ka[:, :], k.vec[:, r:r + 4], -1.0, 1.0, ALU.mult, ALU.add).then_inc(kept, 1)


def build_modulation(nc, k):
    NS, SW = 12, 512
    with ExitStack() as ctx:
        wa = ctx.enter_context(nc.sbuf_tensor("ada_w", [P, 3, KD, SW], F32))
        sil = ctx.enter_context(nc.sbuf_tensor("silu_c", [P, 2, KD], F32))
        tnh = ctx.enter_context(nc.sbuf_tensor("tanh_c", [P, 2 * KD], F32))
        ps = ctx.enter_context(nc.psum_tensor("ada_ps", [P, 48, 2], F32))
        loaded = [ctx.enter_context(nc.semaphore(f"ada_loaded{i}")) for i in range(3)]
        used = ctx.enter_context(nc.semaphore("ada_used"))
        tanh_done = ctx.enter_context(nc.semaphore("tanh_done"))
        v = ctx.enter_context(nc.semaphore("mod_steps"))
        w_ada = k.w_ada.rearrange("(k p) n -> p k n", p=P)
        with nc.Block() as block:
            @block.sync
            def _(sp):
                for s in range(NS):
                    if s >= 3:
                        sp.wait_ge(used, s - 2)
                    sp.dma_start(wa[:, s % 3], w_ada[:, :, s * SW:(s + 1) * SW]).then_inc(loaded[s % 3], 16)

            @block.scalar
            def _(act):
                act.activation(tnh[:, :], k.cvec[:, 0:2 * KD], ACT.Tanh, scale=0.5).then_inc(tanh_done, 1)

            @block.tensor
            def _(pe):
                pe.wait_ge(v, 2)
                for s in range(NS):
                    pe.wait_ge(loaded[s % 3], 16 * (s // 3 + 1))
                    for j in range(4):
                        for kk in range(KD):
                            mm = pe.matmul(ps[:, 4 * s + j, :], wa[:, s % 3, kk, j * P:(j + 1) * P], sil[:, :, kk],
                                           start=(kk == 0), stop=(kk == KD - 1))
                    mm.then_inc(used, 1)

            @block.vector
            def _(dve):
                dve.wait_ge(tanh_done, 1)
                dve.tensor_scalar(tnh[:, :], tnh[:, :], 0.5, 0.5, ALU.mult, ALU.add).then_inc(v, 1)
                dve.wait_ge(v, 1)
                dve.tensor_tensor(sil[:, :, :].rearrange("p c k -> p (c k)"), tnh[:, :], k.cvec[:, 0:2 * KD],
                                  ALU.mult).then_inc(v, 1)
                dve.wait_ge(used, NS)
                dve.tensor_tensor(k.mod[:, :, :], ps[:, :, :], bc(k.vec[:, 0:48], 2), ALU.add).then_inc(v, 1)
                dve.wait_ge(v, 3)
                n = 3
                for gain, row, sc in ((k.gain1, "norm_mix_g", 8), (k.gain2, "norm_mlp_g", 32)):
                    r = VROW[row]
                    dve.tensor_scalar(gain[:, :, :], k.mod[:, sc:sc + 8, :], 1.0, None, ALU.add).then_inc(v, 1)
                    n += 1
                    dve.wait_ge(v, n)
                    dve.tensor_tensor(gain[:, :, :], gain[:, :, :], bc(k.vec[:, r:r + 8], 2), ALU.mult).then_inc(v, 1)
                    n += 1
                dve.wait_ge(v, n)
                for b in range(NB):
                    g = 1 if b == NB - 1 else 0
                    dve.tensor_copy(k.tail[:, b, 0:8], k.gain2[:, :, g]).then_inc(v, 1)
                    dve.tensor_copy(k.tail[:, b, 8:16], k.mod[:, 24:32, g]).then_inc(v, 1)
                    dve.tensor_copy(k.tail[:, b, 16:24], k.mod[:, 40:48, g]).then_inc(v, 1)


def build_first_norm(nc, k):
    with ExitStack() as ctx:
        xt = ctx.enter_context(nc.sbuf_tensor("x_rows", [P, 2, D], F32))
        xn = ctx.enter_context(nc.sbuf_tensor("x_normed", [P, 2, D], F32))
        junk = ctx.enter_context(nc.sbuf_tensor("x_squares", [P, D], F32))
        xs = ctx.enter_context(nc.sbuf_tensor("x_turned", [P, 2, KD, P], F32))
        h = ctx.enter_context(nc.sbuf_tensor("h_tile", [P, KD, P], F32))
        ss = ctx.enter_context(nc.sbuf_tensor("x_ss", [P, 2], F32))
        rs = ctx.enter_context(nc.sbuf_tensor("x_rstd", [P, 2], F32))
        px = [ctx.enter_context(nc.psum_tensor(f"x_ps{i}", [P, KD, P], F32)) for i in range(2)]
        pn = [ctx.enter_context(nc.psum_tensor(f"xn_ps{i}", [P, KD, P], F32)) for i in range(2)]
        loaded = [ctx.enter_context(nc.semaphore(f"x_loaded{i}")) for i in range(2)]
        stored = [ctx.enter_context(nc.semaphore(f"xT_stored{i}")) for i in range(2)]
        act_s = Steps(ctx, nc, "norm1_act", ["squares", "xT"])
        pool_s = Steps(ctx, nc, "norm1_pool", ["rstd"])
        dve_s = Steps(ctx, nc, "norm1_dve", ["mean", "xn", "gain", "shift", "hi", "lo"])
        pe_s = Steps(ctx, nc, "norm1_pe", ["x", "xn"])
        xT = k.xT.rearrange("(k p) t -> p k t", p=P)
        NTILE = SEQ // P
        with nc.Block() as block:
            @block.sync
            def _(sp):
                def load(turn, par, src, n):
                    pe_s.wait(sp, "x", turn - 2)
                    dve_s.wait(sp, "xn", turn - 2)
                    sp.dma_start(xt[0:n, par, :], src).then_inc(loaded[par], 16)
                with sp.Fori(0, NTILE // 2) as i:
                    for par in range(2):
                        load(2 * i + par + 2, par, k.x_prompt[ds((2 * i + par) * P, P), :], P)
                load(NTILE + 2, 0, k.x_sample, DEC)

            @block.scalar
            def _(act):
                act_s.open(act)
                act_s.open(act)
                for par in range(2):
                    act.sem_inc(stored[par], 16)

                def tile(turn, nth, par, tok, n):
                    act.wait_ge(loaded[par], 16 * nth)
                    dve_s.wait(act, "xn", turn - 1)
                    act_s.done(act.activation(junk[0:n, :], xt[0:n, par, :], ACT.Square,
                                              accum_out=ss[0:n, par:par + 1]), "squares")
                    act.wait_ge(stored[par], 16 * nth)
                    pe_s.wait(act, "x", turn)
                    act_s.done(act.activation(xs[:, par, :, 0:n], px[par][:, :, 0:n], ACT.Copy), "xT")
                    act_s.wait(act, "xT", turn)
                    act.dma_start(xT[:, :, tok], xs[:, par, :, 0:n]).then_inc(stored[par], 16)
                with act.Fori(0, NTILE // 2) as i:
                    for par in range(2):
                        tile(2 * i + par + 2, i + 1, par, ds((2 * i + par) * P, P), P)
                tile(NTILE + 2, NTILE // 2 + 1, 0, slice(SEQ, NT), DEC)
                act.wait_ge(stored[0], 16 * (NTILE // 2 + 2))
                act.wait_ge(stored[1], 16 * (NTILE // 2 + 1))

            @block.gpsimd
            def _(pool):
                pool_s.open(pool)
                pool_s.open(pool)

                def tile(turn, par, n):
                    dve_s.wait(pool, "mean", turn)
                    pool_s.done(pool.tensor_tensor(rs[0:n, par:par + 1], rs[0:n, par:par + 1], k.half_power[0:n, 0:1], ALU.pow), "rstd")
                with pool.Fori(0, NTILE // 2) as i:
                    for par in range(2):
                        tile(2 * i + par + 2, par, P)
                tile(NTILE + 2, 0, DEC)

            @block.tensor
            def _(pe):
                pe_s.open(pe)
                pe_s.open(pe)

                def tile(turn, nth, par, n):
                    pe.wait_ge(loaded[par], 16 * nth)
                    act_s.wait(pe, "xT", turn - 2)
                    for kk in range(KD):
                        mm = pe.transpose(px[par][:, kk, 0:n], xt[0:n, par, kk * P:(kk + 1) * P], k.ident[0:n, 0:n])
                    pe_s.done(mm, "x")
                    dve_s.wait(pe, "xn", turn)
                    dve_s.wait(pe, "gain", turn - 2)
                    for kk in range(KD):
                        mm = pe.transpose(pn[par][:, kk, 0:n], xn[0:n, par, kk * P:(kk + 1) * P], k.ident[0:n, 0:n])
                    pe_s.done(mm, "xn")
                with pe.Fori(0, NTILE // 2) as i:
                    for par in range(2):
                        tile(2 * i + par + 2, i + 1, par, P)
                tile(NTILE + 2, NTILE // 2 + 1, 0, DEC)

            @block.vector
            def _(dve):
                dve_s.open(dve)
                dve_s.open(dve)

                def tile(turn, par, tok, n, g):
                    act_s.wait(dve, "squares", turn)
                    dve_s.done(dve.tensor_scalar(rs[0:n, par:par + 1], ss[0:n, par:par + 1], 1.0 / D, EPS, ALU.mult, ALU.add), "mean")
                    pool_s.wait(dve, "rstd", turn)
                    pe_s.wait(dve, "xn", turn - 2)
                    dve_s.done(dve.tensor_scalar(xn[0:n, par, :], xt[0:n, par, :], rs[0:n, par:par + 1], None, ALU.mult), "xn")
                    pe_s.wait(dve, "xn", turn)
                    dve_s.done(dve.tensor_tensor(h[:, :, 0:n], pn[par][:, :, 0:n], bc(k.gain1[:, :, g], n), ALU.mult), "gain")
                    dve_s.wait(dve, "gain", turn)
                    dve_s.done(dve.tensor_tensor(h[:, :, 0:n], h[:, :, 0:n], bc(k.mod[:, 0:8, g], n), ALU.add), "shift")
                    dve_s.wait(dve, "shift", turn)
                    dve_s.done(dve.tensor_copy(k.h_hi[:, :, tok], h[:, :, 0:n]), "hi")
                    dve_s.wait(dve, "hi", turn)
                    dve_s.done(dve.tensor_tensor(k.h_lo[:, :, tok], h[:, :, 0:n], k.h_hi[:, :, tok].bitcast(F32), ALU.subtract), "lo")
                with dve.Fori(0, NTILE // 2) as i:
                    for par in range(2):
                        tile(2 * i + par + 2, par, ds((2 * i + par) * P, P), P, 0)
                tile(NTILE + 2, 0, slice(SEQ, NT), DEC, 1)


class Projection:

    def __init__(self, ctx, nc, k):
        self.k = k
        self.raw = ctx.enter_context(nc.sbuf_tensor("w_raw", [P, KD, P], F32))
        self.hi = ctx.enter_context(nc.sbuf_tensor("w_hi", [P, 2, KD, P], F32R))
        self.lo = ctx.enter_context(nc.sbuf_tensor("w_lo", [P, 2, KD, P], F32R))
        self.out = ctx.enter_context(nc.sbuf_tensor("proj_out", [P, 2, BW], F32))
        self.ps = [ctx.enter_context(nc.psum_tensor(f"proj_ps{i}", [P, 512], F32)) for i in range(2)]
        self.loaded = ctx.enter_context(nc.semaphore("w_loaded"))
        self.stored = [ctx.enter_context(nc.semaphore(f"proj_stored{i}")) for i in range(2)]
        self.hi_s = Steps(ctx, nc, "w_hi_made", ["hi"])
        self.lo_s = Steps(ctx, nc, "w_lo_made", ["lo"])
        self.mm_s = Steps(ctx, nc, "proj_mm", [0, 1, 2, 3, 4])
        self.out_s = Steps(ctx, nc, "proj_evacuated", [0, 1, 2, 3, 4])
        self.w = k.w_in.rearrange("(k p) n -> p k n", p=P)

    def load(self, sp, turn):
        self.lo_s.wait(sp, "lo", turn - 1)
        sp.dma_start(self.raw[:, :, :], self.w[:, :, ds((turn - 2) * P, P)]).then_inc(self.loaded, 16)

    def make_hi(self, act, turn, par):
        act.wait_ge(self.loaded, 16 * (turn - 1))
        self.mm_s.wait(act, 4, turn - 2)
        self.hi_s.done(act.activation(self.hi[:, par], self.raw[:, :, :], ACT.Copy), "hi")

    def make_lo(self, pool, turn, par):
        self.hi_s.wait(pool, "hi", turn)
        self.lo_s.done(pool.tensor_tensor(self.lo[:, par], self.raw[:, :, :], self.hi[:, par].bitcast(F32), ALU.subtract), "lo")

    def products(self, pe, turn, par):
        self.lo_s.wait(pe, "lo", turn)
        for b in range(NB):
            u = (par * NB + b) % 2
            if b >= 2:
                self.out_s.wait(pe, b - 2, turn)
            else:
                self.out_s.wait(pe, b + 3, turn - 1)
            cols = slice(b * BW, (b + 1) * BW)
            for kk in range(KD):
                for j, (w, a) in enumerate(((self.hi, self.k.h_hi), (self.hi, self.k.h_lo), (self.lo, self.k.h_hi))):
                    mm = pe.matmul(self.ps[u][:, 0:BW], w[:, par, kk, :], a[:, kk, cols],
                                   start=(kk == 0 and j == 0), stop=(kk == KD - 1 and j == 2))
                    if kk == KD - 1 and j == 2:
                        self.mm_s.done(mm, b)
                    yield

    def evacuate(self, act, turn, par, b):
        u = par * NB + b
        act.wait_ge(self.stored[u % 2], 8 * NB * (turn - 2 - par) + 16 * (u // 2) + 16)
        self.mm_s.wait(act, b, turn)
        self.out_s.done(act.activation(self.out[:, u % 2, :], self.ps[u % 2][:, 0:BW], ACT.Copy), b)
        self.out_s.wait(act, b, turn)
        act.dma_start(self.k.proj[ds((turn - 2) * P, P), b * BW:(b + 1) * BW], self.out[:, u % 2, :]).then_inc(self.stored[u % 2], 16)

    def wait_stored(self, act, turns):
        for j in range(2):
            act.wait_ge(self.stored[j], 16 * (turns * NB // 2) + 16)

    def open(self, steps, eng):
        steps.open(eng)
        steps.open(eng)


def build_projection_rwkv(nc, k, pj):
    with nc.Block() as block:
        @block.sync
        def _(sp):
            pj.load(sp, 2)
            with sp.Fori(0, RT // 2) as i:
                for par in range(2):
                    pj.load(sp, 2 * i + par + 3)

        @block.scalar
        def _(act):
            pj.open(pj.hi_s, act)
            pj.open(pj.out_s, act)
            for stored in pj.stored:
                act.sem_inc(stored, 16)
            pj.make_hi(act, 2, 0)
            with act.Fori(0, RT // 2) as i:
                for par in range(2):
                    pj.make_hi(act, 2 * i + par + 3, 1 - par)
                    for b in range(NB):
                        pj.evacuate(act, 2 * i + par + 2, par, b)
            pj.wait_stored(act, RT)

        @block.gpsimd
        def _(pool):
            pj.open(pj.lo_s, pool)
            pj.make_lo(pool, 2, 0)
            with pool.Fori(0, RT // 2) as i:
                for par in range(2):
                    pj.make_lo(pool, 2 * i + par + 3, 1 - par)

        @block.tensor
        def _(pe):
            pj.open(pj.mm_s, pe)
            with pe.Fori(0, RT // 2) as i:
                for par in range(2):
                    for _product in pj.products(pe, 2 * i + par + 2, par):
                        pass


DVE_STEPS = ["diff", "scaled", "xs", "sg", "z", "sig", "scan", "t1", "t2", "k2", "ssm", "inv", "kkn", "b", "kap0", "kap1", "rho0",
             "rho1", "bh0", "bh1", "kh0", "kh1", "bv", "Nd", "Mb", "Lk", "Mk", "Ld", "Lo", "L2", "X2", "X3", "y",
             "Y2", "Q2", "Q3", "Sa", "S", "sum", "mean", "oc", "var", "varm", "on0", "on1", "yg", "yb", "yv", "yr"]
ACT_STEPS = ["tanh", "xa", "tsg", "tz", "W", "Wi", "norm", "g", "Vp", "Kt", "Bt", "N2", "L4", "yt", "Y2T", "Y4T", "RH", "R2",
             "SA", "osq"]
POOL_STEPS = ["kk", "sq", "v0", "v1", "prev", "rk", "rkk", "X1", "Q1", "rstd"]
PE_STEPS = ["wa", "g", "ss", "V", "bon", "gb", "gk", "gl", "KtT", "BtT", "N2", "L2", "X2", "L4", "X3", "y", "yt",
            "Y2T", "Y2", "Q2", "Y4T", "Q3", "RH", "R2", "SA", "O", "S", "OT"]


class Rwkv:

    def __init__(self, ctx, nc, k, pj):
        self.k, self.pj = k, pj

        def sb(name, shape):
            return ctx.enter_context(nc.sbuf_tensor(name, shape, F32))
        self.praw = sb("rows_in", [P, RT, C + 1])
        self.xs = sb("rows_mixed", [P, RT, C])
        self.th = sb("lora_in", [P, 3, C])
        self.z = sb("decay_and_a", [P, 2 * NP, C])
        self.L = sb("decay_sums", [P, NP, C])
        self.W = sb("decays", [P, NP, C + 1])
        self.kk = sb("kk", [P, NP, C])
        self.inv = sb("kk_scale", [P, NP, C])
        self.KR = sb("kap_rho_wide", [P, NP, 2, P])
        self.KB = sb("kh_bh_wide", [P, 2, NP, P])
        self.vw = sb("v_or_o_wide", [P, NP, P])
        self.Mb, self.Lk, self.Mk = (sb(n, [P, NP, P]) for n in ("rho_bh", "kap_kh", "rho_kh"))
        solve = sb("solve", [P, 6 * NP * P])
        self.R = [solve[:, j * NP * P:(j + 1) * NP * P].rearrange("p (a t) -> p a t", t=P) for j in range(6)]
        self.S = sb("state", [P, NP, C])
        self.stat = sb("o_stats", [P, 2, NP])
        late = solve[:, 4 * NP * P:4 * NP * P + RT * C].rearrange("p (a t) -> p a t", t=C)
        self.dx, self.t, self.b, self.rk = late, late[:, 0:4, :], late[:, 4:8, :], late[:, 8:12, :]
        self.sq, self.RH, self.R2, self.SA = (self.R[j][:, :, 0:C] for j in (1, 1, 2, 4))
        self.Wi = self.Vp = self.z[:, 0:NP, :]
        self.g = self.z[:, NP:2 * NP, :]
        self.osq, self.oc, self.bv = self.kk, self.inv, self.L
        self.two = [ctx.enter_context(nc.psum_tensor(f"wkv_two{j}", [P, 1024], F32)) for j in range(2)]
        one = [ctx.enter_context(nc.psum_tensor(f"wkv_ps{j}", [P, 512], F32)) for j in range(2)]
        self.bank = [self.two[j // 2][:, (j % 2) * 512:(j % 2 + 1) * 512] for j in range(4)] + [t[:, :] for t in one]
        self.rows_loaded = ctx.enter_context(nc.semaphore("rows_loaded"))
        self.cleared = ctx.enter_context(nc.semaphore("wkv_cleared"))
        self.y_stored = ctx.enter_context(nc.semaphore("yr_stored"))
        self.dve_s = Steps(ctx, nc, "wkv_dve", DVE_STEPS)
        self.act_s = Steps(ctx, nc, "wkv_act", ACT_STEPS)
        self.pool_s = Steps(ctx, nc, "wkv_pool", POOL_STEPS)
        self.pe_s = Steps(ctx, nc, "wkv_pe", PE_STEPS)

    def narrow(self, j):
        return self.bank[j][:, 0:NP * C].rearrange("p (a t) -> p a t", t=C)

    def full(self, j):
        return self.bank[j][:, :].rearrange("p (a t) -> p a t", t=P)

    def cv(self, name, n):
        r = VROW[name]
        return bc(self.k.vec[:, r:r + n], C)

    def sync_chunk(self, sp, turn, cols, n=C):
        self.pool_s.wait(sp, "prev", turn - 1)
        sp.dma_start(self.praw[:, :, 1:n + 1],
                     self.k.proj[0:R_PROJ, cols].rearrange("(r p) t -> p r t", p=P)).then_inc(self.rows_loaded, 16)

    def store_chunk(self, sp, turn, cols, n=C):
        self.dve_s.wait(sp, "yr", turn)
        sp.dma_start(self.k.yrT[:, cols].rearrange("(a p) t -> p a t", p=P), self.oc[:, :, 0:n]).then_inc(self.y_stored, 16)

    def vector_chunk(self, dve, turn, par, sample=False):
        k, R = self.k, self.R
        v, a, g, p = self.dve_s, self.act_s, self.pool_s, self.pe_s

        def op(ins, name):
            v.done(ins, name)

        def tt(out, x, y, o, name):
            v.done(dve.tensor_tensor(out, x, y, o), name)
        cur, prev = self.praw[:, :, 1:C + 1], self.praw[:, :, 0:C]
        dve.wait_ge(self.rows_loaded, 16 * turn)
        g.wait(dve, "prev", turn - 1)
        p.wait(dve, "S", turn - 1)
        p.wait(dve, "O", turn - 1)
        tt(self.dx[:, :, :], prev, cur, ALU.subtract, "diff")
        v.wait(dve, "diff", turn)
        tt(self.dx[:, :, :], self.dx[:, :, :], self.cv("mu_shift", RT), ALU.mult, "scaled")
        v.wait(dve, "scaled", turn)
        n = DEC if sample else C
        tt(self.xs[:, :, 0:n], self.dx[:, :, 0:n], cur[:, :, 0:n], ALU.add, "xs")
        a.wait(dve, "tsg", turn)
        op(dve.tensor_scalar(self.th[:, 2, :], self.th[:, 2, :], 0.5, 0.5, ALU.mult, ALU.add), "sg")
        p.wait(dve, "wa", turn)
        r = VROW["w0"]
        tt(self.z[:, :, 0:n], self.bank[0].rearrange("p (a t) -> p a t", t=C)[:, :, 0:n], bc(k.vec[:, r:r + 8], n), ALU.add, "z")
        a.wait(dve, "tz", turn)
        op(dve.tensor_scalar(self.z[:, :, 0:n], self.z[:, :, 0:n], 0.5, 0.5, ALU.mult, ALU.add), "sig")
        v.wait(dve, "sig", turn)
        op(dve.tensor_tensor_scan(self.L[:, :, :].rearrange("p a t -> p (a t)"), k.restart[:, :],
                                  self.z[:, 0:NP, :].rearrange("p a t -> p (a t)"), 0.0, ALU.mult, ALU.add), "scan")
        av = self.z[:, NP:2 * NP, :]
        tt(self.t, av, self.cv("k_a", 4), ALU.mult, "t1")
        v.wait(dve, "t1", turn)
        tt(self.t, self.t, bc(k.one_minus_ka[:, :], C), ALU.add, "t2")
        v.wait(dve, "t2", turn)
        tt(self.t, self.t, self.xs[:, 4:8, :], ALU.mult, "k2")
        a.wait(dve, "norm", turn)
        op(dve.tensor_scalar(self.inv[:, :, :], self.inv[:, :, :], 1e-12, None, ALU.max), "ssm")
        v.wait(dve, "ssm", turn)
        op(dve.reciprocal(self.inv[:, :, :], self.inv[:, :, :]), "inv")
        v.wait(dve, "inv", turn)
        tt(self.kk[:, :, :], self.kk[:, :, :], self.inv[:, :, :], ALU.mult, "kkn")
        v.wait(dve, "kkn", turn)
        tt(self.b, self.kk[:, :, :], av, ALU.mult, "b")
        a.wait(dve, "Wi", turn)
        lo, hi = slice(0, 64), slice(64, 128)
        for h, rows in ((0, lo), (1, hi)):
            tt(self.KR[rows, :, 0, rows], self.kk[rows, :, :], self.W[rows, :, 0:C], ALU.mult, f"kap{h}")
        for h, rows in ((0, lo), (1, hi)):
            tt(self.KR[rows, :, 1, rows], self.xs[rows, 0:4, :], self.W[rows, :, 1:C + 1], ALU.mult, f"rho{h}")
        v.wait(dve, "b", turn)
        for h, rows in ((0, lo), (1, hi)):
            op(dve.scalar_tensor_tensor(out=self.KB[rows, 1, :, rows], in0=self.b[rows], scalar=-1.0,
                                        in1=self.Wi[rows], op0=ALU.mult, op1=ALU.mult), f"bh{h}")
        for h, rows in ((0, lo), (1, hi)):
            tt(self.KB[rows, 0, :, rows], self.t[rows], self.Wi[rows], ALU.mult, f"kh{h}")
        p.wait(dve, "bon", turn)
        tt(self.bv[:, :, :], self.narrow(3), self.xs[:, 8:12, :], ALU.mult, "bv")
        both = [self.two[0][:, :].rearrange("p (a w t) -> p a w t", a=NP, w=2), self.two[1][:, :].rearrange("p (a w t) -> p a w t", a=NP, w=2)]
        p.wait(dve, "gb", turn)
        tt(R[0][:, :, :], both[0][:, :, 0, :], bcm(k.m_lt8[:, :], NP), ALU.mult, "Nd")
        tt(self.Mb[:, :, :], both[0][:, :, 1, :], bcm(k.m_le[:, :], NP), ALU.mult, "Mb")
        p.wait(dve, "gk", turn)
        tt(self.Lk[:, :, :], both[1][:, :, 0, :], bcm(k.m_lt[:, :], NP), ALU.mult, "Lk")
        tt(self.Mk[:, :, :], both[1][:, :, 1, :], bcm(k.m_le[:, :], NP), ALU.mult, "Mk")
        p.wait(dve, "gl", turn)
        tt(R[1][:, :, :], self.full(4), bcm(k.m_gt8[:, :], NP), ALU.mult, "Ld")
        tt(R[2][:, :, :], self.full(4), bcm(k.m_gto[:, :], NP), ALU.mult, "Lo")
        p.wait(dve, "L2", turn)
        op(dve.tensor_copy(R[4][:, :, :], self.full(2)), "L2")
        p.wait(dve, "X2", turn)
        g.wait(dve, "X1", turn)
        tt(R[0][:, :, :], self.full(3), R[5][:, :, :], ALU.add, "X2")
        p.wait(dve, "X3", turn)
        v.wait(dve, "X2", turn)
        tt(R[3][:, :, :], self.full(5), R[0][:, :, :], ALU.add, "X3")
        p.wait(dve, "y", turn)
        op(dve.tensor_copy(R[4][:, :, :], self.full(0)), "y")
        p.wait(dve, "Y2", turn)
        op(dve.tensor_copy(R[1][:, :, :], self.full(3)), "Y2")
        p.wait(dve, "Q2", turn)
        g.wait(dve, "Q1", turn)
        tt(R[5][:, :, :], self.full(4), R[2][:, :, :], ALU.add, "Q2")
        p.wait(dve, "Q3", turn)
        v.wait(dve, "Q2", turn)
        tt(R[0][:, :, :], self.full(0), R[5][:, :, :], ALU.add, "Q3")
        p.wait(dve, "S", turn)
        tt(self.S[:, :, :], self.narrow(5), self.S[:, :, :], ALU.add, "Sa")
        v.wait(dve, "Sa", turn)
        tt(self.S[:, :, :], self.S[:, :, :], self.W[:, :, C:C + 1].broadcast_to([P, NP, C]), ALU.mult, "S")
        op(dve.tensor_reduce(self.stat[:, 0, :], self.narrow(4), AX.X, ALU.add), "sum")
        v.wait(dve, "sum", turn)
        op(dve.tensor_scalar(self.stat[:, 0, :], self.stat[:, 0, :], 1.0 / HD, None, ALU.mult), "mean")
        v.wait(dve, "mean", turn)
        tt(self.oc[:, :, :], self.narrow(4), bc(self.stat[:, 0, :], C), ALU.subtract, "oc")
        a.wait(dve, "osq", turn)
        op(dve.tensor_reduce(self.stat[:, 1, :], self.osq[:, :, :], AX.X, ALU.add), "var")
        v.wait(dve, "var", turn)
        op(dve.tensor_scalar(self.stat[:, 1, :], self.stat[:, 1, :], 1.0 / HD, GN_EPS, ALU.mult, ALU.add), "varm")
        g.wait(dve, "rstd", turn)
        for h, rows in ((0, lo), (1, hi)):
            tt(self.vw[rows, :, rows], self.oc[rows, :, :], bc(self.stat[rows, 1, :], C), ALU.mult, f"on{h}")
        p.wait(dve, "OT", turn)
        tt(self.oc[:, :, :], self.narrow(0), self.cv("lnx_g", 4), ALU.mult, "yg")
        v.wait(dve, "yg", turn)
        tt(self.oc[:, :, :], self.oc[:, :, :], self.cv("lnx_b", 4), ALU.add, "yb")
        v.wait(dve, "yb", turn)
        tt(self.oc[:, :, :], self.oc[:, :, :], self.bv[:, :, :], ALU.add, "yv")
        v.wait(dve, "yv", turn)
        tt(self.oc[:, :, :], self.oc[:, :, :], self.g[:, :, :], ALU.mult, "yr")

    def scalar_chunk(self, act, turn, par, evac):
        v, a, p = self.dve_s, self.act_s, self.pe_s

        def f(out, x, func, name, **kw):
            a.done(act.activation(out, x, func, **kw), name)
        v.wait(act, "xs", turn)
        p.wait(act, "wa", turn - 1)
        p.wait(act, "g", turn - 1)
        f(self.th[0:64, 0, :], self.xs[0:64, 12, :], ACT.Tanh, "tanh")
        f(self.th[64:128, 1, :], self.xs[64:128, 12, :], ACT.Copy, "xa")
        f(self.th[:, 2, :], self.xs[:, 13, :], ACT.Tanh, "tsg", scale=0.5)
        v.wait(act, "z", turn)
        f(self.z[:, :, :], self.z[:, :, :], ACT.Tanh, "tz", scale=0.5)
        evac(0)
        v.wait(act, "scan", turn)
        f(self.W[:, :, 1:C + 1], self.L[:, :, :], ACT.Exp, "W", scale=-KAPPA)
        f(self.Wi[:, :, :], self.L[:, :, :], ACT.Exp, "Wi", scale=KAPPA)
        p.wait(act, "ss", turn)
        act.wait_ge(self.y_stored, 16 * turn)
        f(self.inv[:, :, :], self.narrow(2), ACT.Sqrt, "norm")
        p.wait(act, "g", turn)
        v.wait(act, "b", turn)
        f(self.g, self.narrow(1), ACT.Copy, "g")
        p.wait(act, "V", turn)
        v.wait(act, "kh1", turn)
        f(self.Vp[:, :, :], self.narrow(5), ACT.Copy, "Vp")
        evac(1)
        p.wait(act, "KtT", turn)
        f(self.KB[:, 0], self.full(5), ACT.Copy, "Kt")
        p.wait(act, "BtT", turn)
        f(self.KB[:, 1], self.full(0), ACT.Copy, "Bt")
        evac(2)
        p.wait(act, "N2", turn)
        f(self.R[3][:, :, :], self.full(1), ACT.Copy, "N2")
        p.wait(act, "L4", turn)
        f(self.R[1][:, :, :], self.full(4), ACT.Copy, "L4")
        p.wait(act, "yt", turn)
        f(self.R[5][:, :, :], self.full(1), ACT.Copy, "yt")
        evac(3)
        p.wait(act, "Y2T", turn)
        f(self.R[0][:, :, :], self.full(2), ACT.Copy, "Y2T")
        p.wait(act, "Y4T", turn)
        f(self.R[4][:, :, :], self.full(5), ACT.Copy, "Y4T")
        p.wait(act, "RH", turn)
        f(self.RH, self.narrow(1), ACT.Copy, "RH")
        p.wait(act, "R2", turn)
        f(self.R2, self.narrow(2), ACT.Copy, "R2")
        p.wait(act, "SA", turn)
        f(self.SA, self.narrow(3), ACT.Copy, "SA")
        evac(4)
        v.wait(act, "oc", turn)
        f(self.osq[:, :, :], self.oc[:, :, :], ACT.Square, "osq")

    def pool_chunk(self, pool, turn, par, lo_turn):
        k = self.k
        v, a, g, p = self.dve_s, self.act_s, self.pool_s, self.pe_s

        def tt(out, x, y, o, name):
            g.done(pool.tensor_tensor(out, x, y, o), name)
        v.wait(pool, "xs", turn)
        tt(self.kk[:, :, :], self.xs[:, 4:8, :], self.cv("k_k", 4), ALU.mult, "kk")
        g.wait(pool, "kk", turn)
        tt(self.sq[:, :, :], self.kk[:, :, :], self.kk[:, :, :], ALU.mult, "sq")
        p.wait(pool, "OT", turn - 1)
        for h in range(2):
            rows = slice(64 * h, 64 * h + 64)
            g.wait(pool, ("sq", "v0")[h], turn)
            tt(self.vw[rows, :, rows], self.xs[rows, 8:12, :], bc(k.one[rows, :].broadcast_to([64, NP]), C), ALU.mult, f"v{h}")
        g.wait(pool, "v1", turn)
        tt(self.praw[:, :, 0:1], self.praw[:, :, C:C + 1], bc(k.one[:, :].broadcast_to([P, RT]), 1), ALU.mult, "prev")
        v.wait(pool, "k2", turn)
        tt(self.rk, self.xs[:, 0:4, :], self.t, ALU.mult, "rk")
        g.wait(pool, "rk", turn)
        tt(self.rk, self.rk, self.cv("r_k", 4), ALU.mult, "rkk")
        v.wait(pool, "Nd", turn)
        p.wait(pool, "SA", turn - 1)
        tt(self.R[5][:, :, :], self.R[0][:, :, :], bcm(k.ident[:, :], NP), ALU.add, "X1")
        v.wait(pool, "y", turn)
        p.wait(pool, "yt", turn)
        tt(self.R[2][:, :, :], self.R[4][:, :, :], bcm(k.ident[:, :], NP), ALU.add, "Q1")
        if lo_turn is not None:
            self.pj.make_lo(pool, lo_turn, 1 - par)
        v.wait(pool, "varm", turn)
        tt(self.stat[:, 1, :], self.stat[:, 1, :], k.half_power[:, 0:1].broadcast_to([P, NP]), ALU.pow, "rstd")

    def tensor_chunk(self, pe, turn, fill):
        k, R = self.k, self.R
        v, a, g, p = self.dve_s, self.act_s, self.pool_s, self.pe_s

        def wide(bank, lhs, rhs, name):
            for j in range(NP):
                mm = pe.matmul(self.bank[bank][:, j * P:(j + 1) * P], lhs[:, j, :], rhs[:, j, :], start=True, stop=True)
            p.done(mm, name)

        def packed(bank, terms, name):
            for j in range(NP):
                for n, (lhs, rhs) in enumerate(terms):
                    mm = pe.matmul(self.bank[bank][:, j * C:(j + 1) * C], lhs[:, j, :], rhs[:, j, :],
                                   start=(n == 0), stop=(n == len(terms) - 1))
            p.done(mm, name)
        fill(20)
        a.wait(pe, "xa", turn)
        v.wait(pe, "yg", turn - 1)
        for j in range(2 * NP):
            mm = pe.matmul(self.bank[0][:, j * C:(j + 1) * C], k.wa_up[:, (j % NP) * P:(j % NP + 1) * P], self.th[:, j // NP, :],
                           start=True, stop=True)
        p.done(mm, "wa")
        v.wait(pe, "sg", turn)
        for j in range(NP):
            mm = pe.matmul(self.bank[1][:, j * C:(j + 1) * C], k.g_up[:, j * P:(j + 1) * P], self.th[:, 2, :],
                           start=True, stop=True)
        p.done(mm, "g")
        fill(14)
        g.wait(pe, "sq", turn)
        p.done(pe.matmul(self.narrow(2), k.pair[:, :], self.sq,
                         start=True, stop=True), "ss")
        fill(20)
        g.wait(pe, "v1", turn)
        v.wait(pe, "Sa", turn - 1)
        for j in range(NP):
            mm = pe.matmul(self.bank[5][:, j * C:(j + 1) * C], self.vw[:, j, :], k.ii[:, :], start=True, stop=True)
        p.done(mm, "V")
        g.wait(pe, "rkk", turn)
        p.done(pe.matmul(self.narrow(3), k.pair[:, :], self.rk,
                         start=True, stop=True), "bon")
        fill(16)
        v.wait(pe, "kh1", turn)
        a.wait(pe, "g", turn)
        for j in range(NP):
            mm = pe.matmul(self.two[0][:, j * 256:(j + 1) * 256], self.KB[:, 1, j, :],
                           self.KR[:, j, :, :].rearrange("p w t -> p (w t)"), start=True, stop=True)
        p.done(mm, "gb")
        v.wait(pe, "bv", turn)
        for j in range(NP):
            mm = pe.matmul(self.two[1][:, j * 256:(j + 1) * 256], self.KB[:, 0, j, :],
                           self.KR[:, j, :, :].rearrange("p w t -> p (w t)"), start=True, stop=True)
        p.done(mm, "gk")
        v.wait(pe, "oc", turn - 1)
        wide(4, self.KR[:, :, 0, :], self.KB[:, 1], "gl")
        a.wait(pe, "Vp", turn)
        for j in range(NP):
            mm = pe.transpose(self.bank[5][:, j * P:(j + 1) * P], self.KB[:, 0, j, :], k.ident[:, :])
        p.done(mm, "KtT")
        v.wait(pe, "Mb", turn)
        for j in range(NP):
            mm = pe.transpose(self.bank[0][:, j * P:(j + 1) * P], self.KB[:, 1, j, :], k.ident[:, :])
        p.done(mm, "BtT")
        fill(10)
        v.wait(pe, "Lo", turn)
        wide(1, R[1], R[0], "N2")
        wide(2, R[0], R[1], "L2")
        fill(5)
        v.wait(pe, "L2", turn)
        g.wait(pe, "X1", turn)
        wide(3, R[4], R[5], "X2")
        a.wait(pe, "N2", turn)
        wide(4, R[3], R[4], "L4")
        fill(5)
        a.wait(pe, "L4", turn)
        v.wait(pe, "X2", turn)
        wide(5, R[1], R[0], "X3")
        fill(5)
        v.wait(pe, "X3", turn)
        wide(0, R[2], R[3], "y")
        wide(1, R[3], R[2], "yt")
        fill(5)
        v.wait(pe, "y", turn)
        a.wait(pe, "yt", turn)
        wide(2, R[4], R[5], "Y2T")
        wide(3, R[5], R[4], "Y2")
        fill(5)
        a.wait(pe, "Y2T", turn)
        g.wait(pe, "Q1", turn)
        wide(4, R[0], R[2], "Q2")
        v.wait(pe, "Y2", turn)
        wide(5, R[1], R[0], "Y4T")
        fill(5)
        a.wait(pe, "Y4T", turn)
        v.wait(pe, "Q2", turn)
        wide(0, R[4], R[5], "Q3")
        v.wait(pe, "S", turn - 1)
        packed(1, [(self.KR[:, :, 0, :], self.S), (self.Lk, self.Vp)], "RH")
        fill(3)
        a.wait(pe, "RH", turn)
        packed(2, [(R[3], self.RH)], "R2")
        fill(3)
        a.wait(pe, "R2", turn)
        v.wait(pe, "Q3", turn)
        packed(3, [(R[0], self.R2)], "SA")
        fill(4)
        a.wait(pe, "SA", turn)
        packed(4, [(self.KR[:, :, 1, :], self.S), (self.Mb, self.SA), (self.Mk, self.Vp)], "O")
        packed(5, [(self.KB[:, 0], self.Vp), (self.KB[:, 1], self.SA)], "S")
        v.wait(pe, "on1", turn)
        for j in range(NP):
            mm = pe.matmul(self.bank[0][:, j * C:(j + 1) * C], self.vw[:, j, :], k.ii[:, :], start=True, stop=True)
        p.done(mm, "OT")


def build_rwkv(nc, k, pj):
    FILLED = IN_T - RT
    LOOPED = 26
    with ExitStack() as ctx:
        w = Rwkv(ctx, nc, k, pj)
        with nc.Block() as block:
            @block.gpsimd
            def _(pool):
                w.pool_s.open(pool)
                for buf in (w.KR, w.KB, w.vw, w.S):
                    pool.memset(buf[:], 0.0)
                pool.memset(w.praw[:, :, 0:1], 0.0)
                pool.memset(w.th[:, 0:2, :], 0.0)
                pool.memset(w.W[:, :, 0:1], 1.0).then_inc(w.cleared, 1)

            @block.vector
            def _(dve):
                w.dve_s.open(dve)
                dve.sem_inc(w.y_stored, 16)

            @block.scalar
            def _(act):
                w.act_s.open(act)

            @block.tensor
            def _(pe):
                w.pe_s.open(pe)

        def each_chunk(eng, body):
            with eng.Fori(0, LOOPED // 2) as i:
                for par in range(2):
                    body(2 * i + par, par)
            for c in range(LOOPED, NCH):
                body(c, c % 2)

        def filled(c):
            return not isinstance(c, int) or c < FILLED

        def preloads(c):
            return not isinstance(c, int) or c < FILLED - 1

        with nc.Block() as block:
            @block.sync
            def _(sp):
                w.sync_chunk(sp, 1, slice(0, C))

                def body(c, par):
                    if preloads(c):
                        pj.load(sp, c + RT + 3)
                    if not isinstance(c, int) or c + 1 < NCH:
                        w.sync_chunk(sp, c + 2, ds((c + 1) * C, C))
                    w.store_chunk(sp, c + 1, ds(c * C, C))
                each_chunk(sp, body)
                sp.wait_ge(w.y_stored, 16 * (NCH + 1))

            @block.scalar
            def _(act):
                def body(c, par):
                    if preloads(c):
                        pj.make_hi(act, c + RT + 3, 1 - par)

                    def evac(b):
                        if filled(c):
                            pj.evacuate(act, c + RT + 2, par, b)
                    w.scalar_chunk(act, c + 1, par, evac)
                each_chunk(act, body)
                pj.wait_stored(act, IN_T)

            @block.vector
            def _(dve):
                each_chunk(dve, lambda c, par: w.vector_chunk(dve, c + 1, par))

            @block.gpsimd
            def _(pool):
                each_chunk(pool, lambda c, par: w.pool_chunk(pool, c + 1, par, c + RT + 3 if preloads(c) else None))

            @block.tensor
            def _(pe):
                def body(c, par):
                    products = pj.products(pe, c + RT + 2, par) if filled(c) else iter(())

                    def fill(n):
                        for _i in range(n):
                            if next(products, 0) == 0:
                                break
                    w.tensor_chunk(pe, c + 1, fill)
                    for _rest in products:
                        pass
                each_chunk(pe, body)

        turn_state(nc, k, w, out=k.p_wkv, shift=k.p_shift, last=C, load=True)
        T = NCH + 1
        with nc.Block() as block:
            @block.sync
            def _(sp):
                sp.dma_start(w.praw[:, :, 1:DEC + 1], k.proj[0:R_PROJ, SEQ:NT].rearrange("(r p) t -> p r t", p=P))\
                    .then_inc(w.rows_loaded, 16)
                w.store_chunk(sp, T, slice(SEQ, NT), DEC)
                sp.wait_ge(w.y_stored, 16 * (NCH + 2))

            @block.scalar
            def _(act):
                w.scalar_chunk(act, T, 0, lambda b: None)

            @block.vector
            def _(dve):
                w.vector_chunk(dve, T, 0, sample=True)

            @block.gpsimd
            def _(pool):
                w.pool_chunk(pool, T, 0, None)

            @block.tensor
            def _(pe):
                w.tensor_chunk(pe, T, lambda n: None)
        turn_state(nc, k, w, out=k.s_wkv, shift=k.s_shift, last=DEC, load=False)


def turn_state(nc, k, w, out, shift, last, load):
    tag = "p" if load else "s"
    with ExitStack() as ctx:
        done = ctx.enter_context(nc.semaphore(f"state_turned_{tag}"))
        kept = ctx.enter_context(nc.semaphore(f"state_kept_{tag}"))
        stored = ctx.enter_context(nc.semaphore(f"state_stored_{tag}"))
        loaded = ctx.enter_context(nc.semaphore(f"state_loaded_{tag}"))
        vk = w.R[1][0:64, :, :]
        vk_in = w.R[2][0:64, :, :]
        with nc.Block() as block:
            @block.tensor
            def _(pe):
                for j in range(NP):
                    mm = pe.transpose(w.bank[0][0:64, j * P:(j + 1) * P], w.S[:, j, :], k.ident[:, :])
                mm.then_inc(done, 1)
                if load:
                    pe.wait_ge(loaded, 16)
                    for j in range(NP):
                        mm = pe.transpose(w.bank[1][:, j * C:(j + 1) * C], vk_in[:, j, :], k.ident[0:64, 0:64])
                    mm.then_inc(done, 1)

            @block.vector
            def _(dve):
                dve.wait_ge(done, 1)
                dve.tensor_copy(vk, w.full(0)[0:64]).then_inc(kept, 1)
                if load:
                    dve.wait_ge(done, 2)
                    dve.tensor_copy(w.S[:, :, :], w.narrow(1)).then_inc(kept, 1)

            @block.sync
            def _(sp):
                if load:
                    sp.dma_start(vk_in.rearrange("v j (h k) -> v (j h) k", k=HD), k.s_in.rearrange("h v k -> v h k")).then_inc(loaded, 16)
                col = last
                sp.dma_start(shift.rearrange("(r p) -> p r", p=P), w.praw[:, :, col],
                             allow_slow_non_contiguous=True).then_inc(stored, 16)
                sp.wait_ge(kept, 1)
                sp.dma_start(out.rearrange("h v k -> v h k"), vk.rearrange("v j (h k) -> v (j h) k", k=HD)).then_inc(stored, 16)
                sp.wait_ge(stored, 32)

            @block.gpsimd
            def _(pool):
                if load:
                    pool.wait_ge(stored, 32)
                    pool.tensor_copy(w.praw[:, :, 0:1], k.cvec[:, 2 * KD:2 * KD + RT].unsqueeze(2))
                    pool.memset(w.praw[:, :, DEC + 1:C + 1], 0.0)
                    pool.memset(w.xs[:, :, DEC:C], 0.0)
                    pool.memset(w.z[:, :, DEC:C], 0.0)


QW, KT5 = P, BAND // P
NQ = SEQ // P
SKEYS = PAST + DEC


def build_attention(nc, k):
    with ExitStack() as ctx:
        def sb(name, shape):
            return ctx.enter_context(nc.sbuf_tensor(name, shape, F32))
        a = Tensors()
        a.qT, a.kT = sb("qT", [P, NP, NT]), sb("kT", [P, NP, NT])
        a.V = sb("v_rows", [P, NQ + 1, DR])
        a.bias = sb("bias", [P, NH, BAND])
        a.sbias = sb("sample_bias", [DEC, NH, SKEYS])
        a.bias_ready = ctx.enter_context(nc.semaphore("bias_ready"))
        a.rows_ready = ctx.enter_context(nc.semaphore("v_rows_ready"))
        build_attention_rows(nc, k, a)
        build_bias(nc, k, a)
        build_attention_core(nc, k, a)


def build_attention_rows(nc, k, a):
    KEEP0 = (SEQ - WIN) // P
    with ExitStack() as ctx:
        vT = ctx.enter_context(nc.sbuf_tensor("vT", [P, 2, NP, P], F32))
        krow = ctx.enter_context(nc.sbuf_tensor("k_rows", [P, 2, DR], F32))
        pv = [ctx.enter_context(nc.psum_tensor(f"v_ps{i}", [P, 512], F32)) for i in range(2)]
        pk = [ctx.enter_context(nc.psum_tensor(f"k_ps{i}", [P, 512], F32)) for i in range(2)]
        qk_loaded = ctx.enter_context(nc.semaphore("qk_loaded"))
        v_loaded = [ctx.enter_context(nc.semaphore(f"v_loaded{i}")) for i in range(2)]
        turned = ctx.enter_context(nc.semaphore("v_turned"))
        kept = ctx.enter_context(nc.semaphore("v_kept"))
        k_turned = ctx.enter_context(nc.semaphore("k_turned"))
        k_kept = ctx.enter_context(nc.semaphore("k_kept"))
        k_stored = [ctx.enter_context(nc.semaphore(f"k_stored{i}")) for i in range(2)]
        v_stored = ctx.enter_context(nc.semaphore("v_stored"))
        rows = k.proj.rearrange("(r p) t -> p r t", p=P)
        kept_tiles = [j for j in range(KEEP0, NQ + 1)]

        def size(j):
            return P if j < NQ else DEC
        with nc.Block() as block:
            @block.sync
            def _(sp):
                for j in range(NQ + 1):
                    if j >= 2:
                        sp.wait_ge(turned, j - 1)
                    sp.dma_start(vT[:, j % 2, :, 0:size(j)], rows[:, VT:VT + NP, j * P:j * P + size(j)]).then_inc(v_loaded[j % 2], 16)
                    if j == 1:
                        sp.dma_start(a.kT[:, :, :], rows[:, KT_:KT_ + NP, :]).then_inc(qk_loaded, 16)
                        sp.dma_start(a.qT[:, :, :], rows[:, QT:QT + NP, :]).then_inc(qk_loaded, 16)
                sp.wait_ge(kept, NQ + 1)
                sp.dma_start(k.p_v.rearrange("(j p) h d -> p j (h d)", p=P), a.V[:, KEEP0:NQ, :]).then_inc(v_stored, 16)
                sp.dma_start(k.s_v.rearrange("p h d -> p (h d)"), a.V[0:DEC, NQ, :]).then_inc(v_stored, 16)
                sp.wait_ge(v_stored, 32)
                sp.wait_ge(qk_loaded, 32)

            @block.tensor
            def _(pe):
                for j in range(NQ + 1):
                    pe.wait_ge(v_loaded[j % 2], 16 * (j // 2 + 1))
                    if j >= 2:
                        pe.wait_ge(kept, j - 1)
                    for i in range(NP):
                        mm = pe.transpose(pv[j % 2][0:size(j), i * P:(i + 1) * P], vT[:, j % 2, i, 0:size(j)], k.ident[:, :])
                    mm.then_inc(turned, 1)
                pe.wait_ge(qk_loaded, 32)
                for n, j in enumerate(kept_tiles):
                    if n >= 2:
                        pe.wait_ge(k_kept, n - 1)
                    for i in range(NP):
                        mm = pe.transpose(pk[n % 2][0:size(j), i * P:(i + 1) * P], a.kT[:, i, j * P:j * P + size(j)], k.ident[:, :])
                    mm.then_inc(k_turned, 1)

            @block.vector
            def _(dve):
                for j in range(NQ + 1):
                    dve.wait_ge(turned, j + 1)
                    dve.tensor_copy(a.V[0:size(j), j, :], pv[j % 2][0:size(j), :]).then_inc(kept, 1)
                dve.wait_ge(kept, NQ + 1)
                dve.sem_inc(a.rows_ready, 1)

            @block.scalar
            def _(act):
                for n, j in enumerate(kept_tiles):
                    act.wait_ge(k_turned, n + 1)
                    if n >= 2:
                        act.wait_ge(k_stored[n % 2], 16 * (n // 2))
                    act.activation(krow[0:size(j), n % 2, :], pk[n % 2][0:size(j), :], ACT.Copy).then_inc(k_kept, 1)
                    act.wait_ge(k_kept, n + 1)
                    dst = k.p_k[(j - KEEP0) * P:(j - KEEP0 + 1) * P] if j < NQ else k.s_k
                    act.dma_start(dst.rearrange("p h d -> p (h d)"), krow[0:size(j), n % 2, :]).then_inc(k_stored[n % 2], 16)
                act.wait_ge(k_stored[0], 16 * 3)
                act.wait_ge(k_stored[1], 16 * 2)


def build_bias(nc, k, a):
    with ExitStack() as ctx:
        tab = ctx.enter_context(nc.sbuf_tensor("table", [NH, 2 * REL + 1], F32))
        ext = ctx.enter_context(nc.sbuf_tensor("distances", [NH, EXT], F32))
        rev = ctx.enter_context(nc.sbuf_tensor("bias_backwards", [P, 2, BAND], F32))
        srev = ctx.enter_context(nc.sbuf_tensor("sample_bias_backwards", [DEC, NH, SKEYS], F32))
        tab_loaded = ctx.enter_context(nc.semaphore("table_loaded"))
        made = ctx.enter_context(nc.semaphore("distances_made"))
        written = ctx.enter_context(nc.semaphore("distances_written"))
        back = [ctx.enter_context(nc.semaphore(f"bias_loaded{i}")) for i in range(2)]
        sback = ctx.enter_context(nc.semaphore("sample_bias_loaded"))
        turned = ctx.enter_context(nc.semaphore("bias_turned"))
        with nc.Block() as block:
            @block.sync
            def _(sp):
                sp.dma_start(tab[:, :], k.rel_table).then_inc(tab_loaded, 16)
                sp.wait_ge(made, 2)
                sp.dma_start(k.ext, ext[:, :]).then_inc(written, 16)
                sp.wait_ge(written, 16)
                sp.dma_start(srev[:, :, :], bass.AP(tensor=k.ext.tensor, offset=96, ap=[[1, DEC], [EXT, NH], [1, SKEYS]])).then_inc(sback, 16)
                for h in range(NH):
                    if h >= 2:
                        sp.wait_ge(turned, h - 1)
                    sp.dma_start(rev[:, h % 2, :], bass.AP(tensor=k.ext.tensor, offset=h * EXT, ap=[[1, P], [1, BAND]])).then_inc(back[h % 2], 16)

            @block.vector
            def _(dve):
                dve.wait_ge(tab_loaded, 16)
                near = REL + P - 1
                dve.tensor_copy(ext[:, 0:near], tab[:, 1:near + 1]).then_inc(made, 1)
                dve.tensor_copy(ext[:, near:EXT], tab[:, 2 * REL:2 * REL + 1].broadcast_to([NH, EXT - near])).then_inc(made, 1)
                for h in range(NH):
                    dve.wait_ge(back[h % 2], 16 * (h // 2 + 1))
                    dve.tensor_copy(a.bias[:, h, :], rev[:, h % 2, ::-1]).then_inc(turned, 1)
                dve.wait_ge(turned, NH)
                dve.memset(a.bias[0:64, :, BAND - 64:BAND], NEG)
                dve.memset(a.bias[64:128, :, 0:64], NEG)
                dve.wait_ge(sback, 16)
                dve.tensor_copy(a.sbias[:, :, :], srev[:, :, ::-1]).then_inc(a.bias_ready, 1)


class Heads:

    def __init__(self, ctx, nc, k, a):
        self.k, self.a = k, a

        def sb(name, shape):
            return ctx.enter_context(nc.sbuf_tensor(name, shape, F32))
        self.q = sb("q_tile", [P, NP, P])
        self.K = sb("k_window", [P, NP, BAND])
        self.Vw = sb("v_window", [P, KT5, DR])
        self.s = sb("scores", [P, 2, BAND])
        self.e = sb("probs", [P, 2, BAND])
        self.eT = sb("probs_turned", [P, 2, BAND])
        self.nmax, self.sum, self.rec = sb("minus_max", [P, NH]), sb("prob_sums", [P, NH]), sb("prob_recips", [P, NH])
        self.idle = sb("idle", [P, 2, NH])
        self.Y = sb("att_rows", [P, DR])
        self.yT = sb("att_turned", [P, NP, P])
        self.ps_s = [ctx.enter_context(nc.psum_tensor(f"scores_ps{j}", [P, 1024], F32)) for j in range(2)]
        self.ps_t = ctx.enter_context(nc.psum_tensor("probs_ps", [P, 2, 512], F32))
        self.ps_y = ctx.enter_context(nc.psum_tensor("att_ps", [P, 512], F32))
        self.ps_o = ctx.enter_context(nc.psum_tensor("att_turned_ps", [P, 512], F32))
        self.stored = ctx.enter_context(nc.semaphore("ya_stored"))
        order = []
        for h in range(NH + 1):
            order += [("s", h)] * (h < NH) + [("t", h - 1)] * (h >= 1)
        self.dve_s = Steps(ctx, nc, "att_dve", ["K"] + order + ["rec", "Y"])
        self.act_s = Steps(ctx, nc, "att_act", ["q"] + [("e" if s == "s" else "t", h) for s, h in order] + ["yT"])
        self.pool_s = Steps(ctx, nc, "att_pool", ["V"])
        pe = [("s", 0), ("s", 1)]
        for h in range(NH):
            pe += [("t", h)] + [("s", h + 2)] * (h + 2 < NH) + [("y", h)]
        self.pe_s = Steps(ctx, nc, "att_pe", pe + ["yT"])
        self.order = order

    @staticmethod
    def tiles(c0, c1):
        return [(c, min(P, c1 - c)) for c in range(c0, c1, P)]

    def vector_tile(self, dve, turn, key_src, nq, c0, c1, bias):
        v, a, g, p = self.dve_s, self.act_s, self.pool_s, self.pe_s
        p.wait(dve, ("s", NH - 1), turn - 1)
        key_src(dve)
        for s, h in self.order:
            if s == "s":
                a.wait(dve, ("e", h - 2), turn) if h >= 2 else a.wait(dve, ("e", h + NH - 2), turn - 1)
                p.wait(dve, ("s", h), turn)
                dve.memset(self.idle[:, 0, h:h + 1], 0.0)
                v.done(dve.tensor_tensor_reduce(self.s[0:nq, h % 2, c0:c1], self.ps_s[h % 2][0:nq, c0:c1], bias(h), -1.0, 3.0e38,
                                                ALU.add, ALU.min, self.nmax[0:nq, h:h + 1]), (s, h))
            else:
                p.wait(dve, ("t", h), turn)
                ins = self.take_turned(dve.tensor_copy, 0, h, nq, c0, c1)
                if ins is None:
                    ins = dve.memset(self.idle[:, 1, h:h + 1], 0.0)
                v.done(ins, (s, h))
        a.wait(dve, ("e", NH - 1), turn)
        v.done(dve.reciprocal(self.rec[0:nq, :], self.sum[0:nq, :]), "rec")
        v.wait(dve, "rec", turn)
        p.wait(dve, ("y", NH - 1), turn)
        v.done(dve.tensor_tensor(self.Y[0:nq, :].rearrange("p (h d) -> p h d", d=HD),
                                 self.ps_y[0:nq, :].rearrange("p (h d) -> p h d", d=HD),
                                 bc(self.rec[0:nq, :], HD), ALU.mult), "Y")

    def take_turned(self, copy, part, h, nq, c0, c1):
        first, full, last = c0 // P, c1 // P, (c1 + P - 1) // P
        ins = None
        for n, t0, t1 in ((P, first, full), (c1 - full * P, full, last)):
            t0, t1 = max(t0, 2 * part), min(t1, (2, KT5)[part])
            if t1 > t0:
                out = self.eT[0:n, h % 2, t0 * P:t1 * P].rearrange("p (c t) -> p c t", t=P)[:, :, 0:nq]
                src = self.ps_t[0:n, part, (t0 - 2 * part) * P:(t1 - 2 * part) * P].rearrange("p (c t) -> p c t", t=P)[:, :, 0:nq]
                ins = copy(out, src)
        return ins

    def scalar_tile(self, act, turn, q_src, nq, c0, c1, out_cols):
        v, a, g, p = self.dve_s, self.act_s, self.pool_s, self.pe_s
        a.done(act.activation(self.q[:, :, 0:nq], q_src, ACT.Copy, scale=HD ** -0.5), "q")
        for s, h in self.order:
            if s == "s":
                v.wait(act, ("s", h), turn)
                p.wait(act, ("t", h - 2), turn) if h >= 2 else p.wait(act, ("t", h + NH - 2), turn - 1)
                a.done(act.activation(self.e[0:nq, h % 2, c0:c1], self.s[0:nq, h % 2, c0:c1], ACT.Exp, bias=self.nmax[0:nq, h:h + 1],
                                      scale=-1.0, accum_out=self.sum[0:nq, h:h + 1]), ("e", h))
            else:
                p.wait(act, ("t", h), turn)
                a.done(self.take_turned(lambda out, x: act.activation(out, x, ACT.Copy), 1, h, nq, c0, c1), (s, h))
        p.wait(act, "yT", turn)
        act.wait_ge(self.stored, 16 * (turn - 1))
        a.done(act.activation(self.yT[:, :, 0:nq], self.ps_o[:, :].rearrange("p (a t) -> p a t", t=P)[:, :, 0:nq], ACT.Copy), "yT")
        a.wait(act, "yT", turn)
        act.dma_start(self.k.yaT.rearrange("(a p) t -> p a t", p=P)[:, :, out_cols], self.yT[:, :, 0:nq]).then_inc(self.stored, 16)

    def tensor_tile(self, pe, turn, nq, c0, c1):
        v, a, g, p = self.dve_s, self.act_s, self.pool_s, self.pe_s

        def scores(h):
            if h == 0:
                v.wait(pe, "K", turn)
                a.wait(pe, "q", turn)
            v.wait(pe, ("s", h - 2), turn) if h >= 2 else v.wait(pe, ("s", h + NH - 2), turn - 1)
            rows = slice(64 * (h % 2), 64 * (h % 2) + 64)
            for x0, x1 in ((c0, min(c1, 512)), (512, c1)):
                if x1 > x0:
                    mm = pe.matmul(self.ps_s[h % 2][0:nq, x0:x1], self.q[rows, h // 2, 0:nq], self.K[rows, h // 2, x0:x1],
                                   start=True, stop=True)
            p.done(mm, ("s", h))
        scores(0)
        scores(1)
        for h in range(NH):
            a.wait(pe, ("e", h), turn)
            v.wait(pe, ("t", h - 1), turn) if h else v.wait(pe, ("t", NH - 1), turn - 1)
            a.wait(pe, ("t", h - 1), turn) if h else a.wait(pe, ("t", NH - 1), turn - 1)
            for c, n in self.tiles(c0, c1):
                mm = pe.transpose(self.ps_t[0:n, c // (2 * P) if c < 2 * P else 1, (c % (2 * P) if c < 2 * P else c - 2 * P):][:, 0:nq], self.e[0:nq, h % 2, c:c + n], self.k.ident[0:nq, 0:nq])
            p.done(mm, ("t", h))
            if h + 2 < NH:
                scores(h + 2)
            v.wait(pe, ("t", h), turn)
            a.wait(pe, ("t", h), turn)
            if h == 0:
                g.wait(pe, "V", turn)
                v.wait(pe, "Y", turn - 1)
            tl = self.tiles(c0, c1)
            for i, (c, n) in enumerate(tl):
                mm = pe.matmul(self.ps_y[0:nq, h * HD:(h + 1) * HD], self.eT[0:n, h % 2, c:c + nq], self.Vw[0:n, c // P, h * HD:(h + 1) * HD],
                               start=(i == 0), stop=(i == len(tl) - 1))
            p.done(mm, ("y", h))
        v.wait(pe, "Y", turn)
        a.wait(pe, "yT", turn - 1)
        for j in range(NP):
            mm = pe.transpose(self.ps_o[:, j * P:j * P + nq], self.Y[0:nq, j * P:(j + 1) * P], self.k.ident[0:nq, 0:nq])
        p.done(mm, "yT")


def build_attention_core(nc, k, a):
    with ExitStack() as ctx:
        w = Heads(ctx, nc, k, a)
        ck = ctx.enter_context(nc.sbuf_tensor("cache_k_rows", [P, PAST // P, DR], F32))
        cache_loaded = ctx.enter_context(nc.semaphore("cache_loaded"))
        FULL = KT5 - 1

        def each_tile(eng, body):
            for t in range(FULL):
                body(t)
            with eng.Fori(FULL, NQ) as t:
                body(t)

        def first_col(t):
            return (FULL - t) * P if isinstance(t, int) else 0

        def keys(t, c0):
            return ds((t - FULL) * P + c0, BAND - c0)
        with nc.Block() as block:
            @block.vector
            def _(dve):
                w.dve_s.open(dve)
                dve.wait_ge(a.bias_ready, 1)

                def body(t):
                    c0 = first_col(t)
                    w.vector_tile(dve, t + 1, lambda e: w.dve_s.done(e.tensor_copy(w.K[:, :, c0:BAND], a.kT[:, :, keys(t, c0)]), "K"),
                                  P, c0, BAND, lambda h: a.bias[:, h, c0:BAND])
                each_tile(dve, body)

            @block.gpsimd
            def _(pool):
                w.pool_s.open(pool)
                pool.wait_ge(a.rows_ready, 1)

                def body(t):
                    c0 = first_col(t)
                    src = a.V[:, ds(t - FULL + c0 // P, KT5 - c0 // P), :]
                    w.pe_s.wait(pool, ("y", NH - 1), t)
                    w.pool_s.done(pool.tensor_copy(w.Vw[:, c0 // P:KT5, :], src), "V")
                each_tile(pool, body)

            @block.scalar
            def _(act):
                w.act_s.open(act)

                def body(t):
                    w.pe_s.wait(act, ("s", NH - 1), t)
                    w.scalar_tile(act, t + 1, a.qT[:, :, ds(t * P, P)], P, first_col(t), BAND, ds(t * P, P))
                each_tile(act, body)
                act.wait_ge(w.stored, 16 * NQ)

            @block.tensor
            def _(pe):
                w.pe_s.open(pe)
                each_tile(pe, lambda t: w.tensor_tile(pe, t + 1, P, first_col(t), BAND))

        T = NQ + 1
        with nc.Block() as block:
            turned = ctx.enter_context(nc.semaphore("cache_turned"))

            @block.sync
            def _(sp):
                sp.dma_start(ck[:, :, :], k.cache_k.rearrange("(c p) h d -> p c (h d)", p=P)).then_inc(cache_loaded, 16)
                sp.dma_start(w.Vw[:, 0:2, :], k.cache_v.rearrange("(c p) h d -> p c (h d)", p=P)).then_inc(cache_loaded, 16)
                sp.wait_ge(cache_loaded, 32)

            @block.tensor
            def _(pe):
                pe.wait_ge(cache_loaded, 32)
                for c in range(2):
                    for j in range(NP):
                        mm = pe.transpose(w.ps_s[c][:, j * P:(j + 1) * P], ck[:, c, j * P:(j + 1) * P], k.ident[:, :])
                mm.then_inc(turned, 1)
                w.tensor_tile(pe, T, DEC, 0, SKEYS)

            @block.vector
            def _(dve):
                def window(e):
                    e.wait_ge(turned, 1)
                    for c in range(2):
                        e.tensor_copy(w.K[:, :, c * P:(c + 1) * P], w.ps_s[c][:, 0:512].rearrange("p (a t) -> p a t", t=P))
                    w.dve_s.done(e.tensor_copy(w.K[:, :, PAST:SKEYS], a.kT[:, :, SEQ:NT]), "K")
                w.vector_tile(dve, T, window, DEC, 0, SKEYS, lambda h: a.sbias[:, h, :])

            @block.gpsimd
            def _(pool):
                w.pool_s.done(pool.tensor_copy(w.Vw[0:DEC, 2, :], a.V[0:DEC, NQ, :]), "V")

            @block.scalar
            def _(act):
                w.scalar_tile(act, T, a.qT[:, :, SEQ:NT], DEC, 0, SKEYS, slice(SEQ, NT))
                act.wait_ge(w.stored, 16 * T)


def split_products(pe, out, hi, lo, x_hi, x_lo, kts, first=True, last=True):
    n = len(kts)
    for i, kt in enumerate(kts):
        for j, (w, x) in enumerate(((hi, x_hi), (hi, x_lo), (lo, x_hi))):
            mm = pe.matmul(out, w(i), x(kt), start=(first and i == 0 and j == 0), stop=(last and i == n - 1 and j == 2))
    return mm


def build_merge(nc, k):
    with ExitStack() as ctx:
        def sb(name, shape, dt=F32):
            return ctx.enter_context(nc.sbuf_tensor(name, shape, dt))

        def sem(name):
            return ctx.enter_context(nc.semaphore(name))
        wraw = sb("merge_w_raw", [P, 2, D])
        whi, wlo = sb("merge_w_hi", [P, 16, D], F32R), sb("merge_w_lo", [P, 16, D], F32R)
        yraw = sb("y_raw", [P, 2, BW])
        yhi, ylo = sb("y_hi", [P, KD, BW], F32R), sb("y_lo", [P, KD, BW], F32R)
        mhi, mlo = sb("merged_hi", [P, KD, BW], F32R), sb("merged_lo", [P, KD, BW], F32R)
        gate = sb("gates", [P, 2, 2, BW])
        m1, m2 = sb("merged_r", [P, BW]), sb("merged_a", [P, BW])
        xt = sb("x_then_x2", [P, 2, BW])
        pr, pa, po = ([ctx.enter_context(nc.psum_tensor(f"merge_ps{n}{j}", [P, 512], F32)) for j in range(2)] for n in "rao")
        w_loaded = [sem(f"merge_w_loaded{j}") for j in range(2)]
        y_loaded = [sem(f"y_loaded{j}") for j in range(2)]
        g_loaded = [sem(f"gates_loaded{j}") for j in range(2)]
        x_loaded = [sem(f"x_in_loaded{j}") for j in range(2)]
        x2_stored = [sem(f"x2_stored{j}") for j in range(2)]
        whi_s = Steps(ctx, nc, "merge_w_hi_made", list(range(16)))
        wlo_s = Steps(ctx, nc, "merge_w_lo_made", list(range(16)))
        yhi_s = Steps(ctx, nc, "y_hi_made", list(range(8)), base=1)
        ylo_s = Steps(ctx, nc, "y_lo_made", list(range(8)), base=1)
        act_s = Steps(ctx, nc, "merge_act", [(s, m) for m in range(8) for s in ("g", "mh")])
        dve_s = Steps(ctx, nc, "merge_dve", [(s, m) for m in range(8) for s in ("m1", "m2", "ms", "ml")] + [("x", m) for m in range(8)])
        pe_s = Steps(ctx, nc, "merge_pe", [(s, m) for m in range(8) for s in ("r", "a")] + [("o", m) for m in range(8)])
        proj = k.proj.rearrange("(r p) t -> p r t", p=P)
        y_src = [k.yrT.rearrange("(a p) t -> p a t", p=P), k.yaT.rearrange("(a p) t -> p a t", p=P)]
        w_src = [w.rearrange("(a p) n -> p a n", p=P) for w in (k.w_br_r, k.w_br_a, k.w_out)]
        xT, x2T = (t.rearrange("(a p) t -> p a t", p=P) for t in (k.xT, k.x2T))

        def cols(b):
            return ds(b * BW, BW)

        def each_block(eng, body):
            body(0, 1, False)
            with eng.Fori(1, NB - 1) as b:
                body(b, b + 1, False)
            body(NB - 1, NB, True)

        def nth(turn, m):
            return 64 * (turn - 1) + 16 * (m // 2 + 1)

        with nc.Block() as block:
            @block.sync
            def _(sp):
                def load_y(b, turn, kt):
                    if isinstance(turn, int) and turn == 1 and kt < 2:
                        pass
                    else:
                        yt, yk = (turn, kt - 2) if kt >= 2 else (turn - 1, kt + 6)
                        ylo_s.wait(sp, yk, yt)
                    sp.dma_start(yraw[:, kt % 2, :], y_src[kt // 4][:, kt % 4, ds((b + 1) * BW - BW, BW)]).then_inc(y_loaded[kt % 2], 16)

                def load_w(n):
                    if n >= 2:
                        wlo_s.wait(sp, n - 2, 0)
                    src = w_src[0][:, n, :] if n < 4 else w_src[1][:, n - 4, :] if n < 8 else w_src[2][:, n - 8, :]
                    sp.dma_start(wraw[:, n % 2, :], src).then_inc(w_loaded[n % 2], 16)
                for n in range(8):
                    load_y(0, 1, n)
                    load_w(n)

                def body(b, turn, last):
                    for m in range(8):
                        dve_s.wait(sp, ("m2", m - 2), turn) if m >= 2 else dve_s.wait(sp, ("m2", m + 6), turn - 1)
                        for half in range(2):
                            ins = sp.dma_start(gate[:, m % 2, half, :], proj[:, GT + 8 * half + m, cols(b)])
                            ins.then_inc(g_loaded[m % 2], 16)
                        if isinstance(turn, int) and turn == 1:
                            load_w(8 + m)
                    for m in range(8):
                        sp.wait_ge(x2_stored[m % 2], nth(turn, m) - 16)
                        sp.dma_start(xt[:, m % 2, :], xT[:, m, ds(turn * BW - BW, BW)]).then_inc(x_loaded[m % 2], 16)
                        if not last:
                            if m == 0:
                                pe_s.wait(sp, ("a", 7), turn)
                            load_y(b + 1, turn + 1, m)

                each_block(sp, body)

            def y_split_hi(act, turn, kt):
                act.wait_ge(y_loaded[kt % 2], nth(turn, kt))
                yhi_s.done(act.activation(yhi[:, kt, :], yraw[:, kt % 2, :], ACT.Copy), kt)

            def w_hi(act, n):
                act.wait_ge(w_loaded[n % 2], 16 * (n // 2 + 1))
                whi_s.done(act.activation(whi[:, n, :], wraw[:, n % 2, :], ACT.Copy), n)

            @block.scalar
            def _(act):
                act_s.open(act)
                for n in range(8):
                    y_split_hi(act, 1, n)
                    w_hi(act, n)

                def body(b, turn, last):
                    for m in range(8):
                        act.wait_ge(g_loaded[m % 2], 2 * nth(turn, m))
                        act_s.done(act.activation(gate[:, m % 2], gate[:, m % 2], ACT.Tanh, scale=0.5), ("g", m))
                        if isinstance(turn, int) and turn == 1:
                            w_hi(act, 8 + m)
                        dve_s.wait(act, ("ms", m), turn)
                        pe_s.wait(act, ("o", 7), turn - 1)
                        act_s.done(act.activation(mhi[:, m, :], m1[:, :], ACT.Copy, scale=0.5), ("mh", m))
                    for m in range(8):
                        if not last:
                            if m == 0:
                                pe_s.wait(act, ("a", 7), turn)
                            y_split_hi(act, turn + 1, m)
                        dve_s.wait(act, ("x", m), turn)
                        act.dma_start(x2T[:, m, cols(b)], xt[:, m % 2, :]).then_inc(x2_stored[m % 2], 16)
                each_block(act, body)
                for j in range(2):
                    act.wait_ge(x2_stored[j], 64 * NB)

            def y_split_lo(dve, turn, kt):
                yhi_s.wait(dve, kt, turn)
                ylo_s.done(dve.tensor_tensor(ylo[:, kt, :], yraw[:, kt % 2, :], yhi[:, kt, :].bitcast(F32), ALU.subtract), kt)

            def w_lo(dve, n):
                whi_s.wait(dve, n, 0)
                wlo_s.done(dve.tensor_tensor(wlo[:, n, :], wraw[:, n % 2, :], whi[:, n, :].bitcast(F32), ALU.subtract), n)

            @block.vector
            def _(dve):
                dve_s.open(dve)
                for n in range(8):
                    y_split_lo(dve, 1, n)
                    w_lo(dve, n)

                def body(b, turn, last):
                    for m in range(8):
                        if isinstance(turn, int) and turn == 1:
                            w_lo(dve, 8 + m)
                        act_s.wait(dve, ("g", m), turn)
                        pe_s.wait(dve, ("r", m), turn)
                        dve_s.wait(dve, ("ml", m - 1), turn) if m else dve_s.wait(dve, ("ml", 7), turn - 1)
                        for name, out, ps, half in (("m1", m1, pr, 0), ("m2", m2, pa, 1)):
                            pe_s.wait(dve, ("ra"[half], m), turn)
                            dve_s.done(dve.scalar_tensor_tensor(out=out[:, :], in0=gate[:, m % 2, half, :], scalar=1.0, in1=ps[m % 2][:, 0:BW],
                                                                op0=ALU.add, op1=ALU.mult), (name, m))
                        dve_s.wait(dve, ("m2", m), turn)
                        dve_s.done(dve.tensor_tensor(m1[:, :], m1[:, :], m2[:, :], ALU.add), ("ms", m))
                        act_s.wait(dve, ("mh", m), turn)
                        dve_s.done(dve.scalar_tensor_tensor(out=mlo[:, m, :], in0=m1[:, :], scalar=0.5, in1=mhi[:, m, :].bitcast(F32),
                                                            op0=ALU.mult, op1=ALU.subtract), ("ml", m))
                    for m in range(8):
                        pe_s.wait(dve, ("o", m), turn)
                        dve.wait_ge(x_loaded[m % 2], nth(turn, m))
                        for c0, c1, g in pieces(last):
                            ins = dve.scalar_tensor_tensor(out=xt[:, m % 2, c0:c1], in0=po[m % 2][:, c0:c1], scalar=k.mod[:, 16 + m, g:g + 1],
                                                           in1=xt[:, m % 2, c0:c1], op0=ALU.mult, op1=ALU.add)
                        dve_s.done(ins, ("x", m))
                        if not last:
                            y_split_lo(dve, turn + 1, m)
                each_block(dve, body)

            @block.tensor
            def _(pe):
                pe_s.open(pe)

                def body(b, turn, last):
                    for m in range(8):
                        w = slice(m * P, (m + 1) * P)
                        for name, ps, k0 in (("r", pr, 0), ("a", pa, 4)):
                            if m == 0:
                                for kt in range(k0, k0 + 4):
                                    ylo_s.wait(pe, kt, turn)
                                    if isinstance(turn, int) and turn == 1:
                                        wlo_s.wait(pe, kt, 0)
                            step = "m1" if name == "r" else "m2"
                            dve_s.wait(pe, (step, m - 2), turn) if m >= 2 else dve_s.wait(pe, (step, m + 6), turn - 1)
                            mm = split_products(pe, ps[m % 2][:, 0:BW], lambda i: whi[:, k0 + i, w], lambda i: wlo[:, k0 + i, w],
                                                lambda kt: yhi[:, kt, :], lambda kt: ylo[:, kt, :], range(k0, k0 + 4))
                            pe_s.done(mm, (name, m))
                    for m in range(8):
                        w = slice(m * P, (m + 1) * P)
                        dve_s.wait(pe, ("ml", 7), turn)
                        if isinstance(turn, int) and turn == 1:
                            wlo_s.wait(pe, 15, 0)
                        dve_s.wait(pe, ("x", m - 2), turn) if m >= 2 else dve_s.wait(pe, ("x", m + 6), turn - 1)
                        mm = split_products(pe, po[m % 2][:, 0:BW], lambda i: whi[:, 8 + i, w], lambda i: wlo[:, 8 + i, w],
                                            lambda kt: mhi[:, kt, :], lambda kt: mlo[:, kt, :], range(8))
                        pe_s.done(mm, ("o", m))
                each_block(pe, body)


UNITS = 2 * FF_T
SUBS = [(0, P), (P, P), (2 * P, P), (SPLIT_AT, DEC)]


class Mlp:

    def __init__(self, ctx, nc, k):
        self.k = k

        def sb(name, shape, dt=F32):
            return ctx.enter_context(nc.sbuf_tensor(name, shape, dt))

        def sem(name):
            return ctx.enter_context(nc.semaphore(name))
        self.raw = sb("ff_raw", [P, 4, KD, P])
        self.whi, self.wlo = sb("ff_hi", [P, 2, KD, P], F32R), sb("ff_lo", [P, 2, KD, P], F32R)
        self.hhi, self.hlo = sb("h2_hi", [P, KD, BW], F32R), sb("h2_lo", [P, KD, BW], F32R)
        self.uhi, self.ulo = sb("hidden_hi", [P, FF_T, BW], F32R), sb("hidden_lo", [P, FF_T, BW], F32R)
        self.r = sb("hidden", [P, 2, BW])
        self.xa, self.xn = sb("x_now", [P, KD, BW]), sb("x_next", [P, KD, BW])
        self.sq = sb("squares2", [P, 2, BW])
        self.nrm = sb("norms", [P, BW])
        self.h = sb("h2", [P, BW])
        self.yo = sb("y_rows", [P, D])
        self.cur = sb("tail_now", [P, 2, 24])
        self.ones = sb("ones", [P, P])
        self.ps = [ctx.enter_context(nc.psum_tensor(f"ff_ps{j}", [P, 512], F32)) for j in range(2)]
        self.pn = [ctx.enter_context(nc.psum_tensor(f"norm_ps{j}", [P, 512], F32)) for j in range(2)]
        self.pt = [ctx.enter_context(nc.psum_tensor(f"rows_ps{j}", [P, D], F32)) for j in range(2)]
        self.w_loaded = [sem(f"ff_loaded{j}") for j in range(4)]
        self.x_loaded = sem("x2_loaded")
        self.y_stored = sem("y_stored")
        u = list(range(UNITS))
        self.hi_s, self.lo_s = Steps(ctx, nc, "ff_hi_made", u), Steps(ctx, nc, "ff_lo_made", u)
        self.mm_s = Steps(ctx, nc, "ff_products", u)
        self.relu_s, self.uhi_s = Steps(ctx, nc, "relu", range(FF_T)), Steps(ctx, nc, "hidden_hi_made", range(FF_T))
        self.sq_s, self.ulo_s = Steps(ctx, nc, "hidden_squared", range(FF_T)), Steps(ctx, nc, "hidden_lo_made", range(FF_T))
        self.x_s = Steps(ctx, nc, "x3", ["moved"] + list(range(KD)))
        ks = list(range(KD))
        self.n_sq, self.f_sq = Steps(ctx, nc, "next_squares", ks), Steps(ctx, nc, "final_squares", ks)
        self.n_pe, self.f_pe = Steps(ctx, nc, "next_sums", ks), Steps(ctx, nc, "final_sums", ks + ["t0", "t1", "t2", "t3"])
        self.n_rms, self.f_rms = Steps(ctx, nc, "next_rms", ["rms"], base=1), Steps(ctx, nc, "final_rms", ["rms"], base=1)
        self.n_dve = Steps(ctx, nc, "next_norm", ["vec", "rstd"] + [(s, j) for j in ks for s in ("n", "lo")], base=1)
        self.n_act = Steps(ctx, nc, "next_affine", [(s, j) for j in ks for s in ("h", "hi")], base=1)
        self.f_dve = Steps(ctx, nc, "final_norm", ["rstd"] + ks)
        self.f_act = Steps(ctx, nc, "final_rows", ["t0", "t1", "t2", "t3"])

    def strip(self, s):
        k = self.k
        if s < FF_T:
            return k.w_ff1.rearrange("(k p) n -> p k n", p=P)[:, :, s * P:(s + 1) * P]
        m, q = (s - FF_T) // 4, (s - FF_T) % 4
        return k.w_ff2[q * D:(q + 1) * D, m * P:(m + 1) * P].rearrange("(k p) n -> p k n", p=P)

    def next_at(self, u):
        v = u - FF_T
        if 3 <= v < 3 + KD:
            yield "sq", v - 3
        if v == 12:
            yield "mean", 0
        if 14 <= v < 14 + 2 * KD and v % 2 == 0:
            yield "h", (v - 14) // 2

    def final_at(self, u):
        if 1 <= u < 1 + KD:
            yield "sq", u - 1
        if u == 10:
            yield "mean", 0
        if 12 <= u < 12 + KD:
            yield "y", u - 12
        if u in (21, 23, 25, 27):
            yield "t", (u - 21) // 2


def build_mlp(nc, k):
    with ExitStack() as ctx:
        w = Mlp(ctx, nc, k)
        ones_made = ctx.enter_context(nc.semaphore("ones_made"))
        x2T = k.x2T.rearrange("(a p) t -> p a t", p=P)
        GF = VROW["final_norm_g"]
        PIECES = ((0, SPLIT_AT, 0), (SPLIT_AT, BW, 1))

        def next_sync(sp, b, turn):
            w.x_s.wait(sp, "moved", turn - 1)
            sp.dma_start(w.xn[:, :, :], x2T[:, :, ds(b * BW, BW)]).then_inc(w.x_loaded, 16)

        def next_act(act, part, j, turn):
            if part == "sq":
                act.wait_ge(w.x_loaded, 16 * turn)
                if j >= 2:
                    w.n_pe.wait(act, j - 2, turn)
                w.n_sq.done(act.activation(w.sq[:, j % 2, :], w.xn[:, j, :], ACT.Square), j)
            if part == "mean":
                w.n_pe.wait(act, KD - 1, turn)
                if not isinstance(turn, int) or turn > 1:
                    w.f_dve.wait(act, KD - 1, turn - 2)
                w.n_rms.done(act.activation(w.nrm[:, :], w.pn[0][:, 0:BW], ACT.Sqrt, scale=1.0 / D, bias=k.eps[:, 0:1]), "rms")
            if part == "h":
                w.n_dve.wait(act, ("n", j), turn)
                for c0, c1, tail in PIECES:
                    scale = w.cur[:, 0, j:j + 1] if tail else k.gain2[:, j, 0:1]
                    shift = w.cur[:, 0, 8 + j:9 + j] if tail else k.mod[:, 24 + j, 0:1]
                    ins = act.activation(w.h[:, c0:c1], w.h[:, c0:c1], ACT.Identity, scale=scale, bias=shift)
                w.n_act.done(ins, ("h", j))
                w.n_act.wait(act, ("h", j), turn)
                w.n_act.done(act.activation(w.hhi[:, j, :], w.h[:, :], ACT.Copy), ("hi", j))

        def next_dve(dve, part, j, turn, b):
            if part == "mean":
                w.n_dve.done(dve.tensor_copy(w.cur[:, 0, :].unsqueeze(1), k.tail[:, ds(b, 1), :]), "vec")
                w.n_rms.wait(dve, "rms", turn)
                w.n_dve.done(dve.reciprocal(w.nrm[:, :], w.nrm[:, :]), "rstd")
            if part == "h":
                w.n_dve.wait(dve, "rstd", turn)
                if j:
                    w.n_dve.wait(dve, ("lo", j - 1), turn)
                w.n_dve.done(dve.tensor_tensor(w.h[:, :], w.xn[:, j, :], w.nrm[:, :], ALU.mult), ("n", j))
                w.n_act.wait(dve, ("hi", j), turn)
                w.n_dve.done(dve.tensor_tensor(w.hlo[:, j, :], w.h[:, :], w.hhi[:, j, :].bitcast(F32), ALU.subtract), ("lo", j))

        def next_pe(pe, part, j, turn):
            if part == "sq":
                w.n_sq.wait(pe, j, turn)
                w.n_pe.done(pe.matmul(w.pn[0][:, 0:BW], w.ones[:, :], w.sq[:, j % 2, :], start=(j == 0), stop=(j == KD - 1)), j)

        def final_act(act, part, j, turn, rows):
            if part == "sq":
                w.x_s.wait(act, KD - 1, turn)
                if j >= 2:
                    w.f_pe.wait(act, j - 2, turn)
                w.f_sq.done(act.activation(w.sq[:, j % 2, :], w.xa[:, j, :], ACT.Square), j)
            if part == "mean":
                w.f_pe.wait(act, KD - 1, turn)
                w.n_dve.wait(act, ("lo", KD - 1), min(turn + 1, NB) if isinstance(turn, int) else turn + 1)
                w.f_rms.done(act.activation(w.nrm[:, :], w.pn[1][:, 0:BW], ACT.Sqrt, scale=1.0 / D, bias=k.eps[:, 0:1]), "rms")
            if part == "t":
                c0, n = SUBS[j]
                w.f_pe.wait(act, f"t{j}", turn)
                act.wait_ge(w.y_stored, 64 * (turn - 1) + 16 * j)
                w.f_act.done(act.activation(w.yo[0:n, :], w.pt[j % 2][0:n, :], ACT.Copy), f"t{j}")
                w.f_act.wait(act, f"t{j}", turn)
                act.dma_start(rows(c0, n), w.yo[0:n, :]).then_inc(w.y_stored, 16)

        def final_dve(dve, part, j, turn, b_now):
            if part == "mean":
                w.f_rms.wait(dve, "rms", turn)
                w.f_dve.done(dve.reciprocal(w.nrm[:, :], w.nrm[:, :]), "rstd")
            if part == "y":
                w.f_dve.wait(dve, "rstd", turn)
                w.f_dve.done(dve.scalar_tensor_tensor(out=w.xa[:, j, :], in0=w.xa[:, j, :], scalar=k.vec[:, GF + j:GF + j + 1],
                                                      in1=w.nrm[:, :], op0=ALU.mult, op1=ALU.mult), j)

        def final_pe(pe, part, j, turn):
            if part == "sq":
                w.f_sq.wait(pe, j, turn)
                w.f_pe.done(pe.matmul(w.pn[1][:, 0:BW], w.ones[:, :], w.sq[:, j % 2, :], start=(j == 0), stop=(j == KD - 1)), j)
            if part == "t":
                c0, n = SUBS[j]
                w.f_dve.wait(pe, KD - 1, turn)
                w.f_act.wait(pe, f"t{j - 2}", turn) if j >= 2 else w.f_act.wait(pe, f"t{j + 2}", turn - 1)
                for i in range(KD):
                    mm = pe.transpose(w.pt[j % 2][0:n, i * P:(i + 1) * P], w.xa[:, i, c0:c0 + n], k.ident[:, :])
                w.f_pe.done(mm, f"t{j}")

        def rows_of(b):
            def rows(c0, n):
                if isinstance(b, int) and b == NB - 1 and c0 == SPLIT_AT:
                    return k.y_sample
                return k.y_prompt[ds(b * BW + c0, n), :]
            return rows

        def make_hi(act, s, turn):
            act.wait_ge(w.w_loaded[s % 4], 16 * (UNITS // 4) * (turn - 1) + 16 * (s // 4 + 1))
            w.mm_s.wait(act, s - 2, turn) if s >= 2 else w.mm_s.wait(act, UNITS + s - 2, turn - 1)
            w.hi_s.done(act.activation(w.whi[:, s % 2], w.raw[:, s % 4], ACT.Copy), s)

        def make_lo(dve, s, turn):
            w.hi_s.wait(dve, s, turn)
            w.lo_s.done(dve.tensor_tensor(w.wlo[:, s % 2], w.raw[:, s % 4], w.whi[:, s % 2].bitcast(F32), ALU.subtract), s)

        def each_block(eng, body):
            body(0, 1, False, True)
            with eng.Fori(1, NB - 1) as b:
                body(b, b + 1, True, True)
            body(NB - 1, NB, True, False)

        FIRST = [x for u in range(UNITS) for x in w.next_at(u)]
        LAST = [x for u in range(UNITS) for x in w.final_at(u)]
        with nc.Block() as block:
            @block.sync
            def _(sp):
                def body(b, turn, before, after):
                    for s in range(UNITS):
                        w.lo_s.wait(sp, s - 4, turn) if s >= 4 else w.lo_s.wait(sp, UNITS + s - 4, turn - 1)
                        sp.dma_start(w.raw[:, s % 4], w.strip(s)).then_inc(w.w_loaded[s % 4], 16)
                        if s == FF_T and after:
                            next_sync(sp, b + 1, turn + 1)
                next_sync(sp, 0, 1)
                each_block(sp, body)

            @block.scalar
            def _(act):
                for s in (w.hi_s, w.relu_s, w.uhi_s, w.n_sq, w.f_sq, w.f_act):
                    s.open(act)

                def body(b, turn, before, after):
                    for u in range(UNITS):
                        if u + 1 < UNITS:
                            make_hi(act, u + 1, turn)
                        elif after:
                            make_hi(act, 0, turn + 1)
                        if u < FF_T:
                            w.mm_s.wait(act, u, turn)
                            w.sq_s.wait(act, u - 2, turn) if u >= 2 else w.sq_s.wait(act, FF_T + u - 2, turn - 1)
                            w.ulo_s.wait(act, u - 2, turn) if u >= 2 else w.ulo_s.wait(act, FF_T + u - 2, turn - 1)
                            w.relu_s.done(act.activation(w.r[:, u % 2, :], w.ps[u % 2][:, 0:BW], ACT.Relu), u)
                        if 1 <= u <= FF_T:
                            w.sq_s.wait(act, u - 1, turn)
                            if u == 1:
                                w.mm_s.wait(act, UNITS - 1, turn - 1)
                            w.uhi_s.done(act.activation(w.uhi[:, u - 1, :], w.r[:, (u - 1) % 2, :], ACT.Copy), u - 1)
                        if before:
                            for part, j in w.final_at(u):
                                final_act(act, part, j, turn - 1, rows_of(b - 1))
                        if after:
                            for part, j in w.next_at(u):
                                next_act(act, part, j, turn + 1)
                for part, j in FIRST:
                    next_act(act, part, j, 1)
                make_hi(act, 0, 1)
                each_block(act, body)
                for part, j in LAST:
                    final_act(act, part, j, NB, rows_of(NB - 1))
                act.wait_ge(w.y_stored, 64 * NB)

            @block.vector
            def _(dve):
                for s in (w.lo_s, w.sq_s, w.ulo_s, w.x_s, w.f_dve):
                    s.open(dve)
                dve.memset(w.ones[:, :], 1.0).then_inc(ones_made, 1)

                def move(turn, b):
                    w.f_pe.wait(dve, "t3", turn - 1)
                    dve.tensor_copy(w.cur[:, 1, :].unsqueeze(1), k.tail[:, ds(b, 1), :])
                    w.x_s.done(dve.tensor_copy(w.xa[:, :, :], w.xn[:, :, :]), "moved")

                def body(b, turn, before, after):
                    for u in range(UNITS):
                        if u + 1 < UNITS:
                            make_lo(dve, u + 1, turn)
                        elif after:
                            make_lo(dve, 0, turn + 1)
                        if u < FF_T:
                            w.relu_s.wait(dve, u, turn)
                            w.sq_s.done(dve.tensor_tensor(w.r[:, u % 2, :], w.r[:, u % 2, :], w.r[:, u % 2, :], ALU.mult), u)
                        if 1 <= u <= FF_T:
                            w.uhi_s.wait(dve, u - 1, turn)
                            w.ulo_s.done(dve.tensor_tensor(w.ulo[:, u - 1, :], w.r[:, (u - 1) % 2, :], w.uhi[:, u - 1, :].bitcast(F32), ALU.subtract), u - 1)
                        if u >= FF_T and u % 4 == 3:
                            m = (u - FF_T) // 4
                            w.mm_s.wait(dve, u, turn)
                            for c0, c1, tail in PIECES:
                                g = w.cur[:, 1, 16 + m:17 + m] if tail else k.mod[:, 40 + m, 0:1]
                                ins = dve.scalar_tensor_tensor(out=w.xa[:, m, c0:c1], in0=w.ps[m % 2][:, c0:c1], scalar=g, in1=w.xa[:, m, c0:c1],
                                                               op0=ALU.mult, op1=ALU.add)
                            w.x_s.done(ins, m)
                        if before:
                            for part, j in w.final_at(u):
                                final_dve(dve, part, j, turn - 1, b)
                        if u == 29:
                            move(turn, b)
                        if u == FF_T:
                            w.x_s.wait(dve, "moved", turn)
                        if after:
                            for part, j in w.next_at(u):
                                next_dve(dve, part, j, turn + 1, b + 1)
                for part, j in FIRST:
                    next_dve(dve, part, j, 1, 0)
                make_lo(dve, 0, 1)
                each_block(dve, body)
                for part, j in LAST:
                    final_dve(dve, part, j, NB, NB)

            @block.tensor
            def _(pe):
                for s in (w.mm_s, w.n_pe, w.f_pe):
                    s.open(pe)
                pe.wait_ge(ones_made, 1)

                def body(b, turn, before, after):
                    for u in range(UNITS):
                        w.lo_s.wait(pe, u, turn)
                        ops = (lambda i: w.whi[:, u % 2, i, :], lambda i: w.wlo[:, u % 2, i, :])
                        if u < FF_T:
                            if u == 0:
                                w.n_dve.wait(pe, ("lo", KD - 1), turn)
                            if u >= 2:
                                w.relu_s.wait(pe, u - 2, turn)
                            else:
                                w.x_s.wait(pe, 6 + u, turn - 1)
                            mm = split_products(pe, w.ps[u % 2][:, 0:BW], *ops, lambda kt: w.hhi[:, kt, :], lambda kt: w.hlo[:, kt, :], range(KD))
                        else:
                            m, q = (u - FF_T) // 4, u % 4
                            if q == 0:
                                if m < 2:
                                    w.relu_s.wait(pe, FF_T - 2 + m, turn)
                                else:
                                    w.x_s.wait(pe, m - 2, turn)
                            if m == 0:
                                w.ulo_s.wait(pe, 8 * q + 7, turn)
                            mm = split_products(pe, w.ps[m % 2][:, 0:BW], *ops, lambda kt: w.uhi[:, kt, :], lambda kt: w.ulo[:, kt, :],
                                                range(8 * q, 8 * q + 8), first=(q == 0), last=(q == 3))
                        w.mm_s.done(mm, u)
                        if before:
                            for part, j in w.final_at(u):
                                final_pe(pe, part, j, turn - 1)
                        if after:
                            for part, j in w.next_at(u):
                                next_pe(pe, part, j, turn + 1)
                for part, j in FIRST:
                    next_pe(pe, part, j, 1)
                each_block(pe, body)
                for part, j in LAST:
                    final_pe(pe, part, j, NB)


def declare(nc, arrays):
    k = Tensors()
    ap = {n: nc.dram_tensor(f"in_{n}", a.shape, F32, kind="ExternalInput").ap() for n, a in arrays.items()}
    k.vec_in = {n: ap[n][0] if n != "final_norm_g" and n != "r_k" else ap[n] for n, _ in VECS}
    k.vec_in["r_k"] = ap["r_k"].rearrange("a h d -> (a h d)")
    k.vec_in["c_prompt"], k.vec_in["c_sample"] = ap["c_prompt"][0], ap["c_sample"][0]
    k.vec_in["shift"] = ap["state_rwkv_shift"][0, 0]
    k.x_prompt, k.x_sample = ap["x_prompt"][0], ap["x_sample"][0]
    k.s_in = ap["state_rwkv_wkv"][0, 0]
    k.cache_k, k.cache_v = ap["cache_att_k"][0, 0], ap["cache_att_v"][0, 0]
    k.w_ada, k.w_in, k.w_lora_up, k.a_lora_up, k.g_lora_up = (ap[n][0] for n in ("w_ada", "w_in", "w_lora_up", "a_lora_up", "g_lora_up"))
    k.w_br_r, k.w_br_a, k.w_out, k.w_ff1, k.w_ff2 = (ap[n][0] for n in ("w_br_r", "w_br_a", "w_out", "w_ff1", "w_ff2"))
    k.rel_table = ap["rel_table"][0]
    outs = [nc.dram_tensor(f"out_{i}", s, F32, kind="ExternalOutput").ap() for i, s in enumerate(OUT_SHAPES)]
    k.y_prompt, k.y_sample = outs[0][0], outs[1][0]
    k.p_wkv, k.p_shift, k.p_k, k.p_v = outs[2][0, 0], outs[3][0, 0], outs[4][0, 0], outs[5][0, 0]
    k.s_wkv, k.s_shift, k.s_k, k.s_v = outs[6][0, 0], outs[7][0, 0], outs[8][0, 0], outs[9][0, 0]

    def keep(name, rows, cols):
        return nc.dram_tensor(f"keep_{name}", (rows, cols), F32, kind="Internal").ap()
    k.xT, k.proj, k.yrT, k.yaT, k.x2T = keep("xT", D, NT), keep("proj", IN_T * P, NT), keep("yrT", DR, NT), keep("yaT", DR, NT), keep("x2T", D, NT)
    k.ext = keep("ext", NH, EXT)
    return k


OUT_SHAPES = [(1, SEQ, D), (1, DEC, D), (1, 1, NH, HD, HD), (1, 1, R_PROJ), (1, 1, WIN, NH, HD), (1, 1, WIN, NH, HD),
              (1, 1, NH, HD, HD), (1, 1, R_PROJ), (1, 1, DEC, NH, HD), (1, 1, DEC, NH, HD)]


def build(nc, k):
    with ExitStack() as ctx:
        def sb(name, shape, dt=F32):
            return ctx.enter_context(nc.sbuf_tensor(name, shape, dt))
        k.ident, k.half_power, k.one, k.eps, k.vec = sb("identity", [P, P]), sb("minus_half", [P, 1]), sb("one", [P, 1]), sb("epsilon", [P, 1]), sb("channel_vectors", [P, NVEC])
        k.mod, k.gain1, k.gain2 = sb("modulation", [P, 48, 2]), sb("gain_mix", [P, 8, 2]), sb("gain_mlp", [P, 8, 2])
        k.tail = sb("tail_modulation", [P, NB, 24])
        with ExitStack() as early:
            def eb(name, shape, dt=F32):
                return early.enter_context(nc.sbuf_tensor(name, shape, dt))
            k.pair, k.ii = eb("pair_ones", [P, P]), eb("two_identities", [P, 64])
            k.m_lt, k.m_le, k.m_lt8, k.m_gt8, k.m_gto = (eb(n, [P, P]) for n in ("mask_lt", "mask_le", "mask_lt8", "mask_gt8", "mask_gt_outer"))
            k.restart = eb("scan_restart", [P, NP * C])
            k.wa_up, k.g_up = eb("w_a_up", [P, DR]), eb("g_up", [P, DR])
            k.cvec, k.one_minus_ka = eb("c_vectors", [P, NCROW]), eb("one_minus_ka", [P, 4])
            build_constants(nc, k)
            build_modulation(nc, k)
            k.h_hi, k.h_lo = eb("h_hi", [P, KD, NT], F32R), eb("h_lo", [P, KD, NT], F32R)
            build_first_norm(nc, k)
            with ExitStack() as pctx:
                pj = Projection(pctx, nc, k)
                build_projection_rwkv(nc, k, pj)
                build_rwkv(nc, k, pj)
        build_attention(nc, k)
        build_merge(nc, k)
        build_mlp(nc, k)


NAMES = ["x_prompt", "x_sample", "c_prompt", "c_sample", "state_rwkv_wkv", "state_rwkv_shift", "cache_att_k",
         "cache_att_v", "w_ada", "b_ada", "norm_mix_g", "w_in", "mu_shift", "w_lora_up", "w0", "a_lora_up", "a0",
         "g_lora_up", "k_k", "k_a", "r_k", "lnx_g", "lnx_b", "rel_table", "w_br_r", "w_br_a", "w_out", "norm_mlp_g",
         "w_ff1", "w_ff2", "final_norm_g"]


def kernel(**inputs):
    import numpy as np
    import concourse.bacc as bacc
    from concourse.bass_utils import run_bass_kernel_spmd

    nc = bacc.Bacc("TRN2", target_bir_lowering=False, num_devices=1)
    arrays = {n: np.ascontiguousarray(inputs[n]) for n in NAMES}
    build(nc, declare(nc, arrays))
    r = run_bass_kernel_spmd(nc, [{f"in_{n}": a for n, a in arrays.items()}], core_ids=[0])
    return tuple(r.results[0][f"out_{i}"] for i in range(len(OUT_SHAPES)))
```

```python
from contextlib import ExitStack

import concourse.bass as bass
from concourse import mybir

F32 = mybir.dt.float32
F32R = mybir.dt.float32r
ALU = mybir.AluOpType
ACT = mybir.ActivationFunctionType
AX = mybir.AxisListType
ds = bass.ds

P = 128
D = 1024
KD = D // P
SEQ, DEC = 2048, 32
NT = SEQ + DEC
NB, BW = 5, 416
SPLIT_AT = SEQ - (NB - 1) * BW
HD, NH, NP = 64, 8, 4
DR = NH * HD
R_PROJ = 1792
RT = R_PROJ // P
IN_T = 5376 // P
QT, KT_, VT, GT = RT, RT + 4, RT + 8, RT + 12
C = 64
NCH = SEQ // C
FF_T = 32
PAST = 256
WIN = 512
BAND = WIN + P
REL = 128
EXT = BAND + P - 1
NEG = -1.0e30
KAPPA = 0.6065306597126334
GN_EPS = 64e-5
EPS = 1e-6

VECS = [("b_ada", 48), ("norm_mix_g", 8), ("norm_mlp_g", 8), ("final_norm_g", 8), ("mu_shift", 14), ("w0", 4),
        ("a0", 4), ("k_k", 4), ("k_a", 4), ("r_k", 4), ("lnx_g", 4), ("lnx_b", 4)]
VROW = {}
NVEC = 0
for _name, _n in VECS:
    VROW[_name] = NVEC
    NVEC += _n
CROWS = {"c_prompt": 0, "c_sample": KD, "shift": 2 * KD}
NCROW = 2 * KD + RT


class Tensors:
    pass


class Steps:

    def __init__(self, ctx, nc, name, steps, base=0):
        self.sem = ctx.enter_context(nc.semaphore(name))
        self.place = {s: i + 1 for i, s in enumerate(steps)}
        assert len(self.place) == len(steps)
        self.per = len(steps)
        self.base = base
        self.last = 0

    def done(self, ins, step):
        at = self.place[step]
        assert at == self.last % self.per + 1, (step, at, self.last)
        self.last += 1
        ins.then_inc(self.sem, 1)

    def wait(self, eng, step, turn):
        eng.wait_ge(self.sem, (turn - self.base) * self.per + self.place[step])

    def open(self, eng):
        eng.sem_inc(self.sem, self.per)


def bc(ap, n):
    return ap.unsqueeze(2).broadcast_to([ap.shape[0], ap.shape[1], n])


def bcm(ap, m):
    return ap.unsqueeze(1).broadcast_to([ap.shape[0], m, ap.shape[1]])


def pieces(last):
    return [(0, SPLIT_AT, 0), (SPLIT_AT, BW, 1)] if last else [(0, BW, 0)]


def build_constants(nc, k):
    with ExitStack() as ctx:
        rows = ctx.enter_context(nc.sbuf_tensor("vec_rows", [NVEC, P], F32))
        crows = ctx.enter_context(nc.sbuf_tensor("c_rows", [NCROW, P], F32))
        ps = ctx.enter_context(nc.psum_tensor("vec_ps", [P, 512], F32))
        loaded = ctx.enter_context(nc.semaphore("vec_loaded"))
        made = ctx.enter_context(nc.semaphore("masks_made"))
        turned = ctx.enter_context(nc.semaphore("vecs_turned"))
        kept = ctx.enter_context(nc.semaphore("vecs_kept"))
        k.made_total = 0
        with nc.Block() as block:
            @block.sync
            def _(sp):
                for name, n in VECS:
                    r = VROW[name]
                    sp.dma_start(rows[r:r + n, :], k.vec_in[name].rearrange("(r p) -> r p", p=P)).then_inc(loaded, 16)
                for name, r in CROWS.items():
                    n = RT if name == "shift" else KD
                    sp.dma_start(crows[r:r + n, :], k.vec_in[name].rearrange("(r p) -> r p", p=P)).then_inc(loaded, 16)
                sp.dma_start(k.wa_up[0:64, :], k.w_lora_up).then_inc(loaded, 16)
                sp.dma_start(k.wa_up[64:128, :], k.a_lora_up).then_inc(loaded, 16)
                sp.dma_start(k.g_up[:, :], k.g_lora_up).then_inc(loaded, 16)

            @block.gpsimd
            def _(pool):
                n = [0]

                def step(ins):
                    n[0] += 1
                    ins.then_inc(made, 1)
                    pool.wait_ge(made, n[0])

                def select(out, pattern, base, cm, op, fill):
                    step(pool.affine_select(out=out, in_=out, compare_op=op, fill=fill, base=base,
                                            pattern=pattern, channel_multiplier=cm))

                step(pool.memset(k.ident[:, :], 0.0))
                select(k.ident[:, :], [[-1, P]], 0, 1, ALU.not_equal, 1.0)
                step(pool.memset(k.ii[:, :], 0.0))
                select(k.ii[:, :], [[-1, 64]], 0, 1, ALU.not_equal, 1.0)
                select(k.ii[:, :], [[-1, 64]], -64, 1, ALU.not_equal, 1.0)
                step(pool.memset(k.pair[:, :], 0.0))
                step(pool.memset(k.pair[0:64, 0:64], 1.0))
                step(pool.memset(k.pair[64:128, 64:128], 1.0))
                for m, base in ((k.m_lt, 0), (k.m_le, 1)):
                    step(pool.tensor_copy(m[:, :], k.pair[:, :]))
                    select(m[:, :], [[1, P]], base, -1, ALU.is_gt, 0.0)
                eight = k.m_lt8[:, :].rearrange("p (a b) -> p a b", b=8)
                step(pool.memset(k.m_lt8[:, :], 1.0))
                select(eight, [[-8, 16], [0, 8]], 0, 1, ALU.is_ge, 0.0)
                select(eight, [[8, 16], [0, 8]], 7, -1, ALU.is_ge, 0.0)
                step(pool.tensor_copy(k.m_gt8[:, :], k.m_lt8[:, :]))
                select(k.m_lt8[:, :], [[1, P]], 0, -1, ALU.is_gt, 0.0)
                select(k.m_gt8[:, :], [[-1, P]], 0, 1, ALU.is_gt, 0.0)
                step(pool.tensor_copy(k.m_gto[:, :], k.pair[:, :]))
                select(k.m_gto[:, :], [[-1, P]], 0, 1, ALU.is_gt, 0.0)
                step(pool.tensor_tensor(k.m_gto[:, :], k.m_gto[:, :], k.m_gt8[:, :], ALU.subtract))
                step(pool.memset(k.restart[:, :], 1.0))
                step(pool.memset(k.restart[:, :].rearrange("p (a t) -> p a t", t=C)[:, :, 0:1], 0.0))
                step(pool.memset(k.half_power[:, :], -0.5))
                step(pool.memset(k.one[:, :], 1.0))
                step(pool.memset(k.eps[:, :], EPS))
                k.made_total = n[0]

            @block.tensor
            def _(pe):
                pe.wait_ge(made, k.made_total)
                pe.wait_ge(loaded, 16 * (len(VECS) + len(CROWS) + 3))
                pe.transpose(ps[:, 0:NVEC], rows[:, :], k.ident[0:NVEC, 0:NVEC])
                pe.transpose(ps[:, 128:128 + NCROW], crows[:, :], k.ident[0:NCROW, 0:NCROW]).then_inc(turned, 1)

            @block.vector
            def _(dve):
                dve.wait_ge(turned, 1)
                dve.tensor_copy(k.vec[:, :], ps[:, 0:NVEC]).then_inc(kept, 1)
                dve.tensor_copy(k.cvec[:, :], ps[:, 128:128 + NCROW]).then_inc(kept, 1)
                dve.wait_ge(kept, 2)
                r = VROW["k_a"]
                dve.tensor_scalar(k.one_minus_ka[:, :], k.vec[:, r:r + 4], -1.0, 1.0, ALU.mult, ALU.add).then_inc(kept, 1)


SLICE = 2 * P
NSL = 48 * P // SLICE


class Modulation:

    def __init__(self, ctx, nc, k):
        self.k = k
        self.w = ctx.enter_context(nc.sbuf_tensor("ada_w", [P, 2, KD, SLICE], F32))
        self.sil = ctx.enter_context(nc.sbuf_tensor("silu_c", [P, 2, KD], F32))
        self.tnh = ctx.enter_context(nc.sbuf_tensor("tanh_c", [P, 2 * KD], F32))
        self.rows = ctx.enter_context(nc.sbuf_tensor("mod_rows", [2, 2, SLICE], F32))
        self.ps = [ctx.enter_context(nc.psum_tensor(f"mod_ps{i}", [P, 512], F32)) for i in range(2)]
        self.loaded = [ctx.enter_context(nc.semaphore(f"ada_loaded{i}")) for i in range(2)]
        self.rows_s, self.turned_s = Steps(ctx, nc, "mod_rows_made", ["rows"]), Steps(ctx, nc, "mod_turned", ["turned"])
        self.kept_s, self.mod_s = Steps(ctx, nc, "mod_rows_kept", ["kept"]), Steps(ctx, nc, "mod_made", ["mod"])
        self.src = k.w_ada.rearrange("(k p) n -> p k n", p=P)

    def load(self, sp, s, par):
        self.rows_s.wait(sp, "rows", s)
        sp.dma_start(self.w[:, par], self.src[:, :, ds(s * SLICE, SLICE)]).then_inc(self.loaded[par], 16)

    def make_rows(self, pe, s, par, nth):
        pe.wait_ge(self.loaded[par], 16 * nth)
        self.mod_s.wait(pe, "mod", s)
        for kk in range(KD):
            mm = pe.matmul(self.ps[par][0:2, 0:SLICE], self.sil[:, :, kk], self.w[:, par, kk, :], start=(kk == 0), stop=(kk == KD - 1))
        self.rows_s.done(mm, "rows")

    def keep(self, act, s, par):
        self.rows_s.wait(act, "rows", s + 2)
        self.turned_s.wait(act, "turned", s)
        self.kept_s.done(act.activation(self.rows[:, par, :], self.ps[par][0:2, 0:SLICE], ACT.Copy), "kept")

    def turn(self, pe, s, par):
        for j in range(2):
            mm = pe.transpose(self.ps[par][:, SLICE + 2 * j:SLICE + 2 * j + 2], self.rows[:, par, j * P:(j + 1) * P], self.k.ident[0:2, 0:2])
        self.turned_s.done(mm, "turned")

    def add_bias(self, dve, s, par):
        self.turned_s.wait(dve, "turned", s + 2)
        self.mod_s.done(dve.tensor_tensor(self.k.mod[:, ds(2 * s, 2), :], self.ps[par][:, SLICE:SLICE + 4].rearrange("p (j g) -> p j g", g=2),
                                          bc(self.k.vec[:, ds(2 * s, 2)], 2), ALU.add), "mod")


def build_modulation(nc, k, m):
    FIRST = 16 * P // SLICE
    with ExitStack() as ctx:
        tanh_done = ctx.enter_context(nc.semaphore("tanh_done"))
        v = ctx.enter_context(nc.semaphore("silu_steps"))
        with nc.Block() as block:
            @block.sync
            def _(sp):
                for s in range(FIRST):
                    if s >= 2:
                        m.rows_s.wait(sp, "rows", s)
                    sp.dma_start(m.w[:, s % 2], m.src[:, :, s * SLICE:(s + 1) * SLICE]).then_inc(m.loaded[s % 2], 16)

            @block.scalar
            def _(act):
                m.kept_s.open(act)
                m.kept_s.open(act)
                act.activation(m.tnh[:, :], k.cvec[:, 0:2 * KD], ACT.Tanh, scale=0.5).then_inc(tanh_done, 1)
                for s in range(FIRST):
                    m.keep(act, s, s % 2)

            @block.tensor
            def _(pe):
                for steps in (m.rows_s, m.turned_s):
                    steps.open(pe)
                    steps.open(pe)
                pe.wait_ge(v, 2)
                m.make_rows(pe, 0, 0, 1)
                for s in range(FIRST):
                    if s + 1 < FIRST:
                        m.make_rows(pe, s + 1, (s + 1) % 2, (s + 1) // 2 + 1)
                    m.kept_s.wait(pe, "kept", s + 2)
                    m.turn(pe, s, s % 2)

            @block.vector
            def _(dve):
                m.mod_s.open(dve)
                m.mod_s.open(dve)
                dve.wait_ge(tanh_done, 1)
                dve.tensor_scalar(m.tnh[:, :], m.tnh[:, :], 0.5, 0.5, ALU.mult, ALU.add).then_inc(v, 1)
                dve.wait_ge(v, 1)
                dve.tensor_tensor(m.sil[:, :, :].rearrange("p c k -> p (c k)"), m.tnh[:, :], k.cvec[:, 0:2 * KD],
                                  ALU.mult).then_inc(v, 1)
                for s in range(FIRST):
                    m.add_bias(dve, s, s % 2)
                m.mod_s.wait(dve, "mod", FIRST + 1)
                dve.tensor_scalar(k.gain1[:, :, :], k.mod[:, 8:16, :], 1.0, None, ALU.add).then_inc(v, 1)
                dve.wait_ge(v, 3)
                r = VROW["norm_mix_g"]
                dve.tensor_tensor(k.gain1[:, :, :], k.gain1[:, :, :], bc(k.vec[:, r:r + 8], 2), ALU.mult).then_inc(v, 1)


def build_first_norm(nc, k, m):
    with ExitStack() as ctx:
        xt = ctx.enter_context(nc.sbuf_tensor("x_rows", [P, 2, D], F32))
        junk = ctx.enter_context(nc.sbuf_tensor("x_squares", [P, D], F32))
        xs = ctx.enter_context(nc.sbuf_tensor("x_turned", [P, 2, KD, P], F32))
        h = ctx.enter_context(nc.sbuf_tensor("h_tile", [P, 2, KD, P], F32))
        ss = ctx.enter_context(nc.sbuf_tensor("x_ss", [P, 2], F32))
        rs = ctx.enter_context(nc.sbuf_tensor("x_rstd", [P, 2], F32))
        diag = ctx.enter_context(nc.sbuf_tensor("x_rstd_diagonal", [P, 2, P], F32))
        ones = ctx.enter_context(nc.sbuf_tensor("x_ones", [P, P], F32))
        px = [ctx.enter_context(nc.psum_tensor(f"x_ps{i}", [P, KD, P], F32)) for i in range(2)]
        pb = [ctx.enter_context(nc.psum_tensor(f"x_rstd_ps{i}", [P, 512], F32)) for i in range(2)]
        loaded = [ctx.enter_context(nc.semaphore(f"x_loaded{i}")) for i in range(2)]
        stored = [ctx.enter_context(nc.semaphore(f"xT_stored{i}")) for i in range(2)]
        ones_made = ctx.enter_context(nc.semaphore("x_ones_made"))
        fin = ctx.enter_context(nc.semaphore("gain2_steps"))
        squares_s, hi_s = Steps(ctx, nc, "norm1_squares", ["squares"]), Steps(ctx, nc, "norm1_hi", ["hi"])
        xT_s = Steps(ctx, nc, "norm1_xT", ["xT"])
        rstd_s, shift_s = Steps(ctx, nc, "norm1_rstd", ["rstd"]), Steps(ctx, nc, "norm1_shift", ["shift"])
        mean_s = Steps(ctx, nc, "norm1_mean", ["mean", "diag"])
        dve_s = Steps(ctx, nc, "norm1_dve", ["normed", "gain", "lo"])
        pe_s = Steps(ctx, nc, "norm1_pe", ["x", "rstd"])
        xT = k.xT.rearrange("(k p) t -> p k t", p=P)
        NTILE = SEQ // P
        FIRST = 16 * P // SLICE
        assert NSL - FIRST == NTILE

        def each_tile(eng, body):
            with eng.Fori(0, NTILE // 2) as i:
                for par in range(2):
                    body(2 * i + par, i + 1, par, ds((2 * i + par) * P, P), P)
            body(NTILE, NTILE // 2 + 1, 0, slice(SEQ, NT), DEC)

        with nc.Block() as block:
            @block.sync
            def _(sp):
                def body(t, nth, par, tok, n):
                    squares_s.wait(sp, "squares", t)
                    pe_s.wait(sp, "x", t)
                    src = k.x_prompt[ds((t + 3) * P - 3 * P, P), :] if n == P else k.x_sample
                    sp.dma_start(xt[0:n, par, :], src).then_inc(loaded[par], 16)
                    if n == P:
                        m.load(sp, FIRST + t, par)
                each_tile(sp, body)

            @block.scalar
            def _(act):
                for steps in (squares_s, xT_s, hi_s):
                    steps.open(act)
                    steps.open(act)
                for par in range(2):
                    act.sem_inc(stored[par], 16)

                def squares(t, nth, par):
                    act.wait_ge(loaded[par], 16 * nth)
                    mean_s.wait(act, "mean", t)
                    squares_s.wait(act, "squares", t + 1)
                    squares_s.done(act.activation(junk[:, :], xt[:, par, :], ACT.Square, accum_out=ss[:, par:par + 1]), "squares")

                def take_xT(t, nth, par):
                    act.wait_ge(stored[par], 16 * nth)
                    dve_s.wait(act, "normed", t)
                    pe_s.wait(act, "x", t + 2)
                    xT_s.done(act.activation(xs[:, par, :, :], px[par][:, :, :], ACT.Copy), "xT")

                def body(t, nth, par, tok, n):
                    xT_s.wait(act, "xT", t + 2)
                    act.dma_start(xT[:, :, tok], xs[:, par, :, 0:n]).then_inc(stored[par], 16)
                    if n == P:
                        m.keep(act, FIRST + t, par)
                        squares(t + 1, nth + par, 1 - par)
                        take_xT(t + 1, nth + par, 1 - par)
                    shift_s.wait(act, "shift", t + 2)
                    hi_s.done(act.activation(k.h_hi[:, :, tok], h[:, par, :, 0:n], ACT.Copy), "hi")
                squares(0, 1, 0)
                take_xT(0, 1, 0)
                each_tile(act, body)
                act.wait_ge(stored[0], 16 * (NTILE // 2 + 2))
                act.wait_ge(stored[1], 16 * (NTILE // 2 + 1))

            @block.gpsimd
            def _(pool):
                for steps in (rstd_s, shift_s):
                    steps.open(pool)
                    steps.open(pool)
                pool.memset(ones[:, :], 1.0).then_inc(ones_made, 1)

                def rstd(t, par):
                    mean_s.wait(pool, "mean", t + 2)
                    rstd_s.done(pool.tensor_tensor(rs[:, par:par + 1], rs[:, par:par + 1], k.half_power[:, 0:1], ALU.pow), "rstd")

                def body(t, nth, par, tok, n):
                    if n == P:
                        rstd(t + 1, 1 - par)
                    dve_s.wait(pool, "gain", t + 2)
                    g = 0 if n == P else 1
                    shift_s.done(pool.tensor_tensor(h[:, par, :, 0:n], h[:, par, :, 0:n], bc(k.mod[:, 0:8, g], n), ALU.add), "shift")
                rstd(0, 0)
                each_tile(pool, body)

            @block.tensor
            def _(pe):
                pe_s.open(pe)
                pe_s.open(pe)
                pe.wait_ge(ones_made, 1)

                def body(t, nth, par, tok, n):
                    pe.wait_ge(loaded[par], 16 * nth)
                    xT_s.wait(pe, "xT", t)
                    for kk in range(KD):
                        mm = pe.transpose(px[par][:, kk, 0:n], xt[0:n, par, kk * P:(kk + 1) * P], k.ident[0:n, 0:n])
                    pe_s.done(mm, "x")
                    if n == P:
                        m.make_rows(pe, FIRST + t, par, nth + FIRST // 2)
                    mean_s.wait(pe, "diag", t + 2)
                    dve_s.wait(pe, "normed", t)
                    if n == P:
                        m.kept_s.wait(pe, "kept", FIRST + t + 2)
                    pe_s.done(pe.matmul(pb[par][:, 0:n], ones[0:n, :], diag[0:n, par, 0:n], start=True, stop=True), "rstd")
                    if n == P:
                        m.turn(pe, FIRST + t, par)
                each_tile(pe, body)

            @block.vector
            def _(dve):
                for steps in (mean_s, dve_s):
                    steps.open(dve)
                    steps.open(dve)

                def mean(t, par):
                    squares_s.wait(dve, "squares", t + 2)
                    mean_s.done(dve.tensor_scalar(rs[:, par:par + 1], ss[:, par:par + 1], 1.0 / D, EPS, ALU.mult, ALU.add), "mean")
                    rstd_s.wait(dve, "rstd", t + 2)
                    pe_s.wait(dve, "rstd", t)
                    mean_s.done(dve.tensor_scalar(diag[:, par, :], k.ident[:, :], rs[:, par:par + 1], None, ALU.mult), "diag")

                def body(t, nth, par, tok, n):
                    g = 0 if n == P else 1
                    xT_s.wait(dve, "xT", t + 2)
                    hi_s.wait(dve, "hi", t)
                    pe_s.wait(dve, "rstd", t + 2)
                    hp = h[:, par, :, 0:n]
                    dve_s.done(dve.tensor_tensor(hp, xs[:, par, :, 0:n], bcm(pb[par][:, 0:n], KD), ALU.mult), "normed")
                    dve_s.wait(dve, "normed", t + 2)
                    dve_s.done(dve.tensor_tensor(hp, hp, bc(k.gain1[:, :, g], n), ALU.mult), "gain")
                    if n == P:
                        m.add_bias(dve, FIRST + t, par)
                        mean(t + 1, 1 - par)
                    hi_s.wait(dve, "hi", t + 2)
                    dve_s.done(dve.tensor_tensor(k.h_lo[:, :, tok], hp, k.h_hi[:, :, tok].bitcast(F32), ALU.subtract), "lo")
                mean(0, 0)
                each_tile(dve, body)
                m.mod_s.wait(dve, "mod", NSL + 1)
                dve.tensor_scalar(k.gain2[:, :, :], k.mod[:, 32:40, :], 1.0, None, ALU.add).then_inc(fin, 1)
                dve.wait_ge(fin, 1)
                r = VROW["norm_mlp_g"]
                dve.tensor_tensor(k.gain2[:, :, :], k.gain2[:, :, :], bc(k.vec[:, r:r + 8], 2), ALU.mult).then_inc(fin, 1)
                dve.wait_ge(fin, 2)
                for b in range(NB):
                    g = 1 if b == NB - 1 else 0
                    dve.tensor_copy(k.tail[:, b, 0:8], k.gain2[:, :, g])
                    dve.tensor_copy(k.tail[:, b, 8:16], k.mod[:, 24:32, g])
                    dve.tensor_copy(k.tail[:, b, 16:24], k.mod[:, 40:48, g]).then_inc(fin, 1)


class Projection:

    def __init__(self, ctx, nc, k):
        self.k = k
        self.raw = ctx.enter_context(nc.sbuf_tensor("w_raw", [P, KD, P], F32))
        self.hi = ctx.enter_context(nc.sbuf_tensor("w_hi", [P, 2, KD, P], F32R))
        self.lo = ctx.enter_context(nc.sbuf_tensor("w_lo", [P, 2, KD, P], F32R))
        self.out = ctx.enter_context(nc.sbuf_tensor("proj_out", [P, 2, BW], F32))
        self.ps = [ctx.enter_context(nc.psum_tensor(f"proj_ps{i}", [P, 512], F32)) for i in range(2)]
        self.loaded = ctx.enter_context(nc.semaphore("w_loaded"))
        self.stored = [ctx.enter_context(nc.semaphore(f"proj_stored{i}")) for i in range(2)]
        self.hi_s = Steps(ctx, nc, "w_hi_made", ["hi"])
        self.lo_s = Steps(ctx, nc, "w_lo_made", ["lo"])
        self.mm_s = Steps(ctx, nc, "proj_mm", [0, 1, 2, 3, 4])
        self.out_s = Steps(ctx, nc, "proj_evacuated", [0, 1, 2, 3, 4])
        self.w = k.w_in.rearrange("(k p) n -> p k n", p=P)

    def load(self, sp, turn):
        self.lo_s.wait(sp, "lo", turn - 1)
        sp.dma_start(self.raw[:, :, :], self.w[:, :, ds((turn - 2) * P, P)]).then_inc(self.loaded, 16)

    def make_hi(self, act, turn, par):
        act.wait_ge(self.loaded, 16 * (turn - 1))
        self.mm_s.wait(act, 4, turn - 2)
        self.hi_s.done(act.activation(self.hi[:, par], self.raw[:, :, :], ACT.Copy), "hi")

    def make_lo(self, pool, turn, par):
        self.hi_s.wait(pool, "hi", turn)
        self.lo_s.done(pool.tensor_tensor(self.lo[:, par], self.raw[:, :, :], self.hi[:, par].bitcast(F32), ALU.subtract), "lo")

    def products(self, pe, turn, par):
        self.lo_s.wait(pe, "lo", turn)
        for b in range(NB):
            u = (par * NB + b) % 2
            if b >= 2:
                self.out_s.wait(pe, b - 2, turn)
            else:
                self.out_s.wait(pe, b + 3, turn - 1)
            cols = slice(b * BW, (b + 1) * BW)
            for kk in range(KD):
                for j, (w, a) in enumerate(((self.hi, self.k.h_hi), (self.hi, self.k.h_lo), (self.lo, self.k.h_hi))):
                    mm = pe.matmul(self.ps[u][:, 0:BW], w[:, par, kk, :], a[:, kk, cols],
                                   start=(kk == 0 and j == 0), stop=(kk == KD - 1 and j == 2))
                    if kk == KD - 1 and j == 2:
                        self.mm_s.done(mm, b)
                    yield

    def evacuate(self, act, turn, par, b):
        u = par * NB + b
        act.wait_ge(self.stored[u % 2], 8 * NB * (turn - 2 - par) + 16 * (u // 2) + 16)
        self.mm_s.wait(act, b, turn)
        self.out_s.done(act.activation(self.out[:, u % 2, :], self.ps[u % 2][:, 0:BW], ACT.Copy), b)
        self.out_s.wait(act, b, turn)
        act.dma_start(self.k.proj[ds((turn - 2) * P, P), b * BW:(b + 1) * BW], self.out[:, u % 2, :]).then_inc(self.stored[u % 2], 16)

    def wait_stored(self, act, turns):
        for j in range(2):
            act.wait_ge(self.stored[j], 16 * (turns * NB // 2) + 16)

    def open(self, steps, eng):
        steps.open(eng)
        steps.open(eng)


def build_projection_rwkv(nc, k, pj):
    with nc.Block() as block:
        @block.sync
        def _(sp):
            pj.load(sp, 2)
            with sp.Fori(0, RT // 2) as i:
                for par in range(2):
                    pj.load(sp, 2 * i + par + 3)

        @block.scalar
        def _(act):
            pj.open(pj.hi_s, act)
            pj.open(pj.out_s, act)
            for stored in pj.stored:
                act.sem_inc(stored, 16)
            pj.make_hi(act, 2, 0)
            with act.Fori(0, RT // 2) as i:
                for par in range(2):
                    pj.make_hi(act, 2 * i + par + 3, 1 - par)
                    for b in range(NB):
                        pj.evacuate(act, 2 * i + par + 2, par, b)
            pj.wait_stored(act, RT)

        @block.gpsimd
        def _(pool):
            pj.open(pj.lo_s, pool)
            pj.make_lo(pool, 2, 0)
            with pool.Fori(0, RT // 2) as i:
                for par in range(2):
                    pj.make_lo(pool, 2 * i + par + 3, 1 - par)

        @block.tensor
        def _(pe):
            pj.open(pj.mm_s, pe)
            with pe.Fori(0, RT // 2) as i:
                for par in range(2):
                    for _product in pj.products(pe, 2 * i + par + 2, par):
                        pass


POOL_FRONT = ["diff", "scaled", "xs", "prev", "kk"]
ACT_FRONT = ["tanh", "xa", "tsg"]
DVE_FRONT = ["sg"]
DVE_STEPS = ["z0", "z1", "sig", "scan", "t1", "t2", "k2", "rho0", "rho1", "kh0",
             "kh1", "ssm", "inv", "kkn", "b", "kap0", "kap1", "bh0", "bh1", "bv", "Nd", "Mb", "Lk", "Mk", "Ld", "Lo", "L2", "X2", "X3", "y",
             "Y2", "Q2", "Q3", "Sa", "S", "sum", "mean", "oc", "var", "varm", "on0", "on1", "yg", "yb", "yv", "yr"]
ACT_STEPS = ["tz", "W", "Wi", "norm", "g", "Vp", "Kt", "Bt", "N2", "L4", "yt", "Y2T", "Y4T", "RH", "R2",
             "SA", "osq"]
POOL_STEPS = ["sq", "v0", "v1", "rk", "rkk", "X1", "Q1", "rstd"]
PE_STEPS = ["wa", "g", "ss", "V", "bon", "gb", "gk", "gl", "KtT", "BtT", "N2", "L2", "X2", "L4", "X3", "y", "yt",
            "Y2T", "Y2", "Q2", "Y4T", "Q3", "RH", "R2", "SA", "O", "S", "OT"]


class Rwkv:

    def __init__(self, ctx, nc, k, pj):
        self.k, self.pj = k, pj

        def sb(name, shape):
            return ctx.enter_context(nc.sbuf_tensor(name, shape, F32))
        self.praw = sb("rows_in", [P, RT, C + 1])
        self.xs = sb("rows_mixed", [P, RT, C])
        self.th = sb("lora_in", [P, 3, C])
        self.z = sb("decay_and_a", [P, 2 * NP, C])
        self.L = sb("decay_sums", [P, NP, C])
        self.W = sb("decays", [P, NP, C + 1])
        self.kk = sb("kk", [P, NP, C])
        self.inv = sb("kk_scale", [P, NP, C])
        self.KR = sb("kap_rho_wide", [P, NP, 2, P])
        self.KB = sb("kh_bh_wide", [P, 2, NP, P])
        self.vw = sb("v_or_o_wide", [P, NP, P])
        self.Mb, self.Lk, self.Mk = (sb(n, [P, NP, P]) for n in ("rho_bh", "kap_kh", "rho_kh"))
        solve = sb("solve", [P, 6 * NP * P])
        self.R = [solve[:, j * NP * P:(j + 1) * NP * P].rearrange("p (a t) -> p a t", t=P) for j in range(6)]
        self.S = sb("state", [P, NP, C])
        self.stat = sb("o_stats", [P, 2, NP])
        late = solve[:, 4 * NP * P:4 * NP * P + 12 * C].rearrange("p (a t) -> p a t", t=C)
        self.t, self.b, self.rk = late[:, 0:4, :], late[:, 4:8, :], late[:, 8:12, :]
        self.sq, self.RH, self.R2, self.SA = (self.R[j][:, :, 0:C] for j in (1, 1, 2, 4))
        self.Wi = self.Vp = self.z[:, 0:NP, :]
        self.g = self.z[:, NP:2 * NP, :]
        self.osq, self.oc, self.bv = self.R[3][:, :, 0:C], self.inv, self.L
        self.two = [ctx.enter_context(nc.psum_tensor(f"wkv_two{j}", [P, 1024], F32)) for j in range(2)]
        one = [ctx.enter_context(nc.psum_tensor(f"wkv_ps{j}", [P, 512], F32)) for j in range(2)]
        self.bank = [self.two[j // 2][:, (j % 2) * 512:(j % 2 + 1) * 512] for j in range(4)] + [t[:, :] for t in one]
        self.rows_loaded = ctx.enter_context(nc.semaphore("rows_loaded"))
        self.y_stored = ctx.enter_context(nc.semaphore("yr_stored"))
        self.dve_s = Steps(ctx, nc, "wkv_dve", DVE_STEPS)
        self.act_s = Steps(ctx, nc, "wkv_act", ACT_STEPS)
        self.pool_s = Steps(ctx, nc, "wkv_pool", POOL_STEPS)
        self.pool_f, self.act_f = Steps(ctx, nc, "front_pool", POOL_FRONT), Steps(ctx, nc, "front_act", ACT_FRONT)
        self.dve_f = Steps(ctx, nc, "front_dve", DVE_FRONT)
        self.pe_s = Steps(ctx, nc, "wkv_pe", PE_STEPS)

    def narrow(self, j):
        return self.bank[j][:, 0:NP * C].rearrange("p (a t) -> p a t", t=C)

    def full(self, j):
        return self.bank[j][:, :].rearrange("p (a t) -> p a t", t=P)

    def cv(self, name, n):
        r = VROW[name]
        return bc(self.k.vec[:, r:r + n], C)

    def sync_chunk(self, sp, turn, cols, n=C):
        self.pool_f.wait(sp, "prev", turn - 1)
        sp.dma_start(self.praw[:, :, 1:n + 1],
                     self.k.proj[0:R_PROJ, cols].rearrange("(r p) t -> p r t", p=P)).then_inc(self.rows_loaded, 16)

    def store_chunk(self, sp, turn, cols, n=C):
        self.dve_s.wait(sp, "yr", turn)
        sp.dma_start(self.k.yrT[:, cols].rearrange("(a p) t -> p a t", p=P), self.oc[:, :, 0:n]).then_inc(self.y_stored, 16)

    def pool_front(self, pool, turn, n=C):
        f = self.pool_f

        def tt(out, x, y, o, name):
            f.done(pool.tensor_tensor(out, x, y, o), name)
        xs, cur = self.xs[:, :, 0:n], self.praw[:, :, 1:n + 1]
        pool.wait_ge(self.rows_loaded, 16 * turn)
        self.dve_s.wait(pool, "bv", turn - 1)
        tt(xs, self.praw[:, :, 0:n], cur, ALU.subtract, "diff")
        f.wait(pool, "diff", turn)
        r = VROW["mu_shift"]
        tt(xs, xs, bc(self.k.vec[:, r:r + RT], n), ALU.mult, "scaled")
        f.wait(pool, "scaled", turn)
        tt(xs, xs, cur, ALU.add, "xs")
        f.wait(pool, "xs", turn)
        tt(self.praw[:, :, 0:1], self.praw[:, :, C:C + 1], bc(self.k.one[:, :].broadcast_to([P, RT]), 1), ALU.mult, "prev")
        tt(self.kk[:, :, :], self.xs[:, 4:8, :], self.cv("k_k", 4), ALU.mult, "kk")

    def scalar_front(self, act, turn):
        def f(out, x, func, name, **kw):
            self.act_f.done(act.activation(out, x, func, **kw), name)
        self.pool_f.wait(act, "xs", turn)
        self.pe_s.wait(act, "g", turn - 1)
        f(self.th[0:64, 0, :], self.xs[0:64, 12, :], ACT.Tanh, "tanh")
        f(self.th[64:128, 1, :], self.xs[64:128, 12, :], ACT.Copy, "xa")
        f(self.th[:, 2, :], self.xs[:, 13, :], ACT.Tanh, "tsg", scale=0.5)

    def vector_front(self, dve, turn):
        self.act_f.wait(dve, "tsg", turn)
        self.dve_f.done(dve.tensor_scalar(self.th[:, 2, :], self.th[:, 2, :], 0.5, 0.5, ALU.mult, ALU.add), "sg")

    def vector_chunk(self, dve, turn, par, sample=False, ahead=True):
        k, R = self.k, self.R
        v, a, g, p = self.dve_s, self.act_s, self.pool_s, self.pe_s

        def op(ins, name):
            v.done(ins, name)

        def tt(out, x, y, o, name):
            v.done(dve.tensor_tensor(out, x, y, o), name)
        n = DEC if sample else C
        p.wait(dve, "wa", turn)
        v.wait(dve, "yr", turn - 1)
        for half, name in enumerate(("w0", "a0")):
            r = VROW[name]
            tt(self.z[:, half * NP:(half + 1) * NP, 0:n], self.bank[0].rearrange("p (a w t) -> p a w t", a=NP, w=2)[:, :, half, 0:n],
               bc(k.vec[:, r:r + 4], n), ALU.add, f"z{half}")
        a.wait(dve, "tz", turn)
        op(dve.tensor_scalar(self.z[:, :, 0:n], self.z[:, :, 0:n], 0.5, 0.5, ALU.mult, ALU.add), "sig")
        v.wait(dve, "sig", turn)
        op(dve.tensor_tensor_scan(self.L[:, :, :].rearrange("p a t -> p (a t)"), k.restart[:, :],
                                  self.z[:, 0:NP, :].rearrange("p a t -> p (a t)"), 0.0, ALU.mult, ALU.add), "scan")
        av = self.z[:, NP:2 * NP, :]
        p.wait(dve, "S", turn - 1)
        self.pool_f.wait(dve, "xs", turn)
        tt(self.t, av, self.cv("k_a", 4), ALU.mult, "t1")
        v.wait(dve, "t1", turn)
        tt(self.t, self.t, bc(k.one_minus_ka[:, :], C), ALU.add, "t2")
        v.wait(dve, "t2", turn)
        tt(self.t, self.t, self.xs[:, 4:8, :], ALU.mult, "k2")
        a.wait(dve, "Wi", turn)
        lo, hi = slice(0, 64), slice(64, 128)
        for h, rows in ((0, lo), (1, hi)):
            tt(self.KR[rows, :, 1, rows], self.xs[rows, 0:4, :], self.W[rows, :, 1:C + 1], ALU.mult, f"rho{h}")
        v.wait(dve, "k2", turn)
        for h, rows in ((0, lo), (1, hi)):
            tt(self.KB[rows, 0, :, rows], self.t[rows], self.Wi[rows], ALU.mult, f"kh{h}")
        a.wait(dve, "norm", turn)
        op(dve.tensor_scalar(self.inv[:, :, :], self.inv[:, :, :], 1e-12, None, ALU.max), "ssm")
        v.wait(dve, "ssm", turn)
        op(dve.reciprocal(self.inv[:, :, :], self.inv[:, :, :]), "inv")
        v.wait(dve, "inv", turn)
        tt(self.kk[:, :, :], self.kk[:, :, :], self.inv[:, :, :], ALU.mult, "kkn")
        v.wait(dve, "kkn", turn)
        tt(self.b, self.kk[:, :, :], av, ALU.mult, "b")
        for h, rows in ((0, lo), (1, hi)):
            tt(self.KR[rows, :, 0, rows], self.kk[rows, :, :], self.W[rows, :, 0:C], ALU.mult, f"kap{h}")
        v.wait(dve, "b", turn)
        for h, rows in ((0, lo), (1, hi)):
            op(dve.scalar_tensor_tensor(out=self.KB[rows, 1, :, rows], in0=self.b[rows], scalar=-1.0,
                                        in1=self.Wi[rows], op0=ALU.mult, op1=ALU.mult), f"bh{h}")
        p.wait(dve, "bon", turn)
        tt(self.bv[:, :, :], self.narrow(3), self.xs[:, 8:12, :], ALU.mult, "bv")
        both = [self.two[0][:, :].rearrange("p (a w t) -> p a w t", a=NP, w=2), self.two[1][:, :].rearrange("p (a w t) -> p a w t", a=NP, w=2)]
        p.wait(dve, "gb", turn)
        tt(R[0][:, :, :], both[0][:, :, 0, :], bcm(k.m_lt8[:, :], NP), ALU.mult, "Nd")
        tt(self.Mb[:, :, :], both[0][:, :, 1, :], bcm(k.m_le[:, :], NP), ALU.mult, "Mb")
        p.wait(dve, "gk", turn)
        tt(self.Lk[:, :, :], both[1][:, :, 0, :], bcm(k.m_lt[:, :], NP), ALU.mult, "Lk")
        tt(self.Mk[:, :, :], both[1][:, :, 1, :], bcm(k.m_le[:, :], NP), ALU.mult, "Mk")
        p.wait(dve, "gl", turn)
        tt(R[1][:, :, :], self.full(4), bcm(k.m_gt8[:, :], NP), ALU.mult, "Ld")
        tt(R[2][:, :, :], self.full(4), bcm(k.m_gto[:, :], NP), ALU.mult, "Lo")
        p.wait(dve, "L2", turn)
        op(dve.tensor_copy(R[4][:, :, :], self.full(2)), "L2")
        p.wait(dve, "X2", turn)
        g.wait(dve, "X1", turn)
        tt(R[0][:, :, :], self.full(3), R[5][:, :, :], ALU.add, "X2")
        p.wait(dve, "X3", turn)
        v.wait(dve, "X2", turn)
        tt(R[3][:, :, :], self.full(5), R[0][:, :, :], ALU.add, "X3")
        p.wait(dve, "y", turn)
        op(dve.tensor_copy(R[4][:, :, :], self.full(0)), "y")
        p.wait(dve, "Y2", turn)
        op(dve.tensor_copy(R[1][:, :, :], self.full(3)), "Y2")
        p.wait(dve, "Q2", turn)
        g.wait(dve, "Q1", turn)
        tt(R[5][:, :, :], self.full(4), R[2][:, :, :], ALU.add, "Q2")
        p.wait(dve, "Q3", turn)
        v.wait(dve, "Q2", turn)
        tt(R[0][:, :, :], self.full(0), R[5][:, :, :], ALU.add, "Q3")
        if ahead:
            self.vector_front(dve, turn + 1)
        p.wait(dve, "S", turn)
        tt(self.S[:, :, :], self.narrow(5), self.S[:, :, :], ALU.add, "Sa")
        v.wait(dve, "Sa", turn)
        tt(self.S[:, :, :], self.S[:, :, :], self.W[:, :, C:C + 1].broadcast_to([P, NP, C]), ALU.mult, "S")
        op(dve.tensor_reduce(self.stat[:, 0, :], self.narrow(4), AX.X, ALU.add), "sum")
        v.wait(dve, "sum", turn)
        op(dve.tensor_scalar(self.stat[:, 0, :], self.stat[:, 0, :], 1.0 / HD, None, ALU.mult), "mean")
        v.wait(dve, "mean", turn)
        tt(self.oc[:, :, :], self.narrow(4), bc(self.stat[:, 0, :], C), ALU.subtract, "oc")
        a.wait(dve, "osq", turn)
        op(dve.tensor_reduce(self.stat[:, 1, :], self.osq[:, :, :], AX.X, ALU.add), "var")
        v.wait(dve, "var", turn)
        op(dve.tensor_scalar(self.stat[:, 1, :], self.stat[:, 1, :], 1.0 / HD, GN_EPS, ALU.mult, ALU.add), "varm")
        g.wait(dve, "rstd", turn)
        for h, rows in ((0, lo), (1, hi)):
            tt(self.vw[rows, :, rows], self.oc[rows, :, :], bc(self.stat[rows, 1, :], C), ALU.mult, f"on{h}")
        p.wait(dve, "OT", turn)
        tt(self.oc[:, :, :], self.narrow(3), self.cv("lnx_g", 4), ALU.mult, "yg")
        v.wait(dve, "yg", turn)
        tt(self.oc[:, :, :], self.oc[:, :, :], self.cv("lnx_b", 4), ALU.add, "yb")
        v.wait(dve, "yb", turn)
        tt(self.oc[:, :, :], self.oc[:, :, :], self.bv[:, :, :], ALU.add, "yv")
        v.wait(dve, "yv", turn)
        tt(self.oc[:, :, :], self.oc[:, :, :], self.g[:, :, :], ALU.mult, "yr")

    def scalar_chunk(self, act, turn, par, evac, hi_turn, ahead=True):
        v, a, p = self.dve_s, self.act_s, self.pe_s

        def f(out, x, func, name, **kw):
            a.done(act.activation(out, x, func, **kw), name)
        v.wait(act, "z1", turn)
        f(self.z[:, :, :], self.z[:, :, :], ACT.Tanh, "tz", scale=0.5)
        v.wait(act, "scan", turn)
        f(self.W[:, :, 1:C + 1], self.L[:, :, :], ACT.Exp, "W", scale=-KAPPA)
        f(self.Wi[:, :, :], self.L[:, :, :], ACT.Exp, "Wi", scale=KAPPA)
        p.wait(act, "ss", turn)
        act.wait_ge(self.y_stored, 16 * turn)
        f(self.inv[:, :, :], self.narrow(2), ACT.Sqrt, "norm")
        evac(0)
        p.wait(act, "g", turn)
        v.wait(act, "b", turn)
        f(self.g, self.narrow(1), ACT.Copy, "g")
        p.wait(act, "V", turn)
        v.wait(act, "bh1", turn)
        f(self.Vp[:, :, :], self.narrow(5), ACT.Copy, "Vp")
        evac(1)
        p.wait(act, "KtT", turn)
        f(self.KB[:, 0], self.full(5), ACT.Copy, "Kt")
        p.wait(act, "BtT", turn)
        f(self.KB[:, 1], self.full(0), ACT.Copy, "Bt")
        if hi_turn is not None:
            self.pj.make_hi(act, hi_turn, 1 - par)
        p.wait(act, "N2", turn)
        f(self.R[3][:, :, :], self.full(1), ACT.Copy, "N2")
        p.wait(act, "L4", turn)
        f(self.R[1][:, :, :], self.full(4), ACT.Copy, "L4")
        evac(2)
        p.wait(act, "yt", turn)
        f(self.R[5][:, :, :], self.full(1), ACT.Copy, "yt")
        p.wait(act, "Y2T", turn)
        f(self.R[0][:, :, :], self.full(2), ACT.Copy, "Y2T")
        if ahead:
            self.scalar_front(act, turn + 1)
        p.wait(act, "Y4T", turn)
        f(self.R[4][:, :, :], self.full(5), ACT.Copy, "Y4T")
        p.wait(act, "RH", turn)
        f(self.RH, self.narrow(1), ACT.Copy, "RH")
        p.wait(act, "R2", turn)
        f(self.R2, self.narrow(2), ACT.Copy, "R2")
        evac(3)
        p.wait(act, "SA", turn)
        f(self.SA, self.narrow(3), ACT.Copy, "SA")
        v.wait(act, "oc", turn)
        f(self.osq[:, :, :], self.oc[:, :, :], ACT.Square, "osq")
        evac(4)

    def pool_chunk(self, pool, turn, par, lo_turn, ahead=True):
        k = self.k
        v, a, g, p = self.dve_s, self.act_s, self.pool_s, self.pe_s

        def tt(out, x, y, o, name):
            g.done(pool.tensor_tensor(out, x, y, o), name)
        self.pool_f.wait(pool, "kk", turn)
        p.wait(pool, "R2", turn - 1)
        tt(self.sq[:, :, :], self.kk[:, :, :], self.kk[:, :, :], ALU.mult, "sq")
        p.wait(pool, "OT", turn - 1)
        for h in range(2):
            rows = slice(64 * h, 64 * h + 64)
            g.wait(pool, ("sq", "v0")[h], turn)
            tt(self.vw[rows, :, rows], self.xs[rows, 8:12, :], bc(k.one[rows, :].broadcast_to([64, NP]), C), ALU.mult, f"v{h}")
        v.wait(pool, "k2", turn)
        g.wait(pool, "v1", turn)
        tt(self.rk, self.xs[:, 0:4, :], self.t, ALU.mult, "rk")
        g.wait(pool, "rk", turn)
        tt(self.rk, self.rk, self.cv("r_k", 4), ALU.mult, "rkk")
        v.wait(pool, "Nd", turn)
        p.wait(pool, "SA", turn - 1)
        tt(self.R[5][:, :, :], self.R[0][:, :, :], bcm(k.ident[:, :], NP), ALU.add, "X1")
        if ahead:
            self.pool_front(pool, turn + 1)
        v.wait(pool, "y", turn)
        p.wait(pool, "yt", turn)
        tt(self.R[2][:, :, :], self.R[4][:, :, :], bcm(k.ident[:, :], NP), ALU.add, "Q1")
        if lo_turn is not None:
            self.pj.make_lo(pool, lo_turn, 1 - par)
        v.wait(pool, "varm", turn)
        tt(self.stat[:, 1, :], self.stat[:, 1, :], k.half_power[:, 0:1].broadcast_to([P, NP]), ALU.pow, "rstd")

    def tensor_chunk(self, pe, turn, fill):
        k, R = self.k, self.R
        v, a, g, p = self.dve_s, self.act_s, self.pool_s, self.pe_s

        def wide(bank, lhs, rhs, name):
            for j in range(NP):
                mm = pe.matmul(self.bank[bank][:, j * P:(j + 1) * P], lhs[:, j, :], rhs[:, j, :], start=True, stop=True)
            p.done(mm, name)

        def packed(bank, terms, name):
            for j in range(NP):
                for n, (lhs, rhs) in enumerate(terms):
                    mm = pe.matmul(self.bank[bank][:, j * C:(j + 1) * C], lhs[:, j, :], rhs[:, j, :],
                                   start=(n == 0), stop=(n == len(terms) - 1))
            p.done(mm, name)
        self.act_f.wait(pe, "xa", turn)
        v.wait(pe, "Q3", turn - 1)
        for j in range(NP):
            mm = pe.matmul(self.bank[0][:, j * P:(j + 1) * P], k.wa_up[:, j * P:(j + 1) * P],
                           self.th[:, 0:2, :].rearrange("p w t -> p (w t)"), start=True, stop=True)
        p.done(mm, "wa")
        self.dve_f.wait(pe, "sg", turn)
        for j in range(NP):
            mm = pe.matmul(self.bank[1][:, j * C:(j + 1) * C], k.g_up[:, j * P:(j + 1) * P], self.th[:, 2, :],
                           start=True, stop=True)
        p.done(mm, "g")
        fill(14)
        g.wait(pe, "sq", turn)
        p.done(pe.matmul(self.narrow(2), k.pair[:, :], self.sq,
                         start=True, stop=True), "ss")
        fill(20)
        g.wait(pe, "v1", turn)
        v.wait(pe, "Sa", turn - 1)
        for j in range(NP):
            mm = pe.matmul(self.bank[5][:, j * C:(j + 1) * C], self.vw[:, j, :], k.ii[:, :], start=True, stop=True)
        p.done(mm, "V")
        g.wait(pe, "rkk", turn)
        v.wait(pe, "yg", turn - 1)
        p.done(pe.matmul(self.narrow(3), k.pair[:, :], self.rk,
                         start=True, stop=True), "bon")
        fill(16)
        v.wait(pe, "bh1", turn)
        a.wait(pe, "g", turn)
        for j in range(NP):
            mm = pe.matmul(self.two[0][:, j * 256:(j + 1) * 256], self.KB[:, 1, j, :],
                           self.KR[:, j, :, :].rearrange("p w t -> p (w t)"), start=True, stop=True)
        p.done(mm, "gb")
        v.wait(pe, "bv", turn)
        for j in range(NP):
            mm = pe.matmul(self.two[1][:, j * 256:(j + 1) * 256], self.KB[:, 0, j, :],
                           self.KR[:, j, :, :].rearrange("p w t -> p (w t)"), start=True, stop=True)
        p.done(mm, "gk")
        v.wait(pe, "oc", turn - 1)
        wide(4, self.KR[:, :, 0, :], self.KB[:, 1], "gl")
        a.wait(pe, "Vp", turn)
        for j in range(NP):
            mm = pe.transpose(self.bank[5][:, j * P:(j + 1) * P], self.KB[:, 0, j, :], k.ident[:, :])
        p.done(mm, "KtT")
        v.wait(pe, "Mb", turn)
        for j in range(NP):
            mm = pe.transpose(self.bank[0][:, j * P:(j + 1) * P], self.KB[:, 1, j, :], k.ident[:, :])
        p.done(mm, "BtT")
        fill(12)
        v.wait(pe, "Lo", turn)
        wide(1, R[1], R[0], "N2")
        wide(2, R[0], R[1], "L2")
        fill(5)
        v.wait(pe, "L2", turn)
        g.wait(pe, "X1", turn)
        wide(3, R[4], R[5], "X2")
        a.wait(pe, "N2", turn)
        wide(4, R[3], R[4], "L4")
        fill(5)
        a.wait(pe, "L4", turn)
        v.wait(pe, "X2", turn)
        wide(5, R[1], R[0], "X3")
        fill(5)
        v.wait(pe, "X3", turn)
        wide(0, R[2], R[3], "y")
        wide(1, R[3], R[2], "yt")
        fill(5)
        v.wait(pe, "y", turn)
        a.wait(pe, "yt", turn)
        wide(2, R[4], R[5], "Y2T")
        wide(3, R[5], R[4], "Y2")
        fill(5)
        a.wait(pe, "Y2T", turn)
        g.wait(pe, "Q1", turn)
        wide(4, R[0], R[2], "Q2")
        v.wait(pe, "Y2", turn)
        wide(5, R[1], R[0], "Y4T")
        fill(5)
        a.wait(pe, "Y4T", turn)
        v.wait(pe, "Q2", turn)
        wide(0, R[4], R[5], "Q3")
        v.wait(pe, "S", turn - 1)
        packed(1, [(self.KR[:, :, 0, :], self.S), (self.Lk, self.Vp)], "RH")
        fill(3)
        a.wait(pe, "RH", turn)
        packed(2, [(R[3], self.RH)], "R2")
        fill(3)
        a.wait(pe, "R2", turn)
        v.wait(pe, "Q3", turn)
        packed(3, [(R[0], self.R2)], "SA")
        fill(2)
        a.wait(pe, "SA", turn)
        packed(4, [(self.KR[:, :, 1, :], self.S), (self.Mb, self.SA), (self.Mk, self.Vp)], "O")
        packed(5, [(self.KB[:, 0], self.Vp), (self.KB[:, 1], self.SA)], "S")
        fill(20)
        v.wait(pe, "on1", turn)
        for j in range(NP):
            mm = pe.matmul(self.bank[3][:, j * C:(j + 1) * C], self.vw[:, j, :], k.ii[:, :], start=True, stop=True)
        p.done(mm, "OT")


def build_rwkv(nc, k, pj):
    FILLED = IN_T - RT
    LOOPED = 26
    with ExitStack() as ctx:
        w = Rwkv(ctx, nc, k, pj)
        with nc.Block() as block:
            @block.gpsimd
            def _(pool):
                w.pool_s.open(pool)
                w.pool_f.open(pool)
                for buf in (w.KR, w.KB, w.vw, w.S):
                    pool.memset(buf[:], 0.0)
                pool.memset(w.praw[:, :, 0:1], 0.0)
                pool.memset(w.th[:, 0:2, :], 0.0)
                pool.memset(w.W[:, :, 0:1], 1.0)

            @block.vector
            def _(dve):
                w.dve_s.open(dve)
                w.dve_f.open(dve)
                dve.sem_inc(w.y_stored, 16)

            @block.scalar
            def _(act):
                w.act_s.open(act)
                w.act_f.open(act)

            @block.tensor
            def _(pe):
                w.pe_s.open(pe)

        def each_chunk(eng, body):
            with eng.Fori(0, LOOPED // 2) as i:
                for par in range(2):
                    body(2 * i + par, par)
            for c in range(LOOPED, NCH):
                body(c, c % 2)

        def filled(c):
            return not isinstance(c, int) or c < FILLED

        def ahead(c):
            return not isinstance(c, int) or c + 1 < NCH

        def preloads(c):
            return not isinstance(c, int) or c < FILLED - 1

        with nc.Block() as block:
            @block.sync
            def _(sp):
                w.sync_chunk(sp, 1, slice(0, C))

                def body(c, par):
                    if preloads(c):
                        pj.load(sp, c + RT + 3)
                    if ahead(c):
                        w.sync_chunk(sp, c + 2, ds((c + 1) * C, C))
                    w.store_chunk(sp, c + 1, ds(c * C, C))
                each_chunk(sp, body)
                sp.wait_ge(w.y_stored, 16 * (NCH + 1))

            @block.scalar
            def _(act):
                def body(c, par):
                    def evac(b):
                        if filled(c):
                            pj.evacuate(act, c + RT + 2, par, b)
                    w.scalar_chunk(act, c + 1, par, evac, c + RT + 3 if preloads(c) else None, ahead(c))
                w.scalar_front(act, 1)
                each_chunk(act, body)
                pj.wait_stored(act, IN_T)

            @block.vector
            def _(dve):
                w.vector_front(dve, 1)
                each_chunk(dve, lambda c, par: w.vector_chunk(dve, c + 1, par, ahead=ahead(c)))

            @block.gpsimd
            def _(pool):
                w.pool_front(pool, 1)
                each_chunk(pool, lambda c, par: w.pool_chunk(pool, c + 1, par, c + RT + 3 if preloads(c) else None, ahead(c)))

            @block.tensor
            def _(pe):
                def body(c, par):
                    products = pj.products(pe, c + RT + 2, par) if filled(c) else iter(())

                    def fill(n):
                        for _i in range(n):
                            if next(products, 0) == 0:
                                break
                    w.tensor_chunk(pe, c + 1, fill)
                    for _rest in products:
                        pass
                each_chunk(pe, body)

        turn_state(nc, k, w, out=k.p_wkv, shift=k.p_shift, last=C, load=True)
        T = NCH + 1
        with nc.Block() as block:
            @block.sync
            def _(sp):
                sp.dma_start(w.praw[:, :, 1:DEC + 1], k.proj[0:R_PROJ, SEQ:NT].rearrange("(r p) t -> p r t", p=P))\
                    .then_inc(w.rows_loaded, 16)
                w.store_chunk(sp, T, slice(SEQ, NT), DEC)
                sp.wait_ge(w.y_stored, 16 * (NCH + 2))

            @block.scalar
            def _(act):
                w.scalar_front(act, T)
                w.scalar_chunk(act, T, 0, lambda b: None, None, ahead=False)

            @block.vector
            def _(dve):
                w.vector_front(dve, T)
                w.vector_chunk(dve, T, 0, sample=True, ahead=False)

            @block.gpsimd
            def _(pool):
                w.pool_front(pool, T, DEC)
                w.pool_chunk(pool, T, 0, None, ahead=False)

            @block.tensor
            def _(pe):
                w.tensor_chunk(pe, T, lambda n: None)
        turn_state(nc, k, w, out=k.s_wkv, shift=k.s_shift, last=DEC, load=False)


def turn_state(nc, k, w, out, shift, last, load):
    tag = "p" if load else "s"
    with ExitStack() as ctx:
        done = ctx.enter_context(nc.semaphore(f"state_turned_{tag}"))
        kept = ctx.enter_context(nc.semaphore(f"state_kept_{tag}"))
        stored = ctx.enter_context(nc.semaphore(f"state_stored_{tag}"))
        loaded = ctx.enter_context(nc.semaphore(f"state_loaded_{tag}"))
        vk = w.R[1][0:64, :, :]
        vk_in = w.R[2][0:64, :, :]
        with nc.Block() as block:
            @block.tensor
            def _(pe):
                for j in range(NP):
                    mm = pe.transpose(w.bank[0][0:64, j * P:(j + 1) * P], w.S[:, j, :], k.ident[:, :])
                mm.then_inc(done, 1)
                if load:
                    pe.wait_ge(loaded, 16)
                    for j in range(NP):
                        mm = pe.transpose(w.bank[1][:, j * C:(j + 1) * C], vk_in[:, j, :], k.ident[0:64, 0:64])
                    mm.then_inc(done, 1)

            @block.vector
            def _(dve):
                dve.wait_ge(done, 1)
                dve.tensor_copy(vk, w.full(0)[0:64]).then_inc(kept, 1)
                if load:
                    dve.wait_ge(done, 2)
                    dve.tensor_copy(w.S[:, :, :], w.narrow(1)).then_inc(kept, 1)

            @block.sync
            def _(sp):
                if load:
                    sp.dma_start(vk_in.rearrange("v j (h k) -> v (j h) k", k=HD), k.s_in.rearrange("h v k -> v h k")).then_inc(loaded, 16)
                col = last
                sp.dma_start(shift.rearrange("(r p) -> p r", p=P), w.praw[:, :, col],
                             allow_slow_non_contiguous=True).then_inc(stored, 16)
                sp.wait_ge(kept, 1)
                sp.dma_start(out.rearrange("h v k -> v h k"), vk.rearrange("v j (h k) -> v (j h) k", k=HD)).then_inc(stored, 16)
                sp.wait_ge(stored, 32)

            @block.gpsimd
            def _(pool):
                if load:
                    pool.wait_ge(stored, 32)
                    pool.tensor_copy(w.praw[:, :, 0:1], k.cvec[:, 2 * KD:2 * KD + RT].unsqueeze(2))
                    pool.memset(w.praw[:, :, DEC + 1:C + 1], 0.0)
                    pool.memset(w.xs[:, :, DEC:C], 0.0)
                    pool.memset(w.z[:, :, DEC:C], 0.0)


QW, KT5 = P, BAND // P
NQ = SEQ // P
SKEYS = PAST + DEC


def build_attention(nc, k):
    with ExitStack() as ctx:
        def sb(name, shape):
            return ctx.enter_context(nc.sbuf_tensor(name, shape, F32))
        a = Tensors()
        a.qT, a.kT = sb("qT", [P, NP, NT]), sb("kT", [P, NP, NT])
        a.V = sb("v_rows", [P, NQ + 1, DR])
        a.bias = sb("bias", [P, NH, BAND])
        a.sbias = sb("sample_bias", [DEC, NH, SKEYS])
        a.bias_ready = ctx.enter_context(nc.semaphore("bias_ready"))
        a.rows_ready = ctx.enter_context(nc.semaphore("v_rows_ready"))
        build_attention_inputs(nc, k, a)
        build_attention_core(nc, k, a)


def build_attention_inputs(nc, k, a):
    KEEP0 = (SEQ - WIN) // P
    NV = 4
    with ExitStack() as ctx:
        vT = ctx.enter_context(nc.sbuf_tensor("vT", [P, NV, NP, P], F32))
        krow = ctx.enter_context(nc.sbuf_tensor("k_rows", [P, 2, DR], F32))
        pv = [ctx.enter_context(nc.psum_tensor(f"v_ps{i}", [P, 512], F32)) for i in range(2)]
        pk = [ctx.enter_context(nc.psum_tensor(f"k_ps{i}", [P, 512], F32)) for i in range(2)]
        qk_loaded = ctx.enter_context(nc.semaphore("qk_loaded"))
        v_loaded = [ctx.enter_context(nc.semaphore(f"v_loaded{i}")) for i in range(NV)]
        turned = ctx.enter_context(nc.semaphore("v_turned"))
        kept = ctx.enter_context(nc.semaphore("v_kept"))
        k_turned = ctx.enter_context(nc.semaphore("k_turned"))
        k_kept = ctx.enter_context(nc.semaphore("k_kept"))
        k_stored = [ctx.enter_context(nc.semaphore(f"k_stored{i}")) for i in range(2)]
        v_stored = ctx.enter_context(nc.semaphore("v_stored"))
        tab = ctx.enter_context(nc.sbuf_tensor("table", [NH, 2 * REL + 1], F32))
        ext = ctx.enter_context(nc.sbuf_tensor("distances", [NH, EXT], F32))
        rev = ctx.enter_context(nc.sbuf_tensor("bias_backwards", [P, 4, BAND], F32))
        srev = ctx.enter_context(nc.sbuf_tensor("sample_bias_backwards", [DEC, NH, SKEYS], F32))
        tab_loaded = ctx.enter_context(nc.semaphore("table_loaded"))
        made = ctx.enter_context(nc.semaphore("distances_made"))
        written = ctx.enter_context(nc.semaphore("distances_written"))
        back = [ctx.enter_context(nc.semaphore(f"bias_loaded{i}")) for i in range(4)]
        sback = ctx.enter_context(nc.semaphore("sample_bias_loaded"))
        bias_turned = ctx.enter_context(nc.semaphore("bias_turned"))
        rows = k.proj.rearrange("(r p) t -> p r t", p=P)
        kept_tiles = [j for j in range(KEEP0, NQ + 1)]

        def size(j):
            return P if j < NQ else DEC
        with nc.Block() as block:
            @block.sync
            def _(sp):
                for j in range(NQ + 1):
                    if j >= NV:
                        sp.wait_ge(turned, j - NV + 1)
                    sp.dma_start(vT[:, j % NV, :, 0:size(j)], rows[:, VT:VT + NP, j * P:j * P + size(j)]).then_inc(v_loaded[j % NV], 16)
                    if j == NV - 1:
                        sp.dma_start(a.kT[:, :, :], rows[:, KT_:KT_ + NP, :]).then_inc(qk_loaded, 16)
                        sp.dma_start(a.qT[:, :, :], rows[:, QT:QT + NP, :]).then_inc(qk_loaded, 16)
                sp.wait_ge(kept, NQ + 1)
                sp.dma_start(k.p_v.rearrange("(j p) h d -> p j (h d)", p=P), a.V[:, KEEP0:NQ, :]).then_inc(v_stored, 16)
                sp.dma_start(k.s_v.rearrange("p h d -> p (h d)"), a.V[0:DEC, NQ, :]).then_inc(v_stored, 16)
                sp.wait_ge(v_stored, 32)
                sp.wait_ge(qk_loaded, 32)

            @block.tensor
            def _(pe):
                for j in range(NQ + 1):
                    pe.wait_ge(v_loaded[j % NV], 16 * (j // NV + 1))
                    if j >= 2:
                        pe.wait_ge(kept, j - 1)
                    for i in range(NP):
                        mm = pe.transpose(pv[j % 2][0:size(j), i * P:(i + 1) * P], vT[:, j % NV, i, 0:size(j)], k.ident[:, :])
                    mm.then_inc(turned, 1)
                pe.wait_ge(qk_loaded, 32)
                for n, j in enumerate(kept_tiles):
                    if n >= 2:
                        pe.wait_ge(k_kept, n - 1)
                    for i in range(NP):
                        mm = pe.transpose(pk[n % 2][0:size(j), i * P:(i + 1) * P], a.kT[:, i, j * P:j * P + size(j)], k.ident[:, :])
                    mm.then_inc(k_turned, 1)

            @block.vector
            def _(dve):
                dve.wait_ge(tab_loaded, 16)
                near = REL + P - 1
                dve.tensor_copy(ext[:, 0:near], tab[:, 1:near + 1]).then_inc(made, 1)
                dve.tensor_copy(ext[:, near:EXT], tab[:, 2 * REL:2 * REL + 1].broadcast_to([NH, EXT - near])).then_inc(made, 1)
                for j in range(NQ + 1):
                    dve.wait_ge(turned, j + 1)
                    dve.tensor_copy(a.V[0:size(j), j, :], pv[j % 2][0:size(j), :]).then_inc(kept, 1)
                    if j % 2 == 1:
                        h = j // 2
                        dve.wait_ge(back[h % 4], 16 * (h // 4 + 1))
                        dve.tensor_copy(a.bias[:, h, :], rev[:, h % 4, ::-1]).then_inc(bias_turned, 1)
                dve.wait_ge(bias_turned, NH)
                dve.memset(a.bias[0:64, :, BAND - 64:BAND], NEG)
                dve.memset(a.bias[64:128, :, 0:64], NEG)
                dve.wait_ge(sback, 16)
                dve.tensor_copy(a.sbias[:, :, :], srev[:, :, ::-1]).then_inc(a.bias_ready, 1)
                dve.wait_ge(kept, NQ + 1)
                dve.sem_inc(a.rows_ready, 1)

            @block.scalar
            def _(act):
                act.dma_start(tab[:, :], k.rel_table).then_inc(tab_loaded, 16)
                act.wait_ge(made, 2)
                act.dma_start(k.ext, ext[:, :]).then_inc(written, 16)
                act.wait_ge(written, 16)
                for h in range(NH):
                    if h >= 4:
                        act.wait_ge(bias_turned, h - 3)
                    act.dma_start(rev[:, h % 4, :], bass.AP(tensor=k.ext.tensor, offset=h * EXT, ap=[[1, P], [1, BAND]])).then_inc(back[h % 4], 16)
                act.dma_start(srev[:, :, :], bass.AP(tensor=k.ext.tensor, offset=96, ap=[[1, DEC], [EXT, NH], [1, SKEYS]])).then_inc(sback, 16)
                for n, j in enumerate(kept_tiles):
                    act.wait_ge(k_turned, n + 1)
                    if n >= 2:
                        act.wait_ge(k_stored[n % 2], 16 * (n // 2))
                    act.activation(krow[0:size(j), n % 2, :], pk[n % 2][0:size(j), :], ACT.Copy).then_inc(k_kept, 1)
                    act.wait_ge(k_kept, n + 1)
                    dst = k.p_k[(j - KEEP0) * P:(j - KEEP0 + 1) * P] if j < NQ else k.s_k
                    act.dma_start(dst.rearrange("p h d -> p (h d)"), krow[0:size(j), n % 2, :]).then_inc(k_stored[n % 2], 16)
                act.wait_ge(k_stored[0], 16 * 3)
                act.wait_ge(k_stored[1], 16 * 2)


class Heads:

    def __init__(self, ctx, nc, k, a):
        self.k, self.a = k, a

        def sb(name, shape):
            return ctx.enter_context(nc.sbuf_tensor(name, shape, F32))
        self.q = sb("q_tile", [P, NP, P])
        self.K = sb("k_window", [P, NP, BAND])
        self.Vw = sb("v_window", [P, KT5, DR])
        self.s = sb("scores", [P, 2, BAND])
        self.e = sb("probs", [P, 2, BAND])
        self.eT = sb("probs_turned", [P, 2, BAND])
        self.nmax, self.sum, self.rec = sb("minus_max", [P, NH]), sb("prob_sums", [P, NH]), sb("prob_recips", [P, NH])
        self.idle = sb("idle", [P, 2, NH])
        self.yT = sb("att_turned", [P, NP, P])
        self.ps_s = [ctx.enter_context(nc.psum_tensor(f"scores_ps{j}", [P, 1024], F32)) for j in range(2)]
        self.ps_t = ctx.enter_context(nc.psum_tensor("probs_ps", [P, 2, 512], F32))
        self.ps_y = [ctx.enter_context(nc.psum_tensor(f"att_ps{j}", [P, NP, P], F32)) for j in range(2)]
        self.stored = ctx.enter_context(nc.semaphore("ya_stored"))
        order = [("s", 0), ("s", 1), ("n", 0)]
        for h in range(NH):
            order += [("t", h)] + [("n", h + 1)] * (h + 1 < NH) + [("s", h + 2)] * (h + 2 < NH)
        dve = [x for s, h in order for x in ([("r", h)] if s == "n" else []) + [(s, h)]]
        self.keys_s, self.queries_s = Steps(ctx, nc, "att_keys", ["K"]), Steps(ctx, nc, "att_queries", ["q"])
        self.dve_s = Steps(ctx, nc, "att_dve", ["V"] + dve)
        self.act_s = Steps(ctx, nc, "att_act", [("e" if s == "s" else "t", h) for s, h in order if s != "n"] + ["yT0", "yT1"])
        pe = [("s", 0), ("s", 1)]
        for h in range(NH):
            pe += [("t", h)] + [("s", h + 2)] * (h + 2 < NH) + [("y", h)]
        self.pe_s = Steps(ctx, nc, "att_pe", pe)
        self.order = order

    @staticmethod
    def tiles(c0, c1):
        return [(c, min(P, c1 - c)) for c in range(c0, c1, P)]

    def vector_tile(self, dve, turn, take_values, nq, c0, c1, bias, take_next_keys):
        v, a, p = self.dve_s, self.act_s, self.pe_s
        p.wait(dve, ("y", NH - 1), turn - 1)
        take_values()
        for s, h in self.order:
            if s == "s":
                a.wait(dve, ("e", h - 2), turn) if h >= 2 else a.wait(dve, ("e", h + NH - 2), turn - 1)
                p.wait(dve, ("s", h), turn)
                dve.memset(self.idle[:, 0, h:h + 1], 0.0)
                v.done(dve.tensor_tensor_reduce(self.s[0:nq, h % 2, c0:c1], self.ps_s[h % 2][0:nq, c0:c1], bias(h), -1.0, 3.0e38,
                                                ALU.add, ALU.min, self.nmax[0:nq, h:h + 1]), (s, h))
                if h == NH - 1:
                    take_next_keys()
            elif s == "n":
                a.wait(dve, ("e", h), turn)
                v.done(dve.reciprocal(self.rec[0:nq, h:h + 1], self.sum[0:nq, h:h + 1]), ("r", h))
                v.wait(dve, ("r", h), turn)
                e = self.e[0:nq, h % 2, c0:c1]
                v.done(dve.tensor_scalar(e, e, self.rec[0:nq, h:h + 1], None, ALU.mult), (s, h))
            else:
                p.wait(dve, ("t", h), turn)
                ins = self.take_turned(dve.tensor_copy, 0, h, nq, c0, c1)
                if ins is None:
                    ins = dve.memset(self.idle[:, 1, h:h + 1], 0.0)
                v.done(ins, (s, h))

    def take_turned(self, copy, part, h, nq, c0, c1):
        first, full, last = c0 // P, c1 // P, (c1 + P - 1) // P
        ins = None
        for n, t0, t1 in ((P, first, full), (c1 - full * P, full, last)):
            t0, t1 = max(t0, 2 * part), min(t1, (2, KT5)[part])
            if t1 > t0:
                out = self.eT[0:n, h % 2, t0 * P:t1 * P].rearrange("p (c t) -> p c t", t=P)[:, :, 0:nq]
                src = self.ps_t[0:n, part, (t0 - 2 * part) * P:(t1 - 2 * part) * P].rearrange("p (c t) -> p c t", t=P)[:, :, 0:nq]
                ins = copy(out, src)
        return ins

    def take_queries(self, act, turn, cols, nq):
        self.pe_s.wait(act, ("s", NH - 1), turn - 1)
        self.queries_s.done(act.activation(self.q[:, :, 0:nq], self.a.qT[:, :, cols], ACT.Copy, scale=HD ** -0.5), "q")

    def scalar_tile(self, act, turn, nq, c0, c1, out_cols, take_next_queries):
        v, a, p = self.dve_s, self.act_s, self.pe_s
        for s, h in self.order:
            if s == "n":
                continue
            if s == "s":
                v.wait(act, ("s", h), turn)
                p.wait(act, ("t", h - 2), turn) if h >= 2 else p.wait(act, ("t", h + NH - 2), turn - 1)
                a.done(act.activation(self.e[0:nq, h % 2, c0:c1], self.s[0:nq, h % 2, c0:c1], ACT.Exp, bias=self.nmax[0:nq, h:h + 1],
                                      scale=-1.0, accum_out=self.sum[0:nq, h:h + 1]), ("e", h))
                if h == NH - 1:
                    take_next_queries()
            else:
                p.wait(act, ("t", h), turn)
                a.done(self.take_turned(lambda out, x: act.activation(out, x, ACT.Copy), 1, h, nq, c0, c1), (s, h))
        p.wait(act, ("y", NH - 1), turn)
        act.wait_ge(self.stored, 16 * (turn - 1))
        for j in range(2):
            rows = slice(64 * j, 64 * j + 64)
            a.done(act.activation(self.yT[rows, :, 0:nq], self.ps_y[j][rows, :, 0:nq], ACT.Copy), f"yT{j}")
        a.wait(act, "yT1", turn)
        act.dma_start(self.k.yaT.rearrange("(a p) t -> p a t", p=P)[:, :, out_cols], self.yT[:, :, 0:nq]).then_inc(self.stored, 16)

    def tensor_tile(self, pe, turn, nq, c0, c1):
        v, a, p = self.dve_s, self.act_s, self.pe_s

        def scores(h):
            if h == 0:
                self.keys_s.wait(pe, "K", turn)
                self.queries_s.wait(pe, "q", turn)
            v.wait(pe, ("s", h - 2), turn) if h >= 2 else v.wait(pe, ("s", h + NH - 2), turn - 1)
            rows = slice(64 * (h % 2), 64 * (h % 2) + 64)
            for x0, x1 in ((c0, min(c1, 512)), (512, c1)):
                if x1 > x0:
                    mm = pe.matmul(self.ps_s[h % 2][0:nq, x0:x1], self.q[rows, h // 2, 0:nq], self.K[rows, h // 2, x0:x1],
                                   start=True, stop=True)
            p.done(mm, ("s", h))
        scores(0)
        scores(1)
        for h in range(NH):
            v.wait(pe, ("n", h), turn)
            v.wait(pe, ("t", h - 1), turn) if h else v.wait(pe, ("t", NH - 1), turn - 1)
            a.wait(pe, ("t", h - 1), turn) if h else a.wait(pe, ("t", NH - 1), turn - 1)
            for c, n in self.tiles(c0, c1):
                mm = pe.transpose(self.ps_t[0:n, c // (2 * P) if c < 2 * P else 1, (c % (2 * P) if c < 2 * P else c - 2 * P):][:, 0:nq], self.e[0:nq, h % 2, c:c + n], self.k.ident[0:nq, 0:nq])
            p.done(mm, ("t", h))
            if h + 2 < NH:
                scores(h + 2)
            v.wait(pe, ("t", h), turn)
            a.wait(pe, ("t", h), turn)
            if h == 0:
                v.wait(pe, "V", turn)
                a.wait(pe, "yT1", turn - 1)
            tl = self.tiles(c0, c1)
            for i, (c, n) in enumerate(tl):
                mm = pe.matmul(self.ps_y[h % 2][:, h // 2, 0:nq], self.Vw[0:n, c // P, (h // 2) * P:(h // 2 + 1) * P], self.eT[0:n, h % 2, c:c + nq],
                               start=(i == 0), stop=(i == len(tl) - 1))
            p.done(mm, ("y", h))


def build_attention_core(nc, k, a):
    with ExitStack() as ctx:
        w = Heads(ctx, nc, k, a)
        ck = ctx.enter_context(nc.sbuf_tensor("cache_k_rows", [P, PAST // P, DR], F32))
        cache_loaded = ctx.enter_context(nc.semaphore("cache_loaded"))
        FULL = KT5 - 1

        def each_tile(eng, body):
            for t in range(FULL):
                body(t)
            with eng.Fori(FULL, NQ - 1) as t:
                body(t)
            body(NQ - 1)

        def first_col(t):
            return max(FULL - t, 0) * P if isinstance(t, int) else 0

        def nothing():
            pass

        def keys(t, c0):
            return ds((t - FULL) * P + c0, BAND - c0)
        with nc.Block() as block:
            @block.vector
            def _(dve):
                w.dve_s.open(dve)
                w.keys_s.open(dve)
                dve.wait_ge(a.bias_ready, 1)
                dve.wait_ge(a.rows_ready, 1)

                def take_keys(t):
                    c0 = first_col(t)
                    w.pe_s.wait(dve, ("s", NH - 1), t)
                    w.keys_s.done(dve.tensor_copy(w.K[:, :, c0:BAND], a.kT[:, :, keys(t, c0)]), "K")

                def body(t):
                    c0 = first_col(t)

                    def take_values():
                        src = a.V[:, ds(t - FULL + c0 // P, KT5 - c0 // P), :]
                        w.dve_s.done(dve.tensor_copy(w.Vw[:, c0 // P:KT5, :], src), "V")
                    last = isinstance(t, int) and t == NQ - 1
                    w.vector_tile(dve, t + 1, take_values, P, c0, BAND, lambda h: a.bias[:, h, c0:BAND],
                                  nothing if last else lambda: take_keys(t + 1))
                take_keys(0)
                each_tile(dve, body)

            @block.scalar
            def _(act):
                w.act_s.open(act)
                w.queries_s.open(act)

                def take_queries(t):
                    w.take_queries(act, t + 1, ds(t * P, P), P)

                def body(t):
                    last = isinstance(t, int) and t == NQ - 1
                    w.scalar_tile(act, t + 1, P, first_col(t), BAND, ds(t * P, P), nothing if last else lambda: take_queries(t + 1))
                take_queries(0)
                each_tile(act, body)
                act.wait_ge(w.stored, 16 * NQ)

            @block.tensor
            def _(pe):
                w.pe_s.open(pe)
                each_tile(pe, lambda t: w.tensor_tile(pe, t + 1, P, first_col(t), BAND))

        T = NQ + 1
        with nc.Block() as block:
            turned = ctx.enter_context(nc.semaphore("cache_turned"))

            @block.sync
            def _(sp):
                sp.dma_start(ck[:, :, :], k.cache_k.rearrange("(c p) h d -> p c (h d)", p=P)).then_inc(cache_loaded, 16)
                sp.dma_start(w.Vw[:, 0:2, :], k.cache_v.rearrange("(c p) h d -> p c (h d)", p=P)).then_inc(cache_loaded, 16)
                sp.wait_ge(cache_loaded, 32)

            @block.tensor
            def _(pe):
                pe.wait_ge(cache_loaded, 32)
                for c in range(2):
                    for j in range(NP):
                        mm = pe.transpose(w.ps_s[c][:, j * P:(j + 1) * P], ck[:, c, j * P:(j + 1) * P], k.ident[:, :])
                mm.then_inc(turned, 1)
                w.tensor_tile(pe, T, DEC, 0, SKEYS)

            @block.vector
            def _(dve):
                dve.wait_ge(turned, 1)
                for c in range(2):
                    dve.tensor_copy(w.K[:, :, c * P:(c + 1) * P], w.ps_s[c][:, 0:512].rearrange("p (a t) -> p a t", t=P))
                w.keys_s.done(dve.tensor_copy(w.K[:, :, PAST:SKEYS], a.kT[:, :, SEQ:NT]), "K")

                def take_values():
                    w.dve_s.done(dve.tensor_copy(w.Vw[0:DEC, 2, :], a.V[0:DEC, NQ, :]), "V")
                w.vector_tile(dve, T, take_values, DEC, 0, SKEYS, lambda h: a.sbias[:, h, :], nothing)

            @block.scalar
            def _(act):
                w.take_queries(act, T, slice(SEQ, NT), DEC)
                w.scalar_tile(act, T, DEC, 0, SKEYS, slice(SEQ, NT), nothing)
                act.wait_ge(w.stored, 16 * T)


def split_products(pe, out, hi, lo, x_hi, x_lo, kts, first=True, last=True):
    n = len(kts)
    for i, kt in enumerate(kts):
        for j, (w, x) in enumerate(((hi, x_hi), (hi, x_lo), (lo, x_hi))):
            mm = pe.matmul(out, w(i), x(kt), start=(first and i == 0 and j == 0), stop=(last and i == n - 1 and j == 2))
    return mm


def build_merge(nc, k):
    with ExitStack() as ctx:
        def sb(name, shape, dt=F32):
            return ctx.enter_context(nc.sbuf_tensor(name, shape, dt))

        def sem(name):
            return ctx.enter_context(nc.semaphore(name))
        wraw = sb("merge_w_raw", [P, 2, D])
        whi, wlo = sb("merge_w_hi", [P, 16, D], F32R), sb("merge_w_lo", [P, 16, D], F32R)
        yraw = sb("y_raw", [P, 2, BW])
        yhi, ylo = sb("y_hi", [P, KD, BW], F32R), sb("y_lo", [P, KD, BW], F32R)
        mhi, mlo = sb("merged_hi", [P, KD, BW], F32R), sb("merged_lo", [P, KD, BW], F32R)
        gate = sb("gates", [P, 2, 2, BW])
        m1, m2 = sb("merged_r", [P, BW]), sb("merged_a", [P, BW])
        xt = sb("x_then_x2", [P, 2, BW])
        pr, pa, po = ([ctx.enter_context(nc.psum_tensor(f"merge_ps{n}{j}", [P, 512], F32)) for j in range(2)] for n in "rao")
        w_loaded = [sem(f"merge_w_loaded{j}") for j in range(2)]
        y_loaded = [sem(f"y_loaded{j}") for j in range(2)]
        g_loaded = [sem(f"gates_loaded{j}") for j in range(2)]
        x_loaded = [sem(f"x_in_loaded{j}") for j in range(2)]
        x2_stored = [sem(f"x2_stored{j}") for j in range(2)]
        whi_s = Steps(ctx, nc, "merge_w_hi_made", list(range(16)))
        wlo_s = Steps(ctx, nc, "merge_w_lo_made", list(range(16)))
        yhi_s = Steps(ctx, nc, "y_hi_made", list(range(8)), base=1)
        ylo_s = Steps(ctx, nc, "y_lo_made", list(range(8)), base=1)
        act_s = Steps(ctx, nc, "merge_act", [(s, m) for m in range(8) for s in ("g", "mh")])
        dve_s = Steps(ctx, nc, "merge_dve", [(s, m) for m in range(8) for s in ("m1", "m2", "ms", "ml")] + [("x", m) for m in range(8)])
        pe_s = Steps(ctx, nc, "merge_pe", [(s, m) for m in range(8) for s in ("r", "a")] + [("o", m) for m in range(8)])
        proj = k.proj.rearrange("(r p) t -> p r t", p=P)
        y_src = [k.yrT.rearrange("(a p) t -> p a t", p=P), k.yaT.rearrange("(a p) t -> p a t", p=P)]
        w_src = [w.rearrange("(a p) n -> p a n", p=P) for w in (k.w_br_r, k.w_br_a, k.w_out)]
        xT, x2T = (t.rearrange("(a p) t -> p a t", p=P) for t in (k.xT, k.x2T))

        def cols(b):
            return ds(b * BW, BW)

        def each_block(eng, body):
            body(0, 1, False)
            with eng.Fori(1, NB - 1) as b:
                body(b, b + 1, False)
            body(NB - 1, NB, True)

        def nth(turn, m):
            return 64 * (turn - 1) + 16 * (m // 2 + 1)

        with nc.Block() as block:
            @block.sync
            def _(sp):
                def load_y(b, turn, kt):
                    if isinstance(turn, int) and turn == 1 and kt < 2:
                        pass
                    else:
                        yt, yk = (turn, kt - 2) if kt >= 2 else (turn - 1, kt + 6)
                        ylo_s.wait(sp, yk, yt)
                    sp.dma_start(yraw[:, kt % 2, :], y_src[kt // 4][:, kt % 4, ds((b + 1) * BW - BW, BW)]).then_inc(y_loaded[kt % 2], 16)

                def load_w(n):
                    if n >= 2:
                        wlo_s.wait(sp, n - 2, 0)
                    src = w_src[0][:, n, :] if n < 4 else w_src[1][:, n - 4, :] if n < 8 else w_src[2][:, n - 8, :]
                    sp.dma_start(wraw[:, n % 2, :], src).then_inc(w_loaded[n % 2], 16)
                for n in range(8):
                    load_y(0, 1, n)
                    load_w(n)

                def body(b, turn, last):
                    for m in range(8):
                        dve_s.wait(sp, ("m2", m - 2), turn) if m >= 2 else dve_s.wait(sp, ("m2", m + 6), turn - 1)
                        for half in range(2):
                            ins = sp.dma_start(gate[:, m % 2, half, :], proj[:, GT + 8 * half + m, cols(b)])
                            ins.then_inc(g_loaded[m % 2], 16)
                        if isinstance(turn, int) and turn == 1:
                            load_w(8 + m)
                    for m in range(8):
                        sp.wait_ge(x2_stored[m % 2], nth(turn, m) - 16)
                        sp.dma_start(xt[:, m % 2, :], xT[:, m, ds(turn * BW - BW, BW)]).then_inc(x_loaded[m % 2], 16)
                        if not last:
                            if m == 0:
                                pe_s.wait(sp, ("a", 7), turn)
                            load_y(b + 1, turn + 1, m)

                each_block(sp, body)

            def y_split_hi(act, turn, kt):
                act.wait_ge(y_loaded[kt % 2], nth(turn, kt))
                yhi_s.done(act.activation(yhi[:, kt, :], yraw[:, kt % 2, :], ACT.Copy), kt)

            def w_hi(act, n):
                act.wait_ge(w_loaded[n % 2], 16 * (n // 2 + 1))
                whi_s.done(act.activation(whi[:, n, :], wraw[:, n % 2, :], ACT.Copy), n)

            @block.scalar
            def _(act):
                act_s.open(act)
                for n in range(8):
                    y_split_hi(act, 1, n)
                    w_hi(act, n)

                def body(b, turn, last):
                    for m in range(8):
                        act.wait_ge(g_loaded[m % 2], 2 * nth(turn, m))
                        act_s.done(act.activation(gate[:, m % 2], gate[:, m % 2], ACT.Tanh, scale=0.5), ("g", m))
                        if isinstance(turn, int) and turn == 1:
                            w_hi(act, 8 + m)
                        dve_s.wait(act, ("ms", m), turn)
                        pe_s.wait(act, ("o", 7), turn - 1)
                        act_s.done(act.activation(mhi[:, m, :], m1[:, :], ACT.Copy, scale=0.5), ("mh", m))
                    for m in range(8):
                        if not last:
                            if m == 0:
                                pe_s.wait(act, ("a", 7), turn)
                            y_split_hi(act, turn + 1, m)
                        dve_s.wait(act, ("x", m), turn)
                        act.dma_start(x2T[:, m, cols(b)], xt[:, m % 2, :]).then_inc(x2_stored[m % 2], 16)
                each_block(act, body)
                for j in range(2):
                    act.wait_ge(x2_stored[j], 64 * NB)

            def y_split_lo(dve, turn, kt):
                yhi_s.wait(dve, kt, turn)
                ylo_s.done(dve.tensor_tensor(ylo[:, kt, :], yraw[:, kt % 2, :], yhi[:, kt, :].bitcast(F32), ALU.subtract), kt)

            def w_lo(dve, n):
                whi_s.wait(dve, n, 0)
                wlo_s.done(dve.tensor_tensor(wlo[:, n, :], wraw[:, n % 2, :], whi[:, n, :].bitcast(F32), ALU.subtract), n)

            @block.vector
            def _(dve):
                dve_s.open(dve)
                for n in range(8):
                    y_split_lo(dve, 1, n)
                    w_lo(dve, n)

                def body(b, turn, last):
                    for m in range(8):
                        if isinstance(turn, int) and turn == 1:
                            w_lo(dve, 8 + m)
                        act_s.wait(dve, ("g", m), turn)
                        pe_s.wait(dve, ("r", m), turn)
                        dve_s.wait(dve, ("ml", m - 1), turn) if m else dve_s.wait(dve, ("ml", 7), turn - 1)
                        for name, out, ps, half in (("m1", m1, pr, 0), ("m2", m2, pa, 1)):
                            pe_s.wait(dve, ("ra"[half], m), turn)
                            dve_s.done(dve.scalar_tensor_tensor(out=out[:, :], in0=gate[:, m % 2, half, :], scalar=1.0, in1=ps[m % 2][:, 0:BW],
                                                                op0=ALU.add, op1=ALU.mult), (name, m))
                        dve_s.wait(dve, ("m2", m), turn)
                        dve_s.done(dve.tensor_tensor(m1[:, :], m1[:, :], m2[:, :], ALU.add), ("ms", m))
                        act_s.wait(dve, ("mh", m), turn)
                        dve_s.done(dve.scalar_tensor_tensor(out=mlo[:, m, :], in0=m1[:, :], scalar=0.5, in1=mhi[:, m, :].bitcast(F32),
                                                            op0=ALU.mult, op1=ALU.subtract), ("ml", m))
                    for m in range(8):
                        pe_s.wait(dve, ("o", m), turn)
                        dve.wait_ge(x_loaded[m % 2], nth(turn, m))
                        for c0, c1, g in pieces(last):
                            ins = dve.scalar_tensor_tensor(out=xt[:, m % 2, c0:c1], in0=po[m % 2][:, c0:c1], scalar=k.mod[:, 16 + m, g:g + 1],
                                                           in1=xt[:, m % 2, c0:c1], op0=ALU.mult, op1=ALU.add)
                        dve_s.done(ins, ("x", m))
                        if not last:
                            y_split_lo(dve, turn + 1, m)
                each_block(dve, body)

            @block.tensor
            def _(pe):
                pe_s.open(pe)

                def body(b, turn, last):
                    for m in range(8):
                        w = slice(m * P, (m + 1) * P)
                        for name, ps, k0 in (("r", pr, 0), ("a", pa, 4)):
                            if m == 0:
                                for kt in range(k0, k0 + 4):
                                    ylo_s.wait(pe, kt, turn)
                                    if isinstance(turn, int) and turn == 1:
                                        wlo_s.wait(pe, kt, 0)
                            step = "m1" if name == "r" else "m2"
                            dve_s.wait(pe, (step, m - 2), turn) if m >= 2 else dve_s.wait(pe, (step, m + 6), turn - 1)
                            mm = split_products(pe, ps[m % 2][:, 0:BW], lambda i: whi[:, k0 + i, w], lambda i: wlo[:, k0 + i, w],
                                                lambda kt: yhi[:, kt, :], lambda kt: ylo[:, kt, :], range(k0, k0 + 4))
                            pe_s.done(mm, (name, m))
                    for m in range(8):
                        w = slice(m * P, (m + 1) * P)
                        dve_s.wait(pe, ("ml", 7), turn)
                        if isinstance(turn, int) and turn == 1:
                            wlo_s.wait(pe, 15, 0)
                        dve_s.wait(pe, ("x", m - 2), turn) if m >= 2 else dve_s.wait(pe, ("x", m + 6), turn - 1)
                        mm = split_products(pe, po[m % 2][:, 0:BW], lambda i: whi[:, 8 + i, w], lambda i: wlo[:, 8 + i, w],
                                            lambda kt: mhi[:, kt, :], lambda kt: mlo[:, kt, :], range(8))
                        pe_s.done(mm, ("o", m))
                each_block(pe, body)


UNITS = 2 * FF_T
SUBS = [(0, P), (P, P), (2 * P, P), (SPLIT_AT, DEC)]


class Mlp:

    def __init__(self, ctx, nc, k):
        self.k = k

        def sb(name, shape, dt=F32):
            return ctx.enter_context(nc.sbuf_tensor(name, shape, dt))

        def sem(name):
            return ctx.enter_context(nc.semaphore(name))
        self.raw = sb("ff_raw", [P, 4, KD, P])
        self.whi, self.wlo = sb("ff_hi", [P, 2, KD, P], F32R), sb("ff_lo", [P, 2, KD, P], F32R)
        self.hhi, self.hlo = sb("h2_hi", [P, KD, BW], F32R), sb("h2_lo", [P, KD, BW], F32R)
        self.uhi, self.ulo = sb("hidden_hi", [P, FF_T, BW], F32R), sb("hidden_lo", [P, FF_T, BW], F32R)
        self.r = sb("hidden", [P, 2, BW])
        self.xa, self.xn = sb("x_now", [P, KD, BW]), sb("x_next", [P, KD, BW])
        self.sq = sb("squares2", [P, 2, BW])
        self.nrm = sb("norms", [P, BW])
        self.h = sb("h2", [P, 2, BW])
        self.yo = sb("y_rows", [P, D])
        self.cur = sb("tail_now", [P, 2, 24])
        self.ones = sb("ones", [P, P])
        self.ps = [ctx.enter_context(nc.psum_tensor(f"ff_ps{j}", [P, 512], F32)) for j in range(2)]
        self.pn = [ctx.enter_context(nc.psum_tensor(f"norm_ps{j}", [P, 512], F32)) for j in range(2)]
        self.pt = [ctx.enter_context(nc.psum_tensor(f"rows_ps{j}", [P, D], F32)) for j in range(2)]
        self.w_loaded = [sem(f"ff_loaded{j}") for j in range(4)]
        self.x_loaded = sem("x2_loaded")
        self.y_stored = sem("y_stored")
        u = list(range(UNITS))
        self.hi_s, self.lo_s = Steps(ctx, nc, "ff_hi_made", u), Steps(ctx, nc, "ff_lo_made", u)
        self.mm_s = Steps(ctx, nc, "ff_products", u)
        self.relu_s, self.uhi_s = Steps(ctx, nc, "relu", range(FF_T)), Steps(ctx, nc, "hidden_hi_made", range(FF_T))
        self.sq_s, self.ulo_s = Steps(ctx, nc, "hidden_squared", range(FF_T)), Steps(ctx, nc, "hidden_lo_made", range(FF_T))
        self.x_s = Steps(ctx, nc, "x3", ["moved"] + list(range(KD)))
        ks = list(range(KD))
        self.n_sq, self.f_sq = Steps(ctx, nc, "next_squares", ks), Steps(ctx, nc, "final_squares", ks)
        self.n_pe, self.f_pe = Steps(ctx, nc, "next_sums", ks), Steps(ctx, nc, "final_sums", ks + ["t0", "t1", "t2", "t3"])
        self.n_rms, self.f_rms = Steps(ctx, nc, "next_rms", ["rms"], base=1), Steps(ctx, nc, "final_rms", ["rms"], base=1)
        self.n_dve = Steps(ctx, nc, "next_norm", ["vec", "rstd", ("n", 0)] + [x for j in ks[1:] for x in (("n", j), ("lo", j - 1))] + [("lo", KD - 1)], base=1)
        self.n_act = Steps(ctx, nc, "next_affine", [(s, j) for j in ks for s in ("h", "hi")], base=1)
        self.f_dve = Steps(ctx, nc, "final_norm", ["rstd"] + ks)
        self.f_act = Steps(ctx, nc, "final_rows", ["t0", "t1", "t2", "t3"])

    def strip(self, s):
        k = self.k
        if s < FF_T:
            return k.w_ff1.rearrange("(k p) n -> p k n", p=P)[:, :, s * P:(s + 1) * P]
        m, q = (s - FF_T) // 4, (s - FF_T) % 4
        return k.w_ff2[q * D:(q + 1) * D, m * P:(m + 1) * P].rearrange("(k p) n -> p k n", p=P)

    def next_at(self, u):
        v = u - FF_T
        if 3 <= v < 3 + KD:
            yield "sq", v - 3
        if v == 12:
            yield "mean", 0
        if 14 <= v < 14 + 2 * KD and v % 2 == 0:
            yield "h", (v - 14) // 2

    def final_at(self, u):
        if 1 <= u < 1 + KD:
            yield "sq", u - 1
        if u == 10:
            yield "mean", 0
        if 12 <= u < 12 + KD:
            yield "y", u - 12
        if u in (21, 23, 25, 27):
            yield "t", (u - 21) // 2


def for_tensor(at, u):
    return [x for x in at(u - 1) if x[0] == "sq"] + [x for x in at(u) if x[0] != "sq"]


def build_mlp(nc, k):
    with ExitStack() as ctx:
        w = Mlp(ctx, nc, k)
        ones_made = ctx.enter_context(nc.semaphore("ones_made"))
        x2T = k.x2T.rearrange("(a p) t -> p a t", p=P)
        GF = VROW["final_norm_g"]
        PIECES = ((0, SPLIT_AT, 0), (SPLIT_AT, BW, 1))

        def next_sync(sp, b, turn):
            w.x_s.wait(sp, "moved", turn - 1)
            sp.dma_start(w.xn[:, :, :], x2T[:, :, ds(b * BW, BW)]).then_inc(w.x_loaded, 16)

        def next_act(act, part, j, turn):
            if part == "sq":
                act.wait_ge(w.x_loaded, 16 * turn)
                if j >= 2:
                    w.n_pe.wait(act, j - 2, turn)
                w.n_sq.done(act.activation(w.sq[:, j % 2, :], w.xn[:, j, :], ACT.Square), j)
            if part == "mean":
                w.n_pe.wait(act, KD - 1, turn)
                if not isinstance(turn, int) or turn > 1:
                    w.f_dve.wait(act, KD - 1, turn - 2)
                w.n_rms.done(act.activation(w.nrm[:, :], w.pn[0][:, 0:BW], ACT.Sqrt, scale=1.0 / D, bias=k.eps[:, 0:1]), "rms")
            if part == "h":
                w.n_dve.wait(act, ("n", j), turn)
                for c0, c1, tail in PIECES:
                    scale = w.cur[:, 0, j:j + 1] if tail else k.gain2[:, j, 0:1]
                    shift = w.cur[:, 0, 8 + j:9 + j] if tail else k.mod[:, 24 + j, 0:1]
                    ins = act.activation(w.h[:, j % 2, c0:c1], w.h[:, j % 2, c0:c1], ACT.Identity, scale=scale, bias=shift)
                w.n_act.done(ins, ("h", j))
                w.n_act.wait(act, ("h", j), turn)
                w.n_act.done(act.activation(w.hhi[:, j, :], w.h[:, j % 2, :], ACT.Copy), ("hi", j))

        def next_dve(dve, part, j, turn, b):
            if part == "mean":
                w.n_dve.done(dve.tensor_copy(w.cur[:, 0, :].unsqueeze(1), k.tail[:, ds(b, 1), :]), "vec")
                w.n_rms.wait(dve, "rms", turn)
                w.n_dve.done(dve.reciprocal(w.nrm[:, :], w.nrm[:, :]), "rstd")
            if part == "h":
                w.n_dve.wait(dve, "rstd", turn)
                if j >= 2:
                    w.n_dve.wait(dve, ("lo", j - 2), turn)
                w.n_dve.done(dve.tensor_tensor(w.h[:, j % 2, :], w.xn[:, j, :], w.nrm[:, :], ALU.mult), ("n", j))
                for i in ([j - 1] if j else []) + ([j] if j == KD - 1 else []):
                    w.n_act.wait(dve, ("hi", i), turn)
                    w.n_dve.done(dve.tensor_tensor(w.hlo[:, i, :], w.h[:, i % 2, :], w.hhi[:, i, :].bitcast(F32), ALU.subtract), ("lo", i))

        def next_pe(pe, part, j, turn):
            if part == "sq":
                w.n_sq.wait(pe, j, turn)
                w.n_pe.done(pe.matmul(w.pn[0][:, 0:BW], w.ones[:, :], w.sq[:, j % 2, :], start=(j == 0), stop=(j == KD - 1)), j)

        def final_act(act, part, j, turn, rows):
            if part == "sq":
                w.x_s.wait(act, KD - 1, turn)
                if j >= 2:
                    w.f_pe.wait(act, j - 2, turn)
                w.f_sq.done(act.activation(w.sq[:, j % 2, :], w.xa[:, j, :], ACT.Square), j)
            if part == "mean":
                w.f_pe.wait(act, KD - 1, turn)
                w.n_dve.wait(act, ("lo", KD - 1), min(turn + 1, NB) if isinstance(turn, int) else turn + 1)
                w.f_rms.done(act.activation(w.nrm[:, :], w.pn[1][:, 0:BW], ACT.Sqrt, scale=1.0 / D, bias=k.eps[:, 0:1]), "rms")
            if part == "t":
                c0, n = SUBS[j]
                w.f_pe.wait(act, f"t{j}", turn)
                act.wait_ge(w.y_stored, 64 * (turn - 1) + 16 * j)
                w.f_act.done(act.activation(w.yo[0:n, :], w.pt[j % 2][0:n, :], ACT.Copy), f"t{j}")
                w.f_act.wait(act, f"t{j}", turn)
                act.dma_start(rows(c0, n), w.yo[0:n, :]).then_inc(w.y_stored, 16)

        def final_dve(dve, part, j, turn, b_now):
            if part == "mean":
                w.f_rms.wait(dve, "rms", turn)
                w.f_dve.done(dve.reciprocal(w.nrm[:, :], w.nrm[:, :]), "rstd")
            if part == "y":
                w.f_dve.wait(dve, "rstd", turn)
                w.f_dve.done(dve.scalar_tensor_tensor(out=w.xa[:, j, :], in0=w.xa[:, j, :], scalar=k.vec[:, GF + j:GF + j + 1],
                                                      in1=w.nrm[:, :], op0=ALU.mult, op1=ALU.mult), j)

        def final_pe(pe, part, j, turn):
            if part == "sq":
                w.f_sq.wait(pe, j, turn)
                w.f_pe.done(pe.matmul(w.pn[1][:, 0:BW], w.ones[:, :], w.sq[:, j % 2, :], start=(j == 0), stop=(j == KD - 1)), j)
            if part == "t":
                c0, n = SUBS[j]
                w.f_dve.wait(pe, KD - 1, turn)
                w.f_act.wait(pe, f"t{j - 2}", turn) if j >= 2 else w.f_act.wait(pe, f"t{j + 2}", turn - 1)
                for i in range(KD):
                    mm = pe.transpose(w.pt[j % 2][0:n, i * P:(i + 1) * P], w.xa[:, i, c0:c0 + n], k.ident[:, :])
                w.f_pe.done(mm, f"t{j}")

        def rows_of(b):
            def rows(c0, n):
                if isinstance(b, int) and b == NB - 1 and c0 == SPLIT_AT:
                    return k.y_sample
                return k.y_prompt[ds(b * BW + c0, n), :]
            return rows

        def make_hi(act, s, turn):
            act.wait_ge(w.w_loaded[s % 4], 16 * (UNITS // 4) * (turn - 1) + 16 * (s // 4 + 1))
            w.mm_s.wait(act, s - 2, turn) if s >= 2 else w.mm_s.wait(act, UNITS + s - 2, turn - 1)
            w.hi_s.done(act.activation(w.whi[:, s % 2], w.raw[:, s % 4], ACT.Copy), s)

        def make_lo(dve, s, turn):
            w.hi_s.wait(dve, s, turn)
            w.lo_s.done(dve.tensor_tensor(w.wlo[:, s % 2], w.raw[:, s % 4], w.whi[:, s % 2].bitcast(F32), ALU.subtract), s)

        def each_block(eng, body):
            body(0, 1, False, True)
            with eng.Fori(1, NB - 1) as b:
                body(b, b + 1, True, True)
            body(NB - 1, NB, True, False)

        FIRST = [x for u in range(UNITS) for x in w.next_at(u)]
        LAST = [x for u in range(UNITS) for x in w.final_at(u)]
        with nc.Block() as block:
            @block.sync
            def _(sp):
                def body(b, turn, before, after):
                    for s in range(UNITS):
                        w.lo_s.wait(sp, s - 4, turn) if s >= 4 else w.lo_s.wait(sp, UNITS + s - 4, turn - 1)
                        sp.dma_start(w.raw[:, s % 4], w.strip(s)).then_inc(w.w_loaded[s % 4], 16)
                        if s == FF_T and after:
                            next_sync(sp, b + 1, turn + 1)
                next_sync(sp, 0, 1)
                each_block(sp, body)

            @block.scalar
            def _(act):
                for s in (w.hi_s, w.relu_s, w.uhi_s, w.n_sq, w.f_sq, w.f_act):
                    s.open(act)

                def body(b, turn, before, after):
                    for u in range(UNITS):
                        if u + 1 < UNITS:
                            make_hi(act, u + 1, turn)
                        elif after:
                            make_hi(act, 0, turn + 1)
                        if u < FF_T:
                            w.mm_s.wait(act, u, turn)
                            w.sq_s.wait(act, u - 2, turn) if u >= 2 else w.sq_s.wait(act, FF_T + u - 2, turn - 1)
                            w.ulo_s.wait(act, u - 2, turn) if u >= 2 else w.ulo_s.wait(act, FF_T + u - 2, turn - 1)
                            w.relu_s.done(act.activation(w.r[:, u % 2, :], w.ps[u % 2][:, 0:BW], ACT.Relu), u)
                        if 1 <= u <= FF_T:
                            w.sq_s.wait(act, u - 1, turn)
                            if u == 1:
                                w.mm_s.wait(act, UNITS - 1, turn - 1)
                            w.uhi_s.done(act.activation(w.uhi[:, u - 1, :], w.r[:, (u - 1) % 2, :], ACT.Copy), u - 1)
                        if before:
                            for part, j in w.final_at(u):
                                final_act(act, part, j, turn - 1, rows_of(b - 1))
                        if after:
                            for part, j in w.next_at(u):
                                next_act(act, part, j, turn + 1)
                for part, j in FIRST:
                    next_act(act, part, j, 1)
                make_hi(act, 0, 1)
                each_block(act, body)
                for part, j in LAST:
                    final_act(act, part, j, NB, rows_of(NB - 1))
                act.wait_ge(w.y_stored, 64 * NB)

            @block.vector
            def _(dve):
                for s in (w.lo_s, w.sq_s, w.ulo_s, w.x_s, w.f_dve):
                    s.open(dve)
                dve.memset(w.ones[:, :], 1.0).then_inc(ones_made, 1)

                def move(turn, b):
                    w.f_pe.wait(dve, "t3", turn - 1)
                    dve.tensor_copy(w.cur[:, 1, :].unsqueeze(1), k.tail[:, ds(b, 1), :])
                    w.x_s.done(dve.tensor_copy(w.xa[:, :, :], w.xn[:, :, :]), "moved")

                def body(b, turn, before, after):
                    for u in range(UNITS):
                        if u + 1 < UNITS:
                            make_lo(dve, u + 1, turn)
                        elif after:
                            make_lo(dve, 0, turn + 1)
                        if u < FF_T:
                            w.relu_s.wait(dve, u, turn)
                            w.sq_s.done(dve.tensor_tensor(w.r[:, u % 2, :], w.r[:, u % 2, :], w.r[:, u % 2, :], ALU.mult), u)
                        if 1 <= u <= FF_T:
                            w.uhi_s.wait(dve, u - 1, turn)
                            w.ulo_s.done(dve.tensor_tensor(w.ulo[:, u - 1, :], w.r[:, (u - 1) % 2, :], w.uhi[:, u - 1, :].bitcast(F32), ALU.subtract), u - 1)
                        if u >= FF_T and u % 4 == 3:
                            m = (u - FF_T) // 4
                            w.mm_s.wait(dve, u, turn)
                            for c0, c1, tail in PIECES:
                                g = w.cur[:, 1, 16 + m:17 + m] if tail else k.mod[:, 40 + m, 0:1]
                                ins = dve.scalar_tensor_tensor(out=w.xa[:, m, c0:c1], in0=w.ps[m % 2][:, c0:c1], scalar=g, in1=w.xa[:, m, c0:c1],
                                                               op0=ALU.mult, op1=ALU.add)
                            w.x_s.done(ins, m)
                        if before:
                            for part, j in w.final_at(u):
                                final_dve(dve, part, j, turn - 1, b)
                        if u == 29:
                            move(turn, b)
                        if u == FF_T:
                            w.x_s.wait(dve, "moved", turn)
                        if after:
                            for part, j in w.next_at(u):
                                next_dve(dve, part, j, turn + 1, b + 1)
                for part, j in FIRST:
                    next_dve(dve, part, j, 1, 0)
                make_lo(dve, 0, 1)
                each_block(dve, body)
                for part, j in LAST:
                    final_dve(dve, part, j, NB, NB)

            @block.tensor
            def _(pe):
                for s in (w.mm_s, w.n_pe, w.f_pe):
                    s.open(pe)
                pe.wait_ge(ones_made, 1)

                def body(b, turn, before, after):
                    for u in range(UNITS):
                        w.lo_s.wait(pe, u, turn)
                        ops = (lambda i: w.whi[:, u % 2, i, :], lambda i: w.wlo[:, u % 2, i, :])
                        if u < FF_T:
                            if u == 0:
                                w.n_dve.wait(pe, ("lo", KD - 1), turn)
                            if u >= 2:
                                w.relu_s.wait(pe, u - 2, turn)
                            else:
                                w.x_s.wait(pe, 6 + u, turn - 1)
                            mm = split_products(pe, w.ps[u % 2][:, 0:BW], *ops, lambda kt: w.hhi[:, kt, :], lambda kt: w.hlo[:, kt, :], range(KD))
                        else:
                            m, q = (u - FF_T) // 4, u % 4
                            if q == 0:
                                if m < 2:
                                    w.relu_s.wait(pe, FF_T - 2 + m, turn)
                                else:
                                    w.x_s.wait(pe, m - 2, turn)
                            if m == 0:
                                w.ulo_s.wait(pe, 8 * q + 7, turn)
                            mm = split_products(pe, w.ps[m % 2][:, 0:BW], *ops, lambda kt: w.uhi[:, kt, :], lambda kt: w.ulo[:, kt, :],
                                                range(8 * q, 8 * q + 8), first=(q == 0), last=(q == 3))
                        w.mm_s.done(mm, u)
                        if before:
                            for part, j in for_tensor(w.final_at, u):
                                final_pe(pe, part, j, turn - 1)
                        if after:
                            for part, j in for_tensor(w.next_at, u):
                                next_pe(pe, part, j, turn + 1)
                for part, j in FIRST:
                    next_pe(pe, part, j, 1)
                each_block(pe, body)
                for part, j in LAST:
                    final_pe(pe, part, j, NB)


def declare(nc, arrays):
    k = Tensors()
    ap = {n: nc.dram_tensor(f"in_{n}", a.shape, F32, kind="ExternalInput").ap() for n, a in arrays.items()}
    k.vec_in = {n: ap[n][0] if n != "final_norm_g" and n != "r_k" else ap[n] for n, _ in VECS}
    k.vec_in["r_k"] = ap["r_k"].rearrange("a h d -> (a h d)")
    k.vec_in["c_prompt"], k.vec_in["c_sample"] = ap["c_prompt"][0], ap["c_sample"][0]
    k.vec_in["shift"] = ap["state_rwkv_shift"][0, 0]
    k.x_prompt, k.x_sample = ap["x_prompt"][0], ap["x_sample"][0]
    k.s_in = ap["state_rwkv_wkv"][0, 0]
    k.cache_k, k.cache_v = ap["cache_att_k"][0, 0], ap["cache_att_v"][0, 0]
    k.w_ada, k.w_in, k.w_lora_up, k.a_lora_up, k.g_lora_up = (ap[n][0] for n in ("w_ada", "w_in", "w_lora_up", "a_lora_up", "g_lora_up"))
    k.w_br_r, k.w_br_a, k.w_out, k.w_ff1, k.w_ff2 = (ap[n][0] for n in ("w_br_r", "w_br_a", "w_out", "w_ff1", "w_ff2"))
    k.rel_table = ap["rel_table"][0]
    outs = [nc.dram_tensor(f"out_{i}", s, F32, kind="ExternalOutput").ap() for i, s in enumerate(OUT_SHAPES)]
    k.y_prompt, k.y_sample = outs[0][0], outs[1][0]
    k.p_wkv, k.p_shift, k.p_k, k.p_v = outs[2][0, 0], outs[3][0, 0], outs[4][0, 0], outs[5][0, 0]
    k.s_wkv, k.s_shift, k.s_k, k.s_v = outs[6][0, 0], outs[7][0, 0], outs[8][0, 0], outs[9][0, 0]

    def keep(name, rows, cols):
        return nc.dram_tensor(f"keep_{name}", (rows, cols), F32, kind="Internal").ap()
    k.xT, k.proj, k.yrT, k.yaT, k.x2T = keep("xT", D, NT), keep("proj", IN_T * P, NT), keep("yrT", DR, NT), keep("yaT", DR, NT), keep("x2T", D, NT)
    k.ext = keep("ext", NH, EXT)
    return k


OUT_SHAPES = [(1, SEQ, D), (1, DEC, D), (1, 1, NH, HD, HD), (1, 1, R_PROJ), (1, 1, WIN, NH, HD), (1, 1, WIN, NH, HD),
              (1, 1, NH, HD, HD), (1, 1, R_PROJ), (1, 1, DEC, NH, HD), (1, 1, DEC, NH, HD)]


def build(nc, k):
    with ExitStack() as ctx:
        def sb(name, shape, dt=F32):
            return ctx.enter_context(nc.sbuf_tensor(name, shape, dt))
        k.ident, k.half_power, k.one, k.eps, k.vec = sb("identity", [P, P]), sb("minus_half", [P, 1]), sb("one", [P, 1]), sb("epsilon", [P, 1]), sb("channel_vectors", [P, NVEC])
        k.mod, k.gain1, k.gain2 = sb("modulation", [P, 48, 2]), sb("gain_mix", [P, 8, 2]), sb("gain_mlp", [P, 8, 2])
        k.tail = sb("tail_modulation", [P, NB, 24])
        with ExitStack() as early:
            def eb(name, shape, dt=F32):
                return early.enter_context(nc.sbuf_tensor(name, shape, dt))
            k.pair, k.ii = eb("pair_ones", [P, P]), eb("two_identities", [P, 64])
            k.m_lt, k.m_le, k.m_lt8, k.m_gt8, k.m_gto = (eb(n, [P, P]) for n in ("mask_lt", "mask_le", "mask_lt8", "mask_gt8", "mask_gt_outer"))
            k.restart = eb("scan_restart", [P, NP * C])
            k.wa_up, k.g_up = eb("w_a_up", [P, DR]), eb("g_up", [P, DR])
            k.cvec, k.one_minus_ka = eb("c_vectors", [P, NCROW]), eb("one_minus_ka", [P, 4])
            build_constants(nc, k)
            k.h_hi, k.h_lo = eb("h_hi", [P, KD, NT], F32R), eb("h_lo", [P, KD, NT], F32R)
            with ExitStack() as mctx:
                m = Modulation(mctx, nc, k)
                build_modulation(nc, k, m)
                build_first_norm(nc, k, m)
            with ExitStack() as pctx:
                pj = Projection(pctx, nc, k)
                build_projection_rwkv(nc, k, pj)
                build_rwkv(nc, k, pj)
        build_attention(nc, k)
        build_merge(nc, k)
        build_mlp(nc, k)


NAMES = ["x_prompt", "x_sample", "c_prompt", "c_sample", "state_rwkv_wkv", "state_rwkv_shift", "cache_att_k",
         "cache_att_v", "w_ada", "b_ada", "norm_mix_g", "w_in", "mu_shift", "w_lora_up", "w0", "a_lora_up", "a0",
         "g_lora_up", "k_k", "k_a", "r_k", "lnx_g", "lnx_b", "rel_table", "w_br_r", "w_br_a", "w_out", "norm_mlp_g",
         "w_ff1", "w_ff2", "final_norm_g"]


def kernel(**inputs):
    import numpy as np
    import concourse.bacc as bacc
    from concourse.bass_utils import run_bass_kernel_spmd

    nc = bacc.Bacc("TRN2", target_bir_lowering=False, num_devices=1)
    arrays = {n: np.ascontiguousarray(inputs[n]) for n in NAMES}
    build(nc, declare(nc, arrays))
    r = run_bass_kernel_spmd(nc, [{f"in_{n}": a for n, a in arrays.items()}], core_ids=[0])
    return tuple(r.results[0][f"out_{i}"] for i in range(len(OUT_SHAPES)))
```
